# Optimizing a Trainium2 kernel written in Bass

```python
import math
import jax
import jax.numpy as jnp
from jax import lax
import numpy as np

D_MODEL = 1024
BATCH = 1
SEQ = 256
DEPTH = 2

GRID_W = 64
CTX_LEN = 256

A_HEADS = D_MODEL // 256
A_DH = 64
A_DV = 2 * A_DH
B_HEADS = D_MODEL // 128
B_DH = 64
NA_ROWS = 8
NA_COLS = 16
C_HEADS = 4
C_DK = D_MODEL // 2 // C_HEADS
C_DV = D_MODEL // C_HEADS
C_RANK = 16
C_TAU = 16.0
C_CHUNK = 64
N_EXPERTS = 16
N_GROUPS = 4
TOP_K = 2
D_EXPERT = D_MODEL // 2

ROPE_BASE = 10000.0
EPS = 1e-6
Q_BLOCK = 128

A_QK = A_HEADS * 2 * A_DH
A_V = A_HEADS * A_DV
B_W = B_HEADS * B_DH
ATT_IN = 2 * A_QK + A_V + 3 * B_W
ATT_OUT = A_V + B_W
GLA_QK = C_HEADS * C_DK
GLA_V = C_HEADS * C_DV
GLA_IN = 2 * GLA_QK + 2 * GLA_V + 2 * C_RANK
N_ATT = (DEPTH + 1) // 2
N_GLA = DEPTH // 2

kernel_name = 'hybrid_diffusion_trunk'

def rmsnorm(x, g):
    xf = x.astype(jnp.float32)
    y = xf * lax.rsqrt(jnp.mean(xf * xf, axis=-1, keepdims=True) + EPS)
    return (y * g.astype(jnp.float32)).astype(x.dtype)

def modulate(h, shift, scale):
    return h * (1.0 + scale) + shift

def heads(t, n_heads, d):
    b, n, _ = t.shape
    return t.reshape(b, n, n_heads, d).transpose(0, 2, 1, 3)

def rope_1d(x, pos):
    n = x.shape[-1]
    inv = ROPE_BASE ** (-jnp.arange(0, n, 2, dtype=jnp.float32) / n)
    ang = pos.astype(jnp.float32)[:, None] * inv[None, :]
    cos = jnp.cos(ang).astype(x.dtype)
    sin = jnp.sin(ang).astype(x.dtype)
    x1, x2 = jnp.split(x, 2, axis=-1)
    return jnp.concatenate([x1 * cos - x2 * sin, x1 * sin + x2 * cos], axis=-1)

def rope_2d(x, rows, cols):
    xr, xc = jnp.split(x, 2, axis=-1)
    return jnp.concatenate([rope_1d(xr, rows), rope_1d(xc, cols)], axis=-1)

def diff_core(q, k, v, lam):
    s = jnp.einsum('bhcqd,bhckd->bhcqk', q, k).astype(jnp.float32) * (q.shape[-1] ** -0.5)
    p = jax.nn.softmax(s, axis=-1)
    a = p[:, :, 0] - lam * p[:, :, 1]
    return jnp.einsum('bhqk,bhkv->bhqv', a.astype(v.dtype), v)

def softmax_attn(q, k, v):
    s = jnp.einsum('bhqd,bhkd->bhqk', q, k).astype(jnp.float32) * (q.shape[-1] ** -0.5)
    p = jax.nn.softmax(s, axis=-1)
    return jnp.einsum('bhqk,bhkd->bhqd', p.astype(v.dtype), v)

def neighbourhood_attn(q, k, v, kc, vc, bias_table):
    b, h, l, dh = q.shape
    rows = l // GRID_W
    wh = min(NA_ROWS, rows)
    qg = q.reshape(b, h, rows, GRID_W, dh)
    kg = k.reshape(b, h, rows, GRID_W, dh)
    vg = v.reshape(b, h, rows, GRID_W, dh)
    col = jnp.arange(GRID_W)
    col_start = jnp.clip(col - NA_COLS // 2, 0, GRID_W - NA_COLS)
    col_idx = col_start[:, None] + jnp.arange(NA_COLS)[None, :]
    dc = col_idx - col[:, None]
    scale = dh ** -0.5
    n_loc = wh * NA_COLS

    def row_block(r):
        r0 = jnp.clip(r - wh // 2, 0, rows - wh)
        q_r = lax.dynamic_index_in_dim(qg, r, axis=2, keepdims=False)
        k_r = lax.dynamic_slice_in_dim(kg, r0, wh, axis=2)
        v_r = lax.dynamic_slice_in_dim(vg, r0, wh, axis=2)
        k_w = k_r[:, :, :, col_idx]
        v_w = v_r[:, :, :, col_idx]
        dr = r0 + jnp.arange(wh) - r
        bias = bias_table[:, (dr + NA_ROWS - 1)[None, :, None], (dc + NA_COLS - 1)[:, None, :]]
        s_loc = jnp.einsum('bhqd,bhrqcd->bhqrc', q_r, k_w).astype(jnp.float32) * scale + bias[None].astype(jnp.float32)
        s_ctx = jnp.einsum('bhqd,bhkd->bhqk', q_r, kc).astype(jnp.float32) * scale
        s = jnp.concatenate([s_loc.reshape(b, h, GRID_W, n_loc), s_ctx], axis=-1)
        p = jax.nn.softmax(s, axis=-1).astype(v.dtype)
        p_loc = p[..., :n_loc].reshape(b, h, GRID_W, wh, NA_COLS)
        return (jnp.einsum('bhqrc,bhrqcd->bhqd', p_loc, v_w)
                + jnp.einsum('bhqk,bhkd->bhqd', p[..., n_loc:], vc))

    o = lax.map(row_block, jnp.arange(rows))
    return o.transpose(1, 2, 0, 3, 4).reshape(b, h, l, dh)

def attn_layer(hx, hc, w_in, w_out, lam_p, lam_init, subln_g, na_bias, need_ctx):
    b, l, _ = hx.shape
    pos = jnp.arange(l)
    rows_pos, cols_pos = pos // GRID_W, pos % GRID_W
    cuts = [A_QK, 2 * A_QK, 2 * A_QK + A_V, 2 * A_QK + A_V + B_W, 2 * A_QK + A_V + 2 * B_W]

    def project(h):
        n = h.shape[1]
        qa, ka, va, qb, kb, vb = jnp.split(h @ w_in, cuts, axis=-1)
        qa = qa.reshape(b, n, A_HEADS, 2, A_DH).transpose(0, 2, 3, 1, 4)
        ka = ka.reshape(b, n, A_HEADS, 2, A_DH).transpose(0, 2, 3, 1, 4)
        return (qa, ka, heads(va, A_HEADS, A_DV), heads(qb, B_HEADS, B_DH),
                heads(kb, B_HEADS, B_DH), heads(vb, B_HEADS, B_DH))

    qa_x, ka_x, va_x, qb_x, kb_x, vb_x = project(hx)
    qa_c, ka_c, va_c, qb_c, kb_c, vb_c = project(hc)
    lp = lam_p.astype(jnp.float32)
    lam = jnp.exp(jnp.sum(lp[0] * lp[1])) - jnp.exp(jnp.sum(lp[2] * lp[3])) + lam_init

    qa_x = rope_2d(qa_x, rows_pos, cols_pos)
    ka_x = rope_2d(ka_x, rows_pos, cols_pos)
    k_all = jnp.concatenate([ka_x, ka_c], axis=3)
    v_all = jnp.concatenate([va_x, va_c], axis=2)
    nb = l // Q_BLOCK
    q_blocks = qa_x.reshape(b, A_HEADS, 2, nb, Q_BLOCK, A_DH).transpose(3, 0, 1, 2, 4, 5)
    oa_x = lax.map(lambda qq: diff_core(qq, k_all, v_all, lam), q_blocks)
    oa_x = oa_x.transpose(1, 2, 0, 3, 4).reshape(b, A_HEADS, l, A_DV)
    ob_x = neighbourhood_attn(qb_x, kb_x, vb_x, kb_c, vb_c, na_bias)

    def merge(oa, ob):
        n = oa.shape[2]
        oa = rmsnorm(oa, subln_g) * (1.0 - lam_init)
        oa = oa.transpose(0, 2, 1, 3).reshape(b, n, A_V)
        ob = ob.transpose(0, 2, 1, 3).reshape(b, n, B_W)
        return jnp.concatenate([oa, ob], axis=-1) @ w_out

    out_x = merge(oa_x, ob_x)
    if not need_ctx:
        return out_x, None
    out_c = merge(diff_core(qa_c, ka_c, va_c, lam), softmax_attn(qb_c, kb_c, vb_c))
    return out_x, out_c

def gla_chunked(q, k, v, g, s0):
    b, h, l, dk = q.shape
    dv = v.shape[-1]
    nc = l // C_CHUNK
    f32 = jnp.float32
    qc = q.astype(f32).reshape(b, h, nc, C_CHUNK, dk)
    kc = k.astype(f32).reshape(b, h, nc, C_CHUNK, dk)
    vc = v.astype(f32).reshape(b, h, nc, C_CHUNK, dv)
    gc = jnp.cumsum(g.astype(f32).reshape(b, h, nc, C_CHUNK, dk), axis=3)
    g_end = gc[:, :, :, -1:]
    g_mid = gc[:, :, :, C_CHUNK // 2 - 1:C_CHUNK // 2]
    k_to_end = kc * jnp.exp(g_end - gc)
    chunk_decay = jnp.exp(g_end[:, :, :, 0])

    def step(s, inp):
        k_e, v_c, dec = inp
        return s * dec[..., None] + jnp.einsum('bhcd,bhcv->bhdv', k_e, v_c), s

    xs = (jnp.moveaxis(k_to_end, 2, 0), jnp.moveaxis(vc, 2, 0), jnp.moveaxis(chunk_decay, 2, 0))
    s_final, s_start = lax.scan(step, s0.astype(f32), xs)
    o_inter = jnp.einsum('bhncd,nbhdv->bhncv', qc * jnp.exp(gc), s_start)
    a = jnp.einsum('bhncd,bhnsd->bhncs', qc * jnp.exp(gc - g_mid), kc * jnp.exp(g_mid - gc))
    upto_t = jnp.tril(jnp.ones((C_CHUNK, C_CHUNK), dtype=bool))
    a = jnp.where(upto_t, a, 0.0)
    o = o_inter + jnp.einsum('bhncs,bhnsv->bhncv', a, vc)
    return o.reshape(b, h, l, dv).astype(v.dtype), s_final

def gla_final_state(k, v, g):
    gc = jnp.cumsum(g.astype(jnp.float32), axis=2)
    k_to_end = k.astype(jnp.float32) * jnp.exp(gc[:, :, -1:] - gc)
    return jnp.einsum('bhld,bhlv->bhdv', k_to_end, v.astype(jnp.float32))

def gla_layer(hx, hc, w_in, w_gate, b_gate, norm_g, w_out, need_ctx):
    b = hx.shape[0]
    cuts = [GLA_QK, 2 * GLA_QK, 2 * GLA_QK + GLA_V, 2 * GLA_QK + 2 * GLA_V, 2 * GLA_QK + 2 * GLA_V + C_RANK]

    def project(h):
        q, k, v, gate, lf, lb = jnp.split(h @ w_in, cuts, axis=-1)

        def log_decay(lr, d):
            z = (lr @ w_gate[d] + b_gate[d]).astype(jnp.float32)
            return heads(jax.nn.log_sigmoid(z) / C_TAU, C_HEADS, C_DK)

        return (heads(q, C_HEADS, C_DK) * (C_DK ** -0.5), heads(k, C_HEADS, C_DK),
                heads(v, C_HEADS, C_DV), gate, log_decay(lf, 0), log_decay(lb, 1))

    qx, kx, vx, gate_x, gfx, gbx = project(hx)
    qc, kc, vc, gate_c, gfc, gbc = project(hc)
    flip = lambda t: jnp.flip(t, axis=2)
    zero = jnp.zeros((b, C_HEADS, C_DK, C_DV), jnp.float32)
    if need_ctx:
        oc_f, sc_f = gla_chunked(qc, kc, vc, gfc, zero)
        oc_b, sc_b = gla_chunked(flip(qc), flip(kc), flip(vc), flip(gbc), zero)
    else:
        sc_f = gla_final_state(kc, vc, gfc)
        sc_b = gla_final_state(flip(kc), flip(vc), flip(gbc))
    ox_f, _ = gla_chunked(qx, kx, vx, gfx, sc_f)
    ox_b, _ = gla_chunked(flip(qx), flip(kx), flip(vx), flip(gbx), sc_b)

    def readout(o, gate):
        n = o.shape[2]
        o = rmsnorm(o, norm_g).transpose(0, 2, 1, 3).reshape(b, n, GLA_V)
        return (o * jax.nn.silu(gate)) @ w_out

    out_x = readout(ox_f + flip(ox_b), gate_x)
    if not need_ctx:
        return out_x, None
    return out_x, readout(oc_f + flip(oc_b), gate_c)

def moe(h, router_w, router_bias, w1, w3, w2):
    t = h.shape[0]
    per_group = N_EXPERTS // N_GROUPS
    scores = jax.nn.sigmoid((h @ router_w).astype(jnp.float32))
    sel = scores + router_bias.astype(jnp.float32)
    grp_score = lax.top_k(sel.reshape(t, N_GROUPS, per_group), 2)[0].sum(-1)
    grp = jnp.argmax(grp_score, axis=-1)
    in_grp = (jnp.arange(N_EXPERTS) // per_group)[None, :] == grp[:, None]
    _, idx = lax.top_k(jnp.where(in_grp, sel, -jnp.inf), TOP_K)
    w_sel = jnp.take_along_axis(scores, idx, axis=-1)
    w_sel = w_sel / jnp.sum(w_sel, axis=-1, keepdims=True)
    gates = jnp.sum(jax.nn.one_hot(idx, N_EXPERTS, dtype=jnp.float32) * w_sel[..., None], axis=1)
    y = jnp.zeros_like(h)
    for e in range(N_EXPERTS):
        he = jax.nn.silu(h @ w1[e]) * (h @ w3[e])
        y = y + gates[:, e:e + 1].astype(h.dtype) * (he @ w2[e])
    return y

def setup_inputs(seed: int = 0) -> dict:
    key = jax.random.key(seed)
    ks = jax.random.split(key, 24)
    nrm = lambda k, shape, s: jax.random.normal(k, shape, jnp.float32) * s
    d = D_MODEL
    return {
        'x': nrm(ks[0], (BATCH, SEQ, d), 1.0),
        'c': nrm(ks[1], (BATCH, d), 1.0),
        'ctx': nrm(ks[2], (BATCH, CTX_LEN, d), 1.0),
        'c_ctx': nrm(ks[3], (d,), 1.0),
        'w_mod': nrm(ks[4], (DEPTH, d, 6 * d), 0.5 * d ** -0.5),
        'b_mod': nrm(ks[5], (DEPTH, 6 * d), 0.02),
        'norm_g': 1.0 + nrm(ks[6], (DEPTH, 2, d), 0.02),
        'final_g': 1.0 + nrm(ks[7], (d,), 0.02),
        'att_w_in': nrm(ks[8], (N_ATT, d, ATT_IN), d ** -0.5),
        'att_w_out': nrm(ks[9], (N_ATT, ATT_OUT, d), ATT_OUT ** -0.5),
        'att_lambda': nrm(ks[10], (N_ATT, 4, A_DH), 0.1),
        'att_subln_g': 1.0 + nrm(ks[11], (N_ATT, A_DV), 0.02),
        'na_bias': nrm(ks[12], (N_ATT, B_HEADS, 2 * NA_ROWS - 1, 2 * NA_COLS - 1), 0.1),
        'gla_w_in': nrm(ks[13], (N_GLA, d, GLA_IN), d ** -0.5),
        'gla_w_gate': nrm(ks[14], (N_GLA, 2, C_RANK, GLA_QK), C_RANK ** -0.5),
        'gla_b_gate': nrm(ks[15], (N_GLA, 2, GLA_QK), 0.1),
        'gla_norm_g': 1.0 + nrm(ks[16], (N_GLA, C_DV), 0.02),
        'gla_w_out': nrm(ks[17], (N_GLA, GLA_V, d), GLA_V ** -0.5),
        'router_w': nrm(ks[18], (d, N_EXPERTS), d ** -0.5),
        'router_bias': nrm(ks[19], (N_EXPERTS,), 0.01),
        'moe_w1': nrm(ks[20], (DEPTH, N_EXPERTS, d, D_EXPERT), d ** -0.5),
        'moe_w3': nrm(ks[21], (DEPTH, N_EXPERTS, d, D_EXPERT), d ** -0.5),
        'moe_w2': nrm(ks[22], (DEPTH, N_EXPERTS, D_EXPERT, d), D_EXPERT ** -0.5),
    }

def reference(x, c, ctx, c_ctx, w_mod, b_mod, norm_g, final_g, att_w_in, att_w_out, att_lambda,
              att_subln_g, na_bias, gla_w_in, gla_w_gate, gla_b_gate, gla_norm_g, gla_w_out,
              router_w, router_bias, moe_w1, moe_w3, moe_w2):
    b, l, d = x.shape
    n_ctx = ctx.shape[1]
    for i in range(DEPTH):
        last = i == DEPTH - 1
        j = i // 2
        mx = jax.nn.silu(c) @ w_mod[i] + b_mod[i]
        mc = jax.nn.silu(c_ctx) @ w_mod[i] + b_mod[i]
        sh1x, sc1x, g1x, sh2x, sc2x, g2x = jnp.split(mx[:, None, :], 6, axis=-1)
        sh1c, sc1c, g1c, sh2c, sc2c, g2c = jnp.split(mc[None, None, :], 6, axis=-1)
        hx = modulate(rmsnorm(x, norm_g[i, 0]), sh1x, sc1x)
        hc = modulate(rmsnorm(ctx, norm_g[i, 0]), sh1c, sc1c)
        if i % 2 == 0:
            lam_init = 0.8 - 0.6 * math.exp(-0.3 * i)
            ox, oc = attn_layer(hx, hc, att_w_in[j], att_w_out[j], att_lambda[j], lam_init,
                                att_subln_g[j], na_bias[j], not last)
        else:
            ox, oc = gla_layer(hx, hc, gla_w_in[j], gla_w_gate[j], gla_b_gate[j], gla_norm_g[j],
                               gla_w_out[j], not last)
        x = x + g1x * ox
        hx2 = modulate(rmsnorm(x, norm_g[i, 1]), sh2x, sc2x)
        if last:
            x = x + g2x * moe(hx2.reshape(-1, d), router_w, router_bias, moe_w1[i], moe_w3[i],
                              moe_w2[i]).reshape(b, l, d)
        else:
            ctx = ctx + g1c * oc
            hc2 = modulate(rmsnorm(ctx, norm_g[i, 1]), sh2c, sc2c)
            y = moe(jnp.concatenate([hc2, hx2], axis=1).reshape(-1, d), router_w, router_bias,
                    moe_w1[i], moe_w3[i], moe_w2[i]).reshape(b, n_ctx + l, d)
            ctx = ctx + g2c * y[:, :n_ctx]
            x = x + g2x * y[:, n_ctx:]
    return rmsnorm(x, final_g)


_drawn_inputs = setup_inputs


def setup_inputs(seed=0):
    import zlib

    import numpy as np

    out = dict(_drawn_inputs(seed))
    spreads = {}
    factors = {'final_g': 8.205,
     'att_subln_g': 3.067,
     'na_bias': 31.024,
     'gla_b_gate': 3.298,
     'gla_norm_g': 11.854}
    for name, (base, spread) in spreads.items():
        noise = np.random.default_rng([zlib.crc32(name.encode()), seed]).standard_normal(out[name].shape)
        drawn = base * np.exp(spread * noise) if base else spread * noise
        out[name] = jnp.asarray(drawn.astype(out[name].dtype))
    for name, factor in factors.items():
        out[name] = (out[name] * factor).astype(out[name].dtype)
    return out
```

```python
import math
from contextlib import ExitStack

import numpy as np

import concourse.bass as bass
from concourse import mybir

F32 = mybir.dt.float32
I32 = mybir.dt.int32
U32 = mybir.dt.uint32
ALU = mybir.AluOpType
ACT = mybir.ActivationFunctionType
AX = mybir.AxisListType

P = 128
D = 1024
KD = D // P
SEQ = 256
CTX = 256
XT = SEQ // P
NT = (SEQ + CTX) // P
EPS = 1e-6
GRID_W = 64
NA_ROWS, NA_COLS = 8, 16
A_HEADS, B_HEADS, DH, A_DV = 4, 8, 64, 128
LAM_INIT = 0.8 - 0.6 * math.exp(-0.3 * 0)
C_HEADS, C_DK, C_DV, RANK, TAU, CHUNK = 4, 128, 256, 16, 16.0, 64
NE, NG, EPG, DE = 16, 4, 4, 512
HALF = 512
BIG = 3.0e38
MASKED = -1.0e30

CH = KD * HALF
RING = 0
LO = 3 * CH
XR = 6 * CH
MOD = XR + NT * D
KEEP = MOD + 12 * D
K_ID, K_ONE, K_SILU, K_LAM, K_GATE, K_SLOT, K_ROWS = 0, 128, 256, 272, 280, 288, 296
K_OVIDX, K_OVEXP, K_NOV, K_CUR, K_IOTA, K_TOK, K_RBIAS = 360, 368, 376, 385, 386, 402, 406
HI = KEEP + 512
END = 53200
SH1, SC1, G1, SH2, SC2, G2 = range(6)


class Steps:

    def __init__(self, engine, sem):
        self.engine, self.sem, self.n = engine, sem, 0

    def __call__(self, ins):
        self.n += 1
        ins.then_inc(self.sem, 1)
        self.engine.wait_ge(self.sem, self.n)


def bc(ap, axis, shape):
    return ap.unsqueeze(axis).to_broadcast(shape)


class Trunk:

    def __init__(self, nc, ctx, t, out):
        self.nc, self.t, self.out = nc, t, out
        self.A = ctx.enter_context(nc.sbuf_tensor("arena", [P, END], F32))
        self.ps = ctx.enter_context(nc.psum_tensor("ps", [P, 8, HALF], F32))
        self.h2_dram = nc.dram_tensor("h2_rows", (NT * P, D), F32).ap()
        self.y_dram = nc.dram_tensor("expert_rows", ((NE + 2 * NT - 1) * P, D), F32).ap()
        self.landed = [ctx.enter_context(nc.semaphore(f"chunk_landed{s}")) for s in range(3)]
        self.w_landed = {k: [ctx.enter_context(nc.semaphore(f"{k}_landed{s}")) for s in range(2)]
                         for k in ("w1", "w3", "w2")}
        self.w_base = {0: 0, 1: 8 * 16}
        self.chunks = []
        for i in range(2):
            for j in range(12):
                self.chunks.append(t["w_mod"][i][:, j * HALF:(j + 1) * HALF])
            w_in = t["att_w_in"][0] if i == 0 else t["gla_w_in"][0]
            w_out = t["att_w_out"][0] if i == 0 else t["gla_w_out"][0]
            for j in range(6):
                self.chunks.append(w_in[:, j * HALF:(j + 1) * HALF])
            for j in range(2):
                self.chunks.append(w_out[:, j * HALF:(j + 1) * HALF])
        self.loaded = 0
        self.cleared = []

    def f(self, at, *shape):
        n = int(np.prod(shape))
        v = self.A[:, at:at + n]
        if len(shape) == 1:
            return v
        names = "abcd"[:len(shape)]
        return v.rearrange(f"p ({' '.join(names)}) -> p {' '.join(names)}",
                           **{a: s for a, s in zip(names, shape)})

    def slot(self, s):
        return self.f(RING + s * CH, KD, HALF)

    def sems(self, ctx, *names):
        sems = [self.nc.alloc_semaphore(n) for n in names]

        def retire():
            for s in sems:
                self.nc.gpsimd.sem_clear(s)
            for s in self.cleared:
                self.nc.release_semaphore(s)
            self.cleared = sems
        ctx.callback(retire)
        return sems

    def chunk(self, c):
        return self.slot(c % 3)

    def wait_chunk(self, engine, c):
        engine.wait_ge(self.landed[c % 3], 16 * (c // 3 + 1))

    def load_chunks(self, sp, end, first, released):
        while self.loaded < end:
            c = self.loaded
            if c - 3 >= first:
                sp.wait_ge(*released(c - 3))
            sp.dma_start(self.chunk(c), self.chunks[c].rearrange("(k p) n -> p k n", p=P))\
              .then_inc(self.landed[c % 3], 16)
            self.loaded += 1


def setup_stage(T):
    nc, t, f = T.nc, T.t, T.f
    with ExitStack() as ctx:
        in_landed, silu_done = T.sems(ctx, "setup_landed", "setup_silu")
        with nc.Block() as block:
            @block.sync
            def _(sp):
                sp.dma_start(f(KEEP + K_ID, P), t["k_ident"]).then_inc(in_landed, 16)
                sp.dma_start(f(KEEP + K_ONE, P), t["k_ones"]).then_inc(in_landed, 16)
                sp.dma_start(f(KEEP + K_IOTA, NE), t["k_iota16"].partition_broadcast(P)).then_inc(in_landed, 16)
                sp.dma_start(f(KEEP + K_TOK, NT), t["k_token"]).then_inc(in_landed, 16)
                sp.dma_start(f(KEEP + K_RBIAS, NE), t["router_bias"].partition_broadcast(P)).then_inc(in_landed, 16)
                sp.dma_start(f(KEEP + K_SILU, 2, KD)[:, 0, :], t["c_cols"]).then_inc(in_landed, 16)
                sp.dma_start(f(KEEP + K_SILU, 2, KD)[:, 1, :], t["c_ctx_cols"]).then_inc(in_landed, 16)
                T.load_chunks(sp, 3, 0, None)
                sp.dma_start(f(XR, NT, D)[:, 0:XT, :], t["x"][0].rearrange("(t p) d -> p t d", p=P)).then_inc(in_landed, 16)
                sp.dma_start(f(XR, NT, D)[:, XT:NT, :], t["ctx"][0].rearrange("(t p) d -> p t d", p=P)).then_inc(in_landed, 16)
                sp.wait_ge(in_landed, 9 * 16)

            @block.scalar
            def _(act):
                act.wait_ge(in_landed, 9 * 16)
                act.activation(f(KEEP + K_SILU, 2 * KD), f(KEEP + K_SILU, 2 * KD), ACT.Silu).then_inc(silu_done, 1)


def mod_stage(T, i):
    nc, t, f, ps = T.nc, T.t, T.f, T.ps
    first = i * 20
    n_ctx = 12 if i == 0 else 4
    spread, brow, acc = f(LO, KD, P), f(LO + KD * P, 12, HALF), f(LO + KD * P + 12 * HALF, 2, HALF)
    silu = f(KEEP + K_SILU, 2, KD)
    mod = f(MOD, 2, 12, HALF)
    ones = f(KEEP + K_ONE, P)
    with ExitStack() as ctx:
        bias_landed, spread_ready, acc_ready, mod_psum, mod_done, step = T.sems(
            ctx, f"b_mod_landed{i}", f"spread_ready{i}", f"acc_ready{i}", f"mod_psum{i}", f"mod_done{i}", f"mod_step{i}")

        def used(c):
            return mod_psum, c - first + 1

        with nc.Block() as block:
            @block.sync
            def _(sp):
                sp.dma_start(brow[0:1], t["b_mod"][i:i + 1, :].rearrange("a (j n) -> a j n", n=HALF)).then_inc(bias_landed, 16)
                T.load_chunks(sp, first + 12 + 3, first, used)
                sp.wait_ge(bias_landed, 16)

            @block.vector
            def _(dve):
                then = Steps(dve, step)
                for k in range(KD):
                    last = dve.tensor_scalar(spread[:, k, :], ones, silu[:, 1, k:k + 1], None, ALU.mult)
                last.then_inc(spread_ready, 1)
                for j in range(12):
                    w = T.chunk(first + j)
                    T.wait_chunk(dve, first + j)
                    if j >= 2:
                        dve.wait_ge(mod_psum, j - 1)
                    for k in range(KD):
                        if k == 0:
                            ins = dve.tensor_scalar(acc[:, j % 2, :], w[:, 0, :], silu[:, 0, 0:1], None, ALU.mult)
                        else:
                            ins = dve.scalar_tensor_tensor(acc[:, j % 2, :], w[:, k, :], silu[:, 0, k:k + 1],
                                                           acc[:, j % 2, :], ALU.mult, ALU.add)
                        if k < KD - 1:
                            then(ins)
                    ins.then_inc(acc_ready, 1)

            @block.tensor
            def _(pe):
                pe.wait_ge(spread_ready, 1)
                pe.wait_ge(bias_landed, 16)
                for j in range(12):
                    w = T.chunk(first + j)
                    T.wait_chunk(pe, first + j)
                    if j >= 2:
                        pe.wait_ge(mod_done, j - 1)
                    bank = 2 * (j % 2)
                    if j < n_ctx:
                        for k in range(KD):
                            pe.matmul(ps[:, bank + 1, :], spread[:, k, :], w[:, k, :], start=(k == 0), stop=False)
                        pe.matmul(ps[:, bank + 1, :], ones[0:1, :], brow[0:1, j, :], start=False, stop=True)
                    pe.matmul(ps[:, bank, :], ones[0:1, :], brow[0:1, j, :], start=True, stop=False)
                    pe.wait_ge(acc_ready, j + 1)
                    pe.matmul(ps[:, bank, :], ones, acc[:, j % 2, :], start=False, stop=True).then_inc(mod_psum, 1)

            @block.scalar
            def _(act):
                for j in range(12):
                    bank = 2 * (j % 2)
                    act.wait_ge(mod_psum, j + 1)
                    ins = act.activation(mod[:, 0, j, :], ps[:, bank, :], ACT.Copy)
                    if j < n_ctx:
                        ins = act.activation(mod[:, 1, j, :], ps[:, bank + 1, :], ACT.Copy)
                    ins.then_inc(mod_done, 1)


def norm_stage(T, i, which, tiles, load_to, store_rows):
    nc, t, f, ps = T.nc, T.t, T.f, T.ps
    tag = f"n{i}{which}"
    X, mod, hT = f(XR, NT, D), f(MOD, 2, 6, D), f(HI, KD, NT * P)
    g_row, junk, h_row = f(LO, D), f(LO + D, NT, D), f(LO + 5 * D, 2, D)
    ss, rstd = f(LO + 7 * D, NT), f(LO + 7 * D + NT, NT)
    shift, scale = (SH1, SC1) if which == 0 else (SH2, SC2)
    ident = f(KEEP + K_ID, P)
    kinds = sorted({0 if n < XT else 1 for n in tiles})
    with ExitStack() as ctx:
        g_landed, ss_ready, var_ready, std_ready, h_ready, h_psum, h_evac, row_stored0, row_stored1, step = T.sems(
            ctx, *[f"{tag}_{n}" for n in ("g_landed", "ss_ready", "var_ready", "std_ready", "h_ready",
                                          "h_psum", "h_evac", "row_stored0", "row_stored1", "step")])
        row_stored = (row_stored0, row_stored1)
        with nc.Block() as block:
            @block.sync
            def _(sp):
                sp.dma_start(g_row, t["norm_g"][i, which:which + 1, :].partition_broadcast(P)).then_inc(g_landed, 16)
                load_to(sp)
                if store_rows:
                    for n, tile in enumerate(tiles):
                        sp.wait_ge(h_ready, n + 1)
                        sp.dma_start(T.h2_dram[tile * P:(tile + 1) * P, :], h_row[:, n % 2, :]).then_inc(row_stored[n % 2], 16)
                    for s in row_stored:
                        sp.wait_ge(s, 16 * len(tiles) // 2)
                sp.wait_ge(g_landed, 16)

            @block.scalar
            def _(act):
                for n, tile in enumerate(tiles):
                    act.activation(junk[:, n, :], X[:, tile, :], ACT.Square, accum_out=ss[:, n:n + 1]).then_inc(ss_ready, 1)
                act.wait_ge(var_ready, 1)
                act.activation(rstd[:, 0:len(tiles)], ss[:, 0:len(tiles)], ACT.Sqrt).then_inc(std_ready, 1)
                for n, tile in enumerate(tiles):
                    act.wait_ge(h_psum, n + 1)
                    for b in range(2):
                        ins = act.activation(hT[:, 4 * b:4 * b + 4, tile * P:(tile + 1) * P],
                                             ps[:, 2 * (n % 2) + b, :].rearrange("p (k n) -> p k n", n=P), ACT.Copy)
                    ins.then_inc(h_evac, 1)

            @block.vector
            def _(dve):
                then = Steps(dve, step)
                dve.wait_ge(g_landed, 16)
                for v in kinds:
                    ins = dve.scalar_tensor_tensor(mod[:, v, scale, :], mod[:, v, scale, :], 1.0, g_row, ALU.add, ALU.mult)
                then(ins)
                dve.wait_ge(ss_ready, len(tiles))
                dve.tensor_scalar(ss[:, 0:len(tiles)], ss[:, 0:len(tiles)], 1.0 / D, EPS, ALU.mult, ALU.add).then_inc(var_ready, 1)
                dve.wait_ge(std_ready, 1)
                then(dve.reciprocal(rstd[:, 0:len(tiles)], rstd[:, 0:len(tiles)]))
                for n, tile in enumerate(tiles):
                    v = 0 if tile < XT else 1
                    if n >= 2:
                        dve.wait_ge(h_psum, n - 1)
                        if store_rows:
                            dve.wait_ge(row_stored[n % 2], 16 * (n // 2))
                    then(dve.scalar_tensor_tensor(h_row[:, n % 2, :], X[:, tile, :], rstd[:, n:n + 1],
                                                  mod[:, v, scale, :], ALU.mult, ALU.mult))
                    dve.tensor_tensor(h_row[:, n % 2, :], h_row[:, n % 2, :], mod[:, v, shift, :], ALU.add).then_inc(h_ready, 1)

            @block.tensor
            def _(pe):
                for n, tile in enumerate(tiles):
                    pe.wait_ge(h_ready, n + 1)
                    if n >= 2:
                        pe.wait_ge(h_evac, n - 1)
                    for k in range(KD):
                        ins = pe.transpose(ps[:, 2 * (n % 2) + k // 4, (k % 4) * P:(k % 4 + 1) * P],
                                           h_row[:, n % 2, k * P:(k + 1) * P], ident)
                    ins.then_inc(h_psum, 1)


QKT, V0 = LO, LO + 16 * HALF


def attn_project_stage(T):
    nc, t, f, ps = T.nc, T.t, T.f, T.ps
    first = 12
    hT, qkT, v = f(HI, KD, NT * P), f(QKT, 16, HALF), f(V0, NT, D)
    rope_r, cos, sin = f(HI + 4 * D, P), f(HI + 4 * D + P, SEQ), f(HI + 4 * D + P + SEQ, SEQ)
    tmp = f(HI + 5 * D, 2, SEQ)
    lp, lq, ls = f(HI + 6 * D, 4, DH), f(HI + 6 * D + 256, 2, DH), f(HI + 6 * D + 384, 2)
    lam = f(KEEP + K_LAM, 4)
    kinds = ["q", "q", "v", "q", "q", "v"]
    dest = [0, 4, 0, 8, 12, 1]
    groups = [(c, g) for c in range(6) for g in range(4)]
    with ExitStack() as ctx:
        tab_landed, proj_done, proj_evac, rot_done, rope_done, lam_step, step = T.sems(
            ctx, "tab_landed", "proj_done", "proj_evac", "rot_done", "rope_done", "lam_exp", "proj_step")
        with nc.Block() as block:
            @block.sync
            def _(sp):
                sp.dma_start(rope_r, t["k_rope"]).then_inc(tab_landed, 16)
                sp.dma_start(cos, t["k_cos"]).then_inc(tab_landed, 16)
                sp.dma_start(sin, t["k_sin"]).then_inc(tab_landed, 16)
                sp.dma_start(lp, t["att_lambda"].partition_broadcast(P)).then_inc(tab_landed, 16)
                T.load_chunks(sp, first + 6 + 2, first, lambda c: (proj_done, 4 * (c - first + 1)))
                sp.wait_ge(tab_landed, 64)

            @block.tensor
            def _(pe):
                def rotate(n):
                    pe.wait_ge(proj_evac, n + 1)
                    if n >= 2:
                        pe.wait_ge(rope_done, n - 1)
                    pe.matmul(ps[:, 4 + n % 2, 0:SEQ], rope_r, qkT[:, n, 0:SEQ], start=True, stop=True).then_inc(rot_done, 1)

                pe.wait_ge(tab_landed, 64)
                for n, (c, g) in enumerate(groups):
                    w = T.chunk(first + c)
                    if g == 0:
                        T.wait_chunk(pe, first + c)
                    if n >= 4:
                        pe.wait_ge(proj_evac, n - 3)
                    for k in range(KD):
                        if kinds[c] == "q":
                            a, b = w[:, k, g * P:(g + 1) * P], hT[:, k, :]
                        else:
                            a, b = hT[:, k, g * P:(g + 1) * P], w[:, k, :]
                        ins = pe.matmul(ps[:, n % 4, :], a, b, start=(k == 0), stop=(k == KD - 1))
                    ins.then_inc(proj_done, 1)
                    if 1 <= n <= 8:
                        rotate(n - 1)

            @block.scalar
            def _(act):
                for n, (c, g) in enumerate(groups):
                    act.wait_ge(proj_done, n + 1)
                    to = qkT[:, dest[c] + g, :] if kinds[c] == "q" else v[:, g, dest[c] * HALF:(dest[c] + 1) * HALF]
                    act.activation(to, ps[:, n % 4, :], ACT.Copy).then_inc(proj_evac, 1)
                act.wait_ge(lam_step, 1)
                act.activation(lam[:, 0:2], ls, ACT.Exp).then_inc(lam_step, 1)

            @block.vector
            def _(dve):
                then = Steps(dve, step)
                dve.wait_ge(tab_landed, 64)
                for n in range(8):
                    q = qkT[:, n, 0:SEQ]
                    dve.wait_ge(rot_done, n + 1)
                    dve.tensor_tensor(tmp[:, 0, :], ps[:, 4 + n % 2, 0:SEQ], sin, ALU.mult)
                    then(dve.tensor_tensor(tmp[:, 1, :], q, cos, ALU.mult))
                    dve.tensor_tensor(q, tmp[:, 1, :], tmp[:, 0, :], ALU.add).then_inc(rope_done, 1)
                    dve.wait_ge(rope_done, n + 1)
                lps = lp.rearrange("p (a b) n -> p a b n", b=2)
                then(dve.tensor_tensor(lq, lps[:, :, 0, :], lps[:, :, 1, :], ALU.mult))
                dve.tensor_reduce(ls, lq, AX.X, ALU.add).then_inc(lam_step, 1)
                dve.wait_ge(lam_step, 2)
                then(dve.tensor_tensor(lam[:, 2:3], lam[:, 1:2], lam[:, 0:1], ALU.subtract))
                then(dve.tensor_scalar(lam[:, 3:4], lam[:, 2:3], LAM_INIT, None, ALU.subtract))


ORow = HI


def attention_stage(T):
    nc, t, f, ps = T.nc, T.t, T.f, T.ps
    qkT, v, O = f(QKT, 16, HALF), f(V0, NT, D), f(ORow, NT, D)
    Pb = f(HI + 4 * D, 2, 2, HALF)
    aT = f(HI + 6 * D, 2, 2, HALF)
    bm = f(HI + 8 * D, 2, 2, XT, SEQ)
    mask = f(HI + 10 * D, XT, SEQ)
    st = HI + 10 * D + 2 * SEQ
    NJ = 32
    mx, nm, sm, rs, cs = (f(st + k * 64, 64) for k in range(5))
    zero = f(st + 5 * 64, HALF)
    neg_lam = f(KEEP + K_LAM, 4)[:, 3:4]
    ident = f(KEEP + K_ID, P)
    jobs = [("A", b, n) for b in range(4) for n in range(NT)] + [("B", b, n) for b in range(4) for n in range(NT)]

    def keys(n):
        return list(range(NT)) if n < XT else list(range(XT, NT))

    def turned(j):
        return j if j <= 16 else 16 + 2 * (j - 16)

    with ExitStack() as ctx:
        zero_ready, zeros_stored, bias_landed0, bias_landed1, mask_landed, bias_half, bias_ready, scored, shifted, exp_done, a_ready, a_turned, at_ready, av_done, o_done, step = T.sems(
            ctx, "zero_ready", "zeros_stored", "bias_landed0", "bias_landed1", "mask_landed", "bias_half", "bias_ready", "scored", "shifted", "exp_done", "a_ready",
            "a_turned", "at_ready", "av_done", "o_done", "att_step")
        bias_landed = (bias_landed0, bias_landed1)
        with nc.Block() as block:
            @block.sync
            def _(sp):
                sp.dma_start(mask, t["k_namask"].rearrange("(t p) n -> p t n", p=P)).then_inc(mask_landed, 16)
                for hp in range(4):
                    if hp >= 2:
                        sp.wait_ge(scored, 2 * (16 + 4 * (hp - 2) + 2))
                    for u in range(2):
                        sp.dma_start(bm[:, hp % 2, u], t["na_window"][2 * hp + u].rearrange("(t p) n -> p t n", p=P))\
                          .then_inc(bias_landed[hp % 2], 16)
                for s in bias_landed:
                    sp.wait_ge(s, 4 * 16)
                sp.wait_ge(zero_ready, 1)
                for m in range(2 * NT - 1):
                    at = (NE + m) * P
                    sp.dma_start(T.y_dram[at:at + P, :].rearrange("p (b n) -> p b n", n=HALF), bc(zero, 1, (P, 2, HALF)))\
                      .then_inc(zeros_stored, 16)
                sp.wait_ge(zeros_stored, 16 * (2 * NT - 1))

            @block.gpsimd
            def _(pool):
                pool.memset(zero, 0.0).then_inc(zero_ready, 1)
                pool.wait_ge(mask_landed, 16)
                for hp in range(4):
                    pool.wait_ge(bias_landed[hp % 2], 32 * (hp // 2 + 1))
                    b = bm[:, hp % 2]
                    pool.tensor_scalar(b, b, float(DH) ** 0.5, None, ALU.mult).then_inc(bias_half, 1)
                    pool.wait_ge(bias_half, hp + 1)
                    pool.tensor_tensor(b, b, bc(mask, 1, (P, 2, XT, SEQ)), ALU.add).then_inc(bias_ready, 1)

            @block.tensor
            def _(pe):
                def scores(j):
                    kind, b, n = jobs[j]
                    ks = keys(n)
                    qb, kb = (b, 4 + b) if kind == "A" else (8 + b, 12 + b)
                    if j >= 2:
                        pe.wait_ge(exp_done, 2 * (j - 1))
                    if kind == "B" and n < XT:
                        pe.wait_ge(bias_ready, b + 1)
                    for u in range(2):
                        rows = slice(DH * u, DH * u + DH)
                        to = ps[:, 2 * (j % 2) + u, 0:P * len(ks)]
                        biased = kind == "B" and n < XT
                        ins = pe.matmul(to, qkT[rows, qb, n * P:(n + 1) * P], qkT[rows, kb, ks[0] * P:NT * P],
                                        start=True, stop=not biased)
                        if biased:
                            ins = pe.matmul(ps[:, 2 * (j % 2) + u, 0:SEQ], ident, bm[:, b % 2, u, n, :],
                                            start=False, stop=True)
                        ins.then_inc(scored, 1)

                def turn(j):
                    kind, b, n = jobs[j]
                    if kind == "A":
                        pe.wait_ge(a_ready, j + 1)
                    else:
                        pe.wait_ge(exp_done, 2 * (j + 1))
                    if j >= 1:
                        pe.wait_ge(at_ready, turned(j))
                    for u in range(1 if kind == "A" else 2):
                        for m in range(len(keys(n))):
                            ins = pe.transpose(ps[:, 4 + u, m * P:(m + 1) * P], Pb[:, j % 2, u, m * P:(m + 1) * P], ident)
                        ins.then_inc(a_turned, 1)

                def values(j):
                    kind, b, n = jobs[j]
                    ks = keys(n)
                    pe.wait_ge(at_ready, turned(j + 1))
                    if j >= 2:
                        pe.wait_ge(o_done, j - 1)
                    for u in range(1 if kind == "A" else 2):
                        w = A_DV if kind == "A" else DH
                        col = b * A_DV if kind == "A" else HALF + (2 * b + u) * DH
                        for m, kt in enumerate(ks):
                            ins = pe.matmul(ps[:, 6 + j % 2, u * w:(u + 1) * w], aT[:, j % 2, u, m * P:(m + 1) * P],
                                            v[:, kt, col:col + w], start=(m == 0), stop=(m == len(ks) - 1))
                    ins.then_inc(av_done, 1)

                scores(0)
                for j in range(NJ):
                    if j + 1 < NJ:
                        scores(j + 1)
                    turn(j)
                    values(j)

            @block.scalar
            def _(act):
                def turned_copy(j):
                    kind, b, n = jobs[j]
                    w = P * len(keys(n))
                    if j >= 2:
                        act.wait_ge(av_done, j - 1)
                    for u in range(1 if kind == "A" else 2):
                        act.wait_ge(a_turned, turned(j) + u + 1)
                        act.activation(aT[:, j % 2, u, 0:w], ps[:, 4 + u, 0:w], ACT.Copy).then_inc(at_ready, 1)

                for j, (kind, b, n) in enumerate(jobs):
                    w = P * len(keys(n))
                    if j >= 2:
                        act.wait_ge(a_turned, turned(j - 1))
                    for u in range(2):
                        act.wait_ge(shifted, 2 * j + u + 1)
                        act.activation(Pb[:, j % 2, u, 0:w], ps[:, 2 * (j % 2) + u, 0:w], ACT.Exp,
                                       bias=nm[:, 2 * j + u:2 * j + u + 1], scale=DH ** -0.5,
                                       accum_out=sm[:, 2 * j + u:2 * j + u + 1]).then_inc(exp_done, 1)
                    if j >= 1:
                        turned_copy(j - 1)
                turned_copy(NJ - 1)

            @block.vector
            def _(dve):
                then = Steps(dve, step)

                def shift(j):
                    w = P * len(keys(jobs[j][2]))
                    for u in range(2):
                        c = slice(2 * j + u, 2 * j + u + 1)
                        dve.wait_ge(scored, 2 * j + u + 1)
                        then(dve.tensor_reduce(mx[:, c], ps[:, 2 * (j % 2) + u, 0:w], AX.X, ALU.max))
                        dve.tensor_scalar(nm[:, c], mx[:, c], -(DH ** -0.5), None, ALU.mult).then_inc(shifted, 1)

                def combine(j):
                    kind, b, n = jobs[j]
                    w = P * len(keys(n))
                    dve.wait_ge(exp_done, 2 * (j + 1))
                    then(dve.reciprocal(rs[:, 2 * j:2 * j + 2], sm[:, 2 * j:2 * j + 2]))
                    if kind == "A":
                        then(dve.tensor_scalar(cs[:, 2 * j:2 * j + 1], rs[:, 2 * j + 1:2 * j + 2], neg_lam, None, ALU.mult))
                        then(dve.tensor_scalar(Pb[:, j % 2, 1, 0:w], Pb[:, j % 2, 1, 0:w], cs[:, 2 * j:2 * j + 1], None, ALU.mult))
                        dve.scalar_tensor_tensor(Pb[:, j % 2, 0, 0:w], Pb[:, j % 2, 0, 0:w], rs[:, 2 * j:2 * j + 1],
                                                 Pb[:, j % 2, 1, 0:w], ALU.mult, ALU.add).then_inc(a_ready, 1)

                def keep(j):
                    kind, b, n = jobs[j]
                    dve.wait_ge(av_done, j + 1)
                    bank = ps[:, 6 + j % 2, :]
                    if kind == "A":
                        dve.tensor_copy(O[:, n, b * A_DV:(b + 1) * A_DV], bank[:, 0:A_DV]).then_inc(o_done, 1)
                    else:
                        for u in range(2):
                            c = HALF + (2 * b + u) * DH
                            ins = dve.tensor_scalar(O[:, n, c:c + DH], bank[:, u * DH:(u + 1) * DH],
                                                    rs[:, 2 * j + u:2 * j + u + 1], None, ALU.mult)
                        ins.then_inc(o_done, 1)

                for j in range(NJ + 2):
                    if j < NJ:
                        shift(j)
                    if 1 <= j <= NJ:
                        combine(j - 1)
                    if j >= 2:
                        keep(j - 2)


def out_stage(T, i, ntiles, O, oT, work, load_to):
    nc, t, f, ps = T.nc, T.t, T.f, T.ps
    first = 20 * i + 18
    X, mod = f(XR, NT, D), f(MOD, 2, 6, D)
    ident = f(KEEP + K_ID, P)
    nh, dv = (A_HEADS, A_DV) if i == 0 else (C_HEADS, C_DV)
    wn = nh * dv
    sub_g, sq, ss, rstd, gate = work
    with ExitStack() as ctx:
        g_landed, var_ready, std_ready, o_ready, o_psum, o_evac, out_done, x_done, silu_done, step = T.sems(
            ctx, *[f"o{i}_{n}" for n in ("g_landed", "var_ready", "std_ready", "o_ready", "o_psum", "o_evac",
                                         "out_done", "x_done", "silu_done", "step")])
        groups = [(c, n) for c in range(2) for n in range(ntiles)]
        with nc.Block() as block:
            @block.sync
            def _(sp):
                g = t["att_subln_g"] if i == 0 else t["gla_norm_g"]
                sp.dma_start(sub_g, g.partition_broadcast(P)).then_inc(g_landed, 16)
                load_to(sp, first, lambda c: (out_done, ntiles * (c - first + 1)))
                sp.wait_ge(g_landed, 16)

            @block.scalar
            def _(act):
                if i == 1:
                    act.activation(gate, gate, ACT.Silu).then_inc(silu_done, 1)
                act.wait_ge(var_ready, 1)
                act.activation(rstd, ss, ACT.Sqrt).then_inc(std_ready, 1)
                for n in range(ntiles):
                    act.wait_ge(o_psum, n + 1)
                    for b in range(2):
                        ins = act.activation(oT[:, 4 * b:4 * b + 4, n * P:(n + 1) * P],
                                             ps[:, 2 * (n % 2) + b, :].rearrange("p (k n) -> p k n", n=P), ACT.Copy)
                    ins.then_inc(o_evac, 1)

            @block.vector
            def _(dve):
                then = Steps(dve, step)
                dve.wait_ge(g_landed, 16)
                if i == 0:
                    then(dve.tensor_scalar(sub_g, sub_g, 1.0 - LAM_INIT, None, ALU.mult))
                for n in range(ntiles):
                    then(dve.tensor_tensor(sq[:, 0:wn], O[:, n, 0:wn], O[:, n, 0:wn], ALU.mult))
                    then(dve.tensor_reduce(ss[:, n * nh:(n + 1) * nh], sq[:, 0:wn].rearrange("p (h d) -> p h d", d=dv), AX.X, ALU.add))
                dve.tensor_scalar(ss, ss, 1.0 / dv, EPS, ALU.mult, ALU.add).then_inc(var_ready, 1)
                dve.wait_ge(std_ready, 1)
                then(dve.reciprocal(rstd, rstd))
                if i == 1:
                    dve.wait_ge(silu_done, 1)
                for n in range(ntiles):
                    for h in range(nh):
                        part = O[:, n, h * dv:(h + 1) * dv]
                        ins = dve.scalar_tensor_tensor(part, part, rstd[:, n * nh + h:n * nh + h + 1], sub_g, ALU.mult, ALU.mult)
                    if i == 1:
                        then(ins)
                        ins = dve.tensor_tensor(O[:, n, :], O[:, n, :], gate[:, n, :], ALU.mult)
                    ins.then_inc(o_ready, 1)
                for m, (c, n) in enumerate(groups):
                    cols = slice(c * HALF, (c + 1) * HALF)
                    dve.wait_ge(out_done, m + 1)
                    v = 0 if n < XT else 1
                    dve.tensor_tensor(sq[:, (m % 2) * HALF:(m % 2 + 1) * HALF], ps[:, 4 + m % 4, :], mod[:, v, G1, cols], ALU.mult).then_inc(x_done, 1)
                    dve.wait_ge(x_done, m + 1)
                    then(dve.tensor_tensor(X[:, n, cols], X[:, n, cols], sq[:, (m % 2) * HALF:(m % 2 + 1) * HALF], ALU.add))

            @block.tensor
            def _(pe):
                for n in range(ntiles):
                    pe.wait_ge(o_ready, n + 1)
                    if n >= 2:
                        pe.wait_ge(o_evac, n - 1)
                    for k in range(KD):
                        ins = pe.transpose(ps[:, 2 * (n % 2) + k // 4, (k % 4) * P:(k % 4 + 1) * P],
                                           O[:, n, k * P:(k + 1) * P], ident)
                    ins.then_inc(o_psum, 1)
                for m, (c, n) in enumerate(groups):
                    w = T.chunk(first + c)
                    if n == 0:
                        T.wait_chunk(pe, first + c)
                    if m < ntiles:
                        pe.wait_ge(o_evac, m + 1)
                    if m >= 4:
                        pe.wait_ge(x_done, m - 3)
                    for k in range(KD):
                        ins = pe.matmul(ps[:, 4 + m % 4, :], oT[:, k, n * P:(n + 1) * P], w[:, k, :], start=(k == 0), stop=(k == KD - 1))
                    ins.then_inc(out_done, 1)


def expert_weights(T, i, kind, e):
    w = T.t[f"moe_{kind}"][i]
    if isinstance(e, int):
        w = w[e:e + 1]
    else:
        w = w[bass.ds(e, 1)]
    return w.rearrange("o (k p) n -> p (o k) n", p=P)


def expert_slot(T, kind, e):
    s = 3 * (e % 2) + ("w1", "w3", "w2").index(kind)
    return T.slot(s) if kind != "w2" else T.f(RING + s * CH, DE // P, D)


def first_expert_loads(T, sp, i):
    for e in range(2):
        for kind in ("w1", "w3", "w2"):
            sp.dma_start(expert_slot(T, kind, e), expert_weights(T, i, kind, e)).then_inc(T.w_landed[kind][e], 16)


def route_stage(T, i, nt):
    nc, t, f, ps = T.nc, T.t, T.f, T.ps
    hT = f(HI, KD, NT * P)
    cap = nt * P
    nb = nt - 1
    nov = 2 * nt - 1
    at = [HI + 4 * D]

    def take(*shape):
        v = f(at[0], *shape)
        at[0] += int(np.prod(shape))
        return v

    pick = take(2 * nt, cap)
    rw = take(KD, NE)
    tri, iota_cap = take(P), take(cap)
    sc, sel, ing, m1, m2, cand, oh0, oh1, rank = (take(nt, NE) for _ in range(9))
    pair = take(nt, NG, 6)
    gs, geq, gc = (take(nt, NG) for _ in range(3))
    gmx, grp, mxv, e0, e1, w0, w1, r0, r1, wsum = (take(nt) for _ in range(10))
    ohtok = take(2 * nt, NE)
    prod = take(nt, NE)
    cnt = take(NE)
    rows = take(nt, NE)
    ovf = take(NE, nb)
    ovp = take(2, 32 + NE * nb)
    ovs = take(nov, NE * nb)
    ovm = take(nov, NE * nb)
    ovr, ovk, ovl = take(2, nov), take(2, NE, nb), take(NE, nb)
    nov_f = take(1)
    ebase = take(NE)
    assert at[0] <= END, at[0]
    i16 = f(KEEP + K_IOTA, NE)
    tok = f(KEEP + K_TOK, NT)
    rbias = f(KEEP + K_RBIAS, NE)
    ones = f(KEEP + K_ONE, P)
    gate = f(KEEP + K_GATE, 2, NT)
    slot = f(KEEP + K_SLOT, 2, NT).bitcast(U32)
    rows_u = f(KEEP + K_ROWS, NT, NE).bitcast(U32)
    S3 = (P, nt, NE)
    with ExitStack() as ctx:
        in_landed, logits, sig, masks, ranks, picked, listed, step = T.sems(
            ctx, *[f"r{i}_{n}" for n in ("in_landed", "logits", "sigmoid", "masks", "ranks", "picked", "listed", "step")])
        with nc.Block() as block:
            @block.sync
            def _(sp):
                sp.dma_start(rw, t["router_w"].rearrange("(k p) e -> p k e", p=P)).then_inc(in_landed, 16)
                sp.dma_start(tri, t["k_before"]).then_inc(in_landed, 16)
                sp.dma_start(iota_cap, t["k_iota512"][:, 0:cap].partition_broadcast(P)).then_inc(in_landed, 16)
                sp.dma_start(ovk, t[f"k_over{i}"].partition_broadcast(P)).then_inc(in_landed, 16)
                first_expert_loads(T, sp, i)
                sp.wait_ge(in_landed, 64)

            @block.tensor
            def _(pe):
                pe.wait_ge(in_landed, 64)
                for n in range(nt):
                    for k in range(KD):
                        ins = pe.matmul(ps[:, 0, n * NE:(n + 1) * NE], hT[:, k, n * P:(n + 1) * P], rw[:, k, :],
                                        start=(k == 0), stop=(k == KD - 1))
                ins.then_inc(logits, 1)
                pe.wait_ge(masks, 1)
                for n in range(nt):
                    for m in range(n + 1):
                        pe.matmul(ps[:, 1, n * NE:(n + 1) * NE], ones if m < n else tri, prod[:, m, :], start=(m == 0), stop=(m == n))
                for m in range(nt):
                    ins = pe.matmul(ps[:, 1, nt * NE:(nt + 1) * NE], ones, prod[:, m, :], start=(m == 0), stop=(m == nt - 1))
                ins.then_inc(ranks, 1)
                pe.wait_ge(picked, 1)
                for b in range(nt):
                    for m in range(2 * nt):
                        ins = pe.matmul(ps[:, 2, b * NE:(b + 1) * NE], pick[:, m, b * P:(b + 1) * P], ohtok[:, m, :],
                                        start=(m == 0), stop=(m == 2 * nt - 1))
                ins.then_inc(listed, 1)

            @block.scalar
            def _(act):
                act.wait_ge(logits, 1)
                act.activation(sc, ps[:, 0, 0:nt * NE].rearrange("p (n e) -> p n e", e=NE), ACT.Sigmoid).then_inc(sig, 1)

            @block.vector
            def _(dve):
                then = Steps(dve, step)
                tt, ts, stt, red = dve.tensor_tensor, dve.tensor_scalar, dve.scalar_tensor_tensor, dve.tensor_reduce
                dve.wait_ge(sig, 1)
                then(tt(sel, sc, bc(rbias, 1, S3), ALU.add))
                s4 = sel.rearrange("p n (g e) -> p n g e", e=EPG)
                tt(pair[:, :, :, 0:3], s4[:, :, :, 0:3], s4[:, :, :, 1:4], ALU.add)
                tt(pair[:, :, :, 3:5], s4[:, :, :, 0:2], s4[:, :, :, 2:4], ALU.add)
                then(tt(pair[:, :, :, 5:6], s4[:, :, :, 0:1], s4[:, :, :, 3:4], ALU.add))
                then(red(gs, pair, AX.X, ALU.max))
                then(red(gmx, gs, AX.X, ALU.max))
                then(tt(geq, gs, bc(gmx, 2, (P, nt, NG)), ALU.is_equal))
                then(ts(geq, geq, -64.0, 64.0, ALU.mult, ALU.add))
                then(tt(gc, geq, bc(i16[:, 0:NG], 1, (P, nt, NG)), ALU.add))
                then(red(grp, gc, AX.X, ALU.min))
                then(tt(geq, bc(i16[:, 0:NG], 1, (P, nt, NG)), bc(grp, 2, (P, nt, NG)), ALU.is_equal))
                then(dve.tensor_copy(ing.rearrange("p n (g e) -> p n g e", e=EPG), bc(geq, 3, (P, nt, NG, EPG))))
                then(ts(m2, ing, 1.0, BIG, ALU.subtract, ALU.mult))
                then(tt(m1, sel, ing, ALU.mult))
                then(tt(m1, m1, m2, ALU.add))
                for oh, e in ((oh0, e0), (oh1, e1)):
                    then(red(mxv, m1, AX.X, ALU.max))
                    then(tt(cand, m1, bc(mxv, 2, S3), ALU.is_equal))
                    then(ts(cand, cand, -64.0, 64.0, ALU.mult, ALU.add))
                    then(tt(cand, cand, bc(i16, 1, S3), ALU.add))
                    then(red(e, cand, AX.X, ALU.min))
                    then(tt(oh, bc(i16, 1, S3), bc(e, 2, S3), ALU.is_equal))
                    if oh is oh0:
                        then(stt(m1, oh, -BIG, m1, ALU.mult, ALU.add))
                dve.tensor_tensor(prod, oh0, oh1, ALU.add).then_inc(masks, 1)
                for oh, w in ((oh0, w0), (oh1, w1)):
                    then(tt(cand, sc, oh, ALU.mult))
                    then(red(w, cand, AX.X, ALU.add))
                then(tt(wsum, w0, w1, ALU.add))
                then(dve.reciprocal(wsum, wsum))
                tt(gate[:, 0, 0:nt], w0, wsum, ALU.mult)
                tt(gate[:, 1, 0:nt], w1, wsum, ALU.mult)
                for m, oh in enumerate((oh0, oh1)):
                    ins = tt(ohtok[:, m * nt:(m + 1) * nt, :], oh, bc(tok[:, 0:nt], 2, S3), ALU.mult)
                then(ins)
                dve.wait_ge(ranks, 1)
                dve.tensor_copy(cnt, ps[:, 1, nt * NE:(nt + 1) * NE])
                then(dve.tensor_copy(rank, ps[:, 1, 0:nt * NE].rearrange("p (n e) -> p n e", e=NE)))
                for m, (oh, e, r) in enumerate(((oh0, e0, r0), (oh1, e1, r1))):
                    then(tt(cand, rank, oh, ALU.mult))
                    then(red(r, cand, AX.X, ALU.add))
                    for n in range(nt):
                        ins = ts(pick[:, m * nt + n, :], iota_cap, r[:, n:n + 1], None, ALU.is_equal)
                ins.then_inc(picked, 1)
                ovflat = ovf.rearrange("p e b -> p (e b)")
                then(tt(ovf, bc(cnt, 2, (P, NE, nb)), ovk[:, 0], ALU.is_gt))
                then(red(nov_f, ovflat, AX.X, ALU.add))
                then(dve.tensor_copy(f(KEEP + K_NOV, 1).bitcast(I32), nov_f))
                width = NE * nb
                then(dve.memset(ovp, 0.0))
                then(dve.tensor_copy(ovp[:, 0, 32:32 + width], ovflat))
                src, d = 0, 1
                while d < width:
                    then(tt(ovp[:, 1 - src, 32:32 + width], ovp[:, src, 32:32 + width], ovp[:, src, 32 - d:32 - d + width], ALU.add))
                    src, d = 1 - src, 2 * d
                run = ovp[:, src, 32:32 + width].rearrange("p (e b) -> p e b", b=nb)[:, :, 0]
                then(tt(ebase, run, ovf[:, :, 0], ALU.subtract))
                then(ts(ebase, ebase, float(P), float((NE - 1) * P), ALU.mult, ALU.add))
                for m, (oh, e, r) in enumerate(((oh0, e0, r0), (oh1, e1, r1))):
                    then(tt(cand, oh, bc(ebase, 1, S3), ALU.mult))
                    then(red(mxv, cand, AX.X, ALU.add))
                    then(stt(mxv, e, -float(P), mxv, ALU.mult, ALU.add))
                    then(ts(wsum, r, float(P), None, ALU.is_ge))
                    then(tt(mxv, mxv, wsum, ALU.mult))
                    then(stt(mxv, e, float(P), mxv, ALU.mult, ALU.add))
                    then(tt(mxv, mxv, r, ALU.add))
                    then(dve.tensor_copy(slot[:, m, 0:nt], mxv))
                then(tt(ovs, bc(ovp[:, src, 32:32 + width], 1, (P, nov, width)),
                        bc(iota_cap[:, 1:nov + 1], 2, (P, nov, width)), ALU.is_equal))
                then(tt(ovs, ovs, bc(ovflat, 1, (P, nov, width)), ALU.mult))
                then(tt(ovm, ovs, bc(ovk[:, 1].rearrange("p e b -> p (e b)"), 1, (P, nov, width)), ALU.mult))
                then(red(ovr[:, 1, :], ovm, AX.X, ALU.add))
                dve.wait_ge(listed, 1)
                then(dve.tensor_copy(rows, ps[:, 2, 0:nt * NE].rearrange("p (b e) -> p b e", e=NE)))
                dve.tensor_copy(rows_u[:, 0:nt, :], rows)
                for b in range(nb):
                    ins = dve.tensor_copy(ovl[:, :, b], rows[:, b + 1, :])
                then(ins)
                then(tt(ovm, ovs, bc(ovl.rearrange("p e b -> p (e b)"), 1, (P, nov, width)), ALU.mult))
                then(red(ovr[:, 0, :], ovm, AX.X, ALU.add))
                dve.tensor_copy(f(KEEP + K_OVIDX, nov).bitcast(U32), ovr[:, 0, :])
                dve.tensor_copy(f(KEEP + K_OVEXP, nov).bitcast(I32), ovr[:, 1, :])



class ExpertBuffers:
    def __init__(self, T):
        f, at = T.f, HI
        self.rows = f(at, 2, D)
        self.rT = f(at + 2 * D, 2, KD, P)
        self.s = f(at + 4 * D, DE)
        self.g = f(at + 4 * D + DE, DE)
        self.gT = f(at + 5 * D, DE // P, P)
        self.y = f(at + 6 * D, 2, D)


def moe_stage(T, i, nt):
    nc, t, f, ps = T.nc, T.t, T.f, T.ps
    B = ExpertBuffers(T)
    ident = f(KEEP + K_ID, P)
    rows_u = f(KEEP + K_ROWS, NT, NE).bitcast(U32)
    base = T.w_base[i]
    with ExitStack() as ctx:
        (rows_turned, rT_ready, up_done, act_done, lin_done, g_ready, g_turned, gT_ready,
         y_psum, y_ready, y_stored0, y_stored1, rows_landed0, rows_landed1) = T.sems(
            ctx, *[f"m{i}_{n}" for n in ("rows_turned", "rT_ready", "up_done", "act_done",
                                         "lin_done", "g_ready", "g_turned", "gT_ready", "y_psum", "y_ready", "y_stored0", "y_stored1", "rows_landed0", "rows_landed1")])
        y_stored, rows_landed = (y_stored0, y_stored1), (rows_landed0, rows_landed1)
        with nc.Block() as block:
            @block.gpsimd
            def _(pool):
                for e in range(NE):
                    if e >= 2:
                        pool.wait_ge(rows_turned, e - 1)
                    pool.indirect_dma_start(B.rows[:, e % 2, :], None, T.h2_dram,
                                            bass.IndirectOffsetOnAxis(ap=rows_u[:, 0, e:e + 1], axis=0)).then_inc(rows_landed[e % 2], 16)

            @block.sync
            def _(sp):
                with sp.Fori(0, (NE - 2) // 2) as n:
                    for s in range(2):
                        e = n * 2 + (2 + s)
                        for kind, done in (("w1", up_done), ("w3", lin_done), ("w2", y_psum)):
                            sp.wait_ge(done, e - 1)
                            sp.dma_start(expert_slot(T, kind, s), expert_weights(T, i, kind, e))\
                              .then_inc(T.w_landed[kind][s], 16)

            @block.tensor
            def _(pe):
                def arrived(kind, s, m):
                    pe.wait_ge(T.w_landed[kind][s], (m + 1) * 16 + base)

                def up(e, s, m):
                    pe.wait_ge(rT_ready, (e + 1) * 2)
                    if not isinstance(e, int) or e >= 1:
                        pe.wait_ge(act_done, e)
                    arrived("w1", s, m)
                    w = expert_slot(T, "w1", s)
                    for k in range(KD):
                        ins = pe.matmul(ps[:, 0, :], B.rT[:, s, k, :], w[:, k, :], start=(k == 0), stop=(k == KD - 1))
                    ins.then_inc(up_done, 1)

                def linear(e, s, m):
                    if not isinstance(e, int) or e >= 1:
                        pe.wait_ge(g_ready, e)
                    arrived("w3", s, m)
                    w = expert_slot(T, "w3", s)
                    for k in range(KD):
                        ins = pe.matmul(ps[:, 1, :], B.rT[:, s, k, :], w[:, k, :], start=(k == 0), stop=(k == KD - 1))
                    ins.then_inc(lin_done, 1)

                def turn_rows(e, s, m):
                    pe.wait_ge(rows_landed[s], (m + 1) * 16)
                    if not isinstance(e, int) or e >= 1:
                        pe.wait_ge(rT_ready, e * 2)
                    for k in range(KD):
                        ins = pe.transpose(ps[:, 2 + k // 4, (k % 4) * P:(k % 4 + 1) * P], B.rows[:, s, k * P:(k + 1) * P], ident)
                    ins.then_inc(rows_turned, 1)

                def turn_hidden(e):
                    pe.wait_ge(g_ready, e + 1)
                    if not isinstance(e, int) or e >= 1:
                        pe.wait_ge(gT_ready, e)
                    for k in range(DE // P):
                        ins = pe.transpose(ps[:, 4, k * P:(k + 1) * P], B.g[:, k * P:(k + 1) * P], ident)
                    ins.then_inc(g_turned, 1)

                def down(e, s, m):
                    pe.wait_ge(gT_ready, e + 1)
                    if not isinstance(e, int) or e >= 1:
                        pe.wait_ge(y_ready, e * 2)
                    arrived("w2", s, m)
                    w = expert_slot(T, "w2", s)
                    for h in range(2):
                        for k in range(DE // P):
                            ins = pe.matmul(ps[:, 5 + h, :], B.gT[:, k, :], w[:, k, h * HALF:(h + 1) * HALF],
                                            start=(k == 0), stop=(k == DE // P - 1))
                    ins.then_inc(y_psum, 1)

                turn_rows(0, 0, 0)
                up(0, 0, 0)
                linear(0, 0, 0)
                turn_rows(1, 1, 0)
                for e in (1, 2):
                    up(e, e % 2, e // 2)
                    turn_hidden(e - 1)
                    linear(e, e % 2, e // 2)
                    turn_rows(e + 1, (e + 1) % 2, (e + 1) // 2)
                    down(e - 1, (e - 1) % 2, (e - 1) // 2)
                with pe.Fori(0, (NE - 4) // 2) as n:
                    for s in range(2):
                        e = n * 2 + (3 + s)
                        up(e, (1 + s) % 2, n + (1 + s))
                        turn_hidden(e - 1)
                        linear(e, (1 + s) % 2, n + (1 + s))
                        turn_rows(e + 1, s, n + 2)
                        down(e - 1, s, n + 1)
                e = NE - 1
                up(e, 1, NE // 2 - 1)
                turn_hidden(e - 1)
                linear(e, 1, NE // 2 - 1)
                down(e - 1, 0, NE // 2 - 1)
                turn_hidden(e)
                down(e, 1, NE // 2 - 1)

            @block.scalar
            def _(act):
                def silu(e):
                    act.wait_ge(up_done, e + 1)
                    if not isinstance(e, int) or e >= 1:
                        act.wait_ge(g_ready, e)
                    act.activation(B.s, ps[:, 0, :], ACT.Silu).then_inc(act_done, 1)

                def copy_rT(e, s):
                    act.wait_ge(rows_turned, e + 1)
                    if not isinstance(e, int) or e >= 2:
                        act.wait_ge(lin_done, e - 1)
                    act.activation(B.rT[:, s, 0:4, :], ps[:, 2, :].rearrange("p (k n) -> p k n", n=P), ACT.Copy).then_inc(rT_ready, 1)

                def copy_y(e, s, m):
                    act.wait_ge(y_psum, e + 1)
                    if not isinstance(m, int) or m >= 1:
                        act.wait_ge(y_stored[s], m * 16)
                    act.activation(B.y[:, s, 0:HALF], ps[:, 5, :], ACT.Copy).then_inc(y_ready, 1)
                    act.wait_ge(y_ready, (e + 1) * 2)
                    to = T.y_dram[e * P:(e + 1) * P, :] if isinstance(e, int) else T.y_dram[bass.ds(e * P, P), :]
                    act.dma_start(to, B.y[:, s, :]).then_inc(y_stored[s], 16)

                copy_rT(0, 0)
                silu(0)
                copy_rT(1, 1)
                silu(1)
                copy_rT(2, 0)
                copy_y(0, 0, 0)
                silu(2)
                copy_rT(3, 1)
                copy_y(1, 1, 0)
                with act.Fori(0, (NE - 4) // 2) as n:
                    for s in range(2):
                        e = n * 2 + (3 + s)
                        silu(e)
                        copy_rT(e + 1, s)
                        copy_y(e - 1, s, n + 1)
                silu(NE - 1)
                copy_y(NE - 2, 0, NE // 2 - 1)
                copy_y(NE - 1, 1, NE // 2 - 1)
                for stored in y_stored:
                    act.wait_ge(stored, NE // 2 * 16)

            @block.vector
            def _(dve):
                def copy_rT(e, s):
                    dve.wait_ge(rows_turned, e + 1)
                    if not isinstance(e, int) or e >= 2:
                        dve.wait_ge(lin_done, e - 1)
                    dve.tensor_copy(B.rT[:, s, 4:8, :], ps[:, 3, :].rearrange("p (k n) -> p k n", n=P)).then_inc(rT_ready, 1)

                def copy_gT(e):
                    dve.wait_ge(g_turned, e + 1)
                    if not isinstance(e, int) or e >= 1:
                        dve.wait_ge(y_psum, e)
                    dve.tensor_copy(B.gT, ps[:, 4, :].rearrange("p (k n) -> p k n", n=P)).then_inc(gT_ready, 1)

                def product(e):
                    dve.wait_ge(act_done, e + 1)
                    dve.wait_ge(lin_done, e + 1)
                    if not isinstance(e, int) or e >= 1:
                        dve.wait_ge(g_turned, e)
                    dve.tensor_tensor(B.g, ps[:, 1, :], B.s, ALU.mult).then_inc(g_ready, 1)

                def copy_y(e, s, m):
                    dve.wait_ge(y_psum, e + 1)
                    if not isinstance(m, int) or m >= 1:
                        dve.wait_ge(y_stored[s], m * 16)
                    dve.tensor_copy(B.y[:, s, HALF:D], ps[:, 6, :]).then_inc(y_ready, 1)

                copy_rT(0, 0)
                product(0)
                copy_rT(1, 1)
                for e in (1, 2):
                    copy_gT(e - 1)
                    product(e)
                    copy_rT(e + 1, (e + 1) % 2)
                    copy_y(e - 1, (e - 1) % 2, 0)
                with dve.Fori(0, (NE - 4) // 2) as n:
                    for s in range(2):
                        e = n * 2 + (3 + s)
                        copy_gT(e - 1)
                        product(e)
                        copy_rT(e + 1, s)
                        copy_y(e - 1, s, n + 1)
                copy_gT(NE - 2)
                product(NE - 1)
                copy_y(NE - 2, 0, NE // 2 - 1)
                copy_gT(NE - 1)
                copy_y(NE - 1, 1, NE // 2 - 1)


def overflow_stage(T, i, nt):
    nc, t, f, ps = T.nc, T.t, T.f, T.ps
    B = ExpertBuffers(T)
    nov = 2 * nt - 1
    ident = f(KEEP + K_ID, P)
    count = f(KEEP + K_NOV, 1).bitcast(I32)[0:1, :]
    ov_idx = f(KEEP + K_OVIDX, nov).bitcast(U32)
    ov_exp = f(KEEP + K_OVEXP, nov).bitcast(I32)
    cur = f(KEEP + K_CUR, 1).bitcast(U32)
    with ExitStack() as ctx:
        (idx_ready, rows_landed, w_landed, rows_turned, rT_ready, up_done, act_done, g_ready, g_turned,
         gT_ready, y_psum, y_ready, y_stored) = T.sems(
            ctx, *[f"v{i}_{n}" for n in ("idx_ready", "rows_landed", "w_landed", "rows_turned", "rT_ready", "up_done",
                                         "act_done", "g_ready", "g_turned", "gT_ready", "y_psum", "y_ready", "y_stored")])

        def repeated(engine, body):
            n_tiles = engine.value_load(count, min_val=0, max_val=nov)
            with engine.If(n_tiles > 0):
                with engine.Fori(0, n_tiles) as n:
                    body(n)
                engine.nop()
            with engine.Else():
                engine.nop()
            engine.nop()

        with nc.Block() as block:
            @block.gpsimd
            def _(pool):
                def tile(n):
                    pool.tensor_copy(cur, ov_idx[:, bass.ds(n, 1)])
                    pool.drain()
                    pool.indirect_dma_start(B.rows[:, 0, :], None, T.h2_dram, bass.IndirectOffsetOnAxis(ap=cur, axis=0))\
                        .then_inc(rows_landed, 16)
                    pool.wait_ge(y_stored, (n + 1) * 16)
                repeated(pool, tile)

            @block.sync
            def _(sp):
                def tile(n):
                    sp.wait_ge(rows_landed, (n + 1) * 16)
                    e = sp.value_load(ov_exp[0:1, bass.ds(n, 1)], min_val=0, max_val=NE - 1)
                    for kind in ("w1", "w3", "w2"):
                        sp.dma_start(expert_slot(T, kind, 0), expert_weights(T, i, kind, e)).then_inc(w_landed, 16)
                repeated(sp, tile)

            @block.tensor
            def _(pe):
                def tile(n):
                    pe.wait_ge(rows_landed, (n + 1) * 16)
                    pe.wait_ge(w_landed, (n + 1) * 48)
                    for k in range(KD):
                        ins = pe.transpose(ps[:, 2 + k // 4, (k % 4) * P:(k % 4 + 1) * P], B.rows[:, 0, k * P:(k + 1) * P], ident)
                    ins.then_inc(rows_turned, 1)
                    pe.wait_ge(rT_ready, n + 1)
                    for b, kind in enumerate(("w1", "w3")):
                        w = expert_slot(T, kind, 0)
                        for k in range(KD):
                            ins = pe.matmul(ps[:, b, :], B.rT[:, 0, k, :], w[:, k, :], start=(k == 0), stop=(k == KD - 1))
                    ins.then_inc(up_done, 1)
                    pe.wait_ge(g_ready, n + 1)
                    for k in range(DE // P):
                        ins = pe.transpose(ps[:, 4, k * P:(k + 1) * P], B.g[:, k * P:(k + 1) * P], ident)
                    ins.then_inc(g_turned, 1)
                    pe.wait_ge(gT_ready, n + 1)
                    w = expert_slot(T, "w2", 0)
                    for h in range(2):
                        for k in range(DE // P):
                            ins = pe.matmul(ps[:, 5 + h, :], B.gT[:, k, :], w[:, k, h * HALF:(h + 1) * HALF],
                                            start=(k == 0), stop=(k == DE // P - 1))
                    ins.then_inc(y_psum, 1)
                repeated(pe, tile)

            @block.scalar
            def _(act):
                def tile(n):
                    act.wait_ge(up_done, n + 1)
                    act.activation(B.s, ps[:, 0, :], ACT.Silu).then_inc(act_done, 1)
                    act.wait_ge(y_ready, n + 1)
                    act.dma_start(T.y_dram[bass.ds(n * P + NE * P, P), :], B.y[:, 0, :]).then_inc(y_stored, 16)
                    act.wait_ge(y_stored, (n + 1) * 16)
                repeated(act, tile)

            @block.vector
            def _(dve):
                def tile(n):
                    dve.wait_ge(rows_turned, n + 1)
                    dve.tensor_copy(B.rT[:, 0].rearrange("p k n -> p (k n)"), ps[:, 2:4, :].rearrange("p b n -> p (b n)")).then_inc(rT_ready, 1)
                    dve.wait_ge(act_done, n + 1)
                    dve.tensor_tensor(B.g, ps[:, 1, :], B.s, ALU.mult).then_inc(g_ready, 1)
                    dve.wait_ge(g_turned, n + 1)
                    dve.tensor_copy(B.gT, ps[:, 4, :].rearrange("p (k n) -> p k n", n=P)).then_inc(gT_ready, 1)
                    dve.wait_ge(y_psum, n + 1)
                    dve.tensor_copy(B.y[:, 0, :], ps[:, 5:7, :].rearrange("p b n -> p (b n)")).then_inc(y_ready, 1)
                repeated(dve, tile)


def combine_stage(T, i, nt, load_to):
    nc, t, f = T.nc, T.t, T.f
    X, mod = f(XR, NT, D), f(MOD, 2, 6, D)
    y = f(HI, 2, 2, D)
    gate, slot = f(KEEP + K_GATE, 2, NT), f(KEEP + K_SLOT, 2, NT).bitcast(U32)
    with ExitStack() as ctx:
        y_landed0, y_landed1, tile_done, step = T.sems(ctx, *[f"c{i}_{n}" for n in ("y_landed0", "y_landed1", "tile_done", "step")])
        y_landed = (y_landed0, y_landed1)
        with nc.Block() as block:
            @block.gpsimd
            def _(pool):
                for n in range(nt):
                    if n >= 2:
                        pool.wait_ge(tile_done, n - 1)
                    for m in range(2):
                        pool.indirect_dma_start(y[:, n % 2, m, :], None, T.y_dram,
                                                bass.IndirectOffsetOnAxis(ap=slot[:, m, n:n + 1], axis=0)).then_inc(y_landed[n % 2], 16)

            @block.sync
            def _(sp):
                load_to(sp)

            @block.vector
            def _(dve):
                then = Steps(dve, step)
                for n in range(nt):
                    v = 0 if n < XT else 1
                    dve.wait_ge(y_landed[n % 2], 32 * (n // 2 + 1))
                    a, b = y[:, n % 2, 0, :], y[:, n % 2, 1, :]
                    then(dve.tensor_scalar(a, a, gate[:, 0, n:n + 1], None, ALU.mult))
                    then(dve.scalar_tensor_tensor(a, b, gate[:, 1, n:n + 1], a, ALU.mult, ALU.add))
                    then(dve.tensor_tensor(a, a, mod[:, v, G2, :], ALU.mult))
                    dve.tensor_tensor(X[:, n, :], X[:, n, :], a, ALU.add).then_inc(tile_done, 1)


QR, KR, VR, GT = LO, LO + XT * HALF, LO + XT * HALF + NT * HALF, LO + XT * HALF + NT * HALF + NT * D
LR, WG = GT + XT * D, GT + XT * D + 2 * HALF
GDEC = HI + 4 * D


def gla_project_stage(T):
    nc, t, f, ps = T.nc, T.t, T.f, T.ps
    first = 20 + 12
    hT = f(HI, KD, NT * P)
    q, k_, v, gate = f(QR, XT, HALF), f(KR, NT, HALF), f(VR, NT, D), f(GT, XT, D)
    lrT, w_lr = f(LR, 2, HALF), f(HI + 4 * D, KD, 2 * RANK)
    dests = [(q, 0, XT), (k_, 0, NT), (v, 0, NT), (v, HALF, NT), (gate, 0, XT), (gate, HALF, XT)]
    groups = [(c, n) for c in range(6) for n in range(dests[c][2])]
    ends = np.cumsum([d[2] for d in dests])
    with ExitStack() as ctx:
        lr_landed, proj_done, proj_evac, lr_done, lr_evac = T.sems(ctx, "lr_landed", "gproj_done", "gproj_evac", "lr_done", "lr_evac")
        with nc.Block() as block:
            @block.sync
            def _(sp):
                sp.dma_start(w_lr, t["gla_w_in"][0][:, 6 * HALF:].rearrange("(k p) n -> p k n", p=P)).then_inc(lr_landed, 16)
                T.load_chunks(sp, first + 6 + 2, first, lambda c: (proj_done, int(ends[c - first])))
                sp.wait_ge(lr_landed, 16)

            @block.tensor
            def _(pe):
                pe.wait_ge(lr_landed, 16)
                for d in range(2):
                    for k in range(KD):
                        ins = pe.matmul(ps[0:RANK, 4 + d, :], w_lr[:, k, d * RANK:(d + 1) * RANK], hT[:, k, :],
                                        start=(k == 0), stop=(k == KD - 1))
                ins.then_inc(lr_done, 1)
                for m, (c, n) in enumerate(groups):
                    w = T.chunk(first + c)
                    if n == 0:
                        T.wait_chunk(pe, first + c)
                    if m >= 4:
                        pe.wait_ge(proj_evac, m - 3)
                    for k in range(KD):
                        ins = pe.matmul(ps[:, m % 4, :], hT[:, k, n * P:(n + 1) * P], w[:, k, :], start=(k == 0), stop=(k == KD - 1))
                    ins.then_inc(proj_done, 1)

            @block.scalar
            def _(act):
                act.wait_ge(lr_done, 1)
                for d in range(2):
                    act.activation(lrT[0:RANK, d, :], ps[0:RANK, 4 + d, :], ACT.Copy)
                for m, (c, n) in enumerate(groups):
                    to, col, _ = dests[c]
                    act.wait_ge(proj_done, m + 1)
                    act.activation(to[:, n, col:col + HALF], ps[:, m % 4, :], ACT.Copy,
                                   scale=C_DK ** -0.5 if c == 0 else 1.0).then_inc(proj_evac, 1)


def decay_stage(T, load_to):
    nc, t, f, ps = T.nc, T.t, T.f, T.ps
    lrT, w_g = f(LR, 2, HALF), f(WG, 2, HALF)
    z, u = f(GDEC, 2 * NT, HALF), f(HI, 2 * NT, HALF)
    b_g = f(HI + 8 * D, 2, HALF)
    with ExitStack() as ctx:
        g_landed, z_psum, z_ready, u_in, u_out, ln_out, step = T.sems(
            ctx, "gate_landed", "z_psum", "z_ready", "u_in", "u_out", "ln_out", "decay_step")
        with nc.Block() as block:
            @block.sync
            def _(sp):
                sp.dma_start(w_g[0:RANK], t["gla_w_gate"][0].rearrange("d r n -> r d n")).then_inc(g_landed, 16)
                sp.dma_start(b_g, t["gla_b_gate"][0].partition_broadcast(P)).then_inc(g_landed, 16)
                load_to(sp)
                sp.wait_ge(g_landed, 32)

            @block.tensor
            def _(pe):
                pe.wait_ge(g_landed, 32)
                for m in range(2 * NT):
                    d, n = m // NT, m % NT
                    if m >= 4:
                        pe.wait_ge(z_ready, m - 3)
                    pe.matmul(ps[:, m % 4, :], lrT[0:RANK, d, n * P:(n + 1) * P], w_g[0:RANK, d, :], start=True, stop=True).then_inc(z_psum, 1)

            @block.vector
            def _(dve):
                then = Steps(dve, step)
                dve.wait_ge(g_landed, 32)
                for m in range(2 * NT):
                    dve.wait_ge(z_psum, m + 1)
                    dve.tensor_tensor(z[:, m, :], ps[:, m % 4, :], b_g[:, m // NT, :], ALU.add).then_inc(z_ready, 1)
                    dve.wait_ge(z_ready, m + 1)
                    dve.scalar_tensor_tensor(u[:, m, :], z[:, m, :], -1.0, z[:, m, :], ALU.mult, ALU.min).then_inc(u_in, 1)
                for m in range(2 * NT):
                    dve.wait_ge(ln_out, m + 1)
                    dve.scalar_tensor_tensor(z[:, m, :], z[:, m, :], 0.0, u[:, m, :], ALU.min, ALU.subtract)

            @block.scalar
            def _(act):
                for m in range(2 * NT):
                    act.wait_ge(u_in, m + 1)
                    act.activation(u[:, m, :], u[:, m, :], ACT.Exp).then_inc(u_out, 1)
                for m in range(2 * NT):
                    act.wait_ge(u_out, m + 1)
                    act.activation(u[:, m, :], u[:, m, :], ACT.Ln, bias=1.0).then_inc(ln_out, 1)


SPARE = MOD + 8 * D
GO = SPARE
GSTATE = SPARE + 2 * D


def gla_stage(T, load_to):
    nc, t, f, ps = T.nc, T.t, T.f, T.ps
    q, k_, v = f(QR, XT, HALF), f(KR, NT, HALF), f(VR, NT, D)
    g = f(GDEC, 2, NT, HALF)
    ke = f(HI, 2, NT, HALF)
    c0 = HI + 8 * D
    tm, end_x, end_c, all16, low = f(c0, 2, 2, P), f(c0 + 4 * P, 2, P), f(c0 + 6 * P, 2, P), f(c0 + 8 * P, P), f(c0 + 9 * P, 2, CHUNK)
    wk = c0 + 10 * P
    ex = f(wk, 3, XT, P)
    qkm = f(wk + 3 * XT * P, 3, XT, P)
    qT, kT = f(LR, C_HEADS, XT * P), f(LR + C_HEADS * XT * P, C_HEADS, XT * P)
    aT = f(LR + 2 * C_HEADS * XT * P, 2, XT, P)
    state = f(GSTATE, 2, 4, C_DV)
    O = f(GO, XT, D)
    ident = f(KEEP + K_ID, P)
    NCH = SEQ // CHUNK
    units = [(h, d) for h in range(C_HEADS) for d in range(2)]
    order = {0: list(range(NCH)), 1: list(range(NCH - 1, -1, -1))}

    def product(d, c):
        if c is None:
            bank, half = (3, 1) if d == 0 else (2, 1)
        else:
            bank, half = 2 + c % 2, (0 if c in (order[d][0], order[d][1]) else 1)
        return ps[:, bank, half * C_DV:(half + 1) * C_DV]
    with ExitStack() as ctx:
        (tab_landed, turned, turn_evac, e_psum, e_exp, ke_ready, t_psum, t_exp, qk_ready, a_psum, a_ready,
         s_psum, s_ready, o_psum, o_ready, zeroed, step) = T.sems(
            ctx, *[f"g_{n}" for n in ("tab_landed", "turned", "turn_evac", "e_psum", "e_exp", "ke_ready", "t_psum",
                                      "t_exp", "qk_ready", "a_psum", "a_ready", "s_psum", "s_ready", "o_psum", "o_ready",
                                      "zeroed", "step")])
        with nc.Block() as block:
            @block.sync
            def _(sp):
                for to, name in ((tm.rearrange("p a b n -> p (a b n)"), "k_sums"), (end_x.rearrange("p a n -> p (a n)"), "k_ends"),
                                 (end_c.rearrange("p a n -> p (a n)"), "k_ends_ctx"), (all16, "k_all"),
                                 (low.rearrange("p a n -> p (a n)"), "k_low")):
                    sp.dma_start(to, t[name]).then_inc(tab_landed, 16)
                load_to(sp)
                sp.wait_ge(tab_landed, 80)

            @block.tensor
            def _(pe):
                pe.wait_ge(tab_landed, 80)
                for n, src in enumerate((q, k_)):
                    for m in range(XT * C_HEADS):
                        h, tile = m // XT, m % XT
                        ins = pe.transpose(ps[:, 2 * n + h // 2, (h % 2) * XT * P + tile * P:(h % 2) * XT * P + (tile + 1) * P],
                                           src[:, tile, h * P:(h + 1) * P], ident)
                    ins.then_inc(turned, 1)
                m = 0
                for d in range(2):
                    for tile in range(NT):
                        bank = 4 + m % 4
                        if m >= 4:
                            pe.wait_ge(e_exp, m - 3)
                        if tile < XT:
                            ins = pe.matmul(ps[:, bank, :], end_x[:, d, :], g[:, d, tile, :], start=True, stop=True)
                        else:
                            whole = (d == 0 and tile == XT) or (d == 1 and tile == NT - 1)
                            ins = pe.matmul(ps[:, bank, :], end_c[:, d, :], g[:, d, tile, :], start=True, stop=not whole)
                            if whole:
                                other = XT if d == 1 else NT - 1
                                ins = pe.matmul(ps[:, bank, :], all16, g[:, d, other, :], start=False, stop=True)
                        ins.then_inc(e_psum, 1)
                        m += 1

                def sums(n):
                    h, d = units[n]
                    pe.wait_ge(t_exp, n)
                    for tile in range(XT):
                        ins = pe.matmul(ps[:, 0, tile * 2 * P:(tile + 1) * 2 * P], g[:, d, tile, h * P:(h + 1) * P],
                                        tm[:, d].rearrange("p a n -> p (a n)"), start=True, stop=True)
                    ins.then_inc(t_psum, 1)

                def states(n):
                    h, d = units[n]
                    hv = slice(h * C_DV, (h + 1) * C_DV)
                    hk = slice(h * P, (h + 1) * P)
                    if n >= 1:
                        pe.wait_ge(s_ready, n)
                    for m, tile in enumerate(range(XT, NT)):
                        pe.matmul(product(d, None), ke[:, d, tile, hk], v[:, tile, hv], start=(m == 0), stop=(m == 1))
                    for m, c in enumerate(order[d][:-1]):
                        rows = slice((c % 2) * CHUNK, (c % 2 + 1) * CHUNK)
                        ins = pe.matmul(product(d, c), ke[rows, d, c // 2, hk],
                                        v[rows, c // 2, hv], start=True, stop=True)
                    ins.then_inc(s_psum, 1)

                def scores(n):
                    pe.wait_ge(qk_ready, n + 1)
                    if n >= 1:
                        pe.wait_ge(a_ready, n)
                    for tile in range(XT):
                        for c in range(2):
                            r = slice(c * CHUNK, (c + 1) * CHUNK)
                            ins = pe.matmul(ps[r, 1, tile * P:tile * P + CHUNK], qkm[:, 2, tile, r], qkm[:, 1, tile, r], start=True, stop=True)
                    ins.then_inc(a_psum, 1)

                def outputs(n):
                    h, d = units[n]
                    hv = slice(h * C_DV, (h + 1) * C_DV)
                    pe.wait_ge(a_ready, n + 1)
                    pe.wait_ge(s_ready, n + 1)
                    if d == 0 and h >= 2:
                        pe.wait_ge(o_ready, h - 1)
                    for tile in range(XT):
                        to = ps[:, 4 + 2 * (h % 2) + tile, 0:C_DV]
                        pe.matmul(to, aT[:, d, tile, :], v[:, tile, hv], start=(d == 0), stop=False, skip_group_check=True)
                        for c in range(2):
                            r = slice(c * CHUNK, (c + 1) * CHUNK)
                            ins = pe.matmul(ps[r, 4 + 2 * (h % 2) + tile, 0:C_DV], qkm[:, 0, tile, r], state[:, d, 2 * tile + c, :],
                                            start=False, stop=(d == 1), skip_group_check=True)
                    ins.then_inc(o_psum, 1)

                pe.wait_ge(turn_evac, 4)
                pe.wait_ge(e_exp, 8)
                pe.wait_ge(ke_ready, 8)
                for n in range(len(units)):
                    sums(n)
                    states(n)
                    scores(n)
                    outputs(n)

            @block.scalar
            def _(act):
                for n, to in enumerate((qT, kT)):
                    act.wait_ge(turned, n + 1)
                    for b in range(2):
                        act.activation(to[:, 2 * b:2 * b + 2, :], ps[:, 2 * n + b, :].rearrange("p (h n) -> p h n", n=XT * P),
                                       ACT.Copy).then_inc(turn_evac, 1)
                for m in range(2 * NT):
                    act.wait_ge(e_psum, m + 1)
                    act.activation(ke[:, m // NT, m % NT, :], ps[:, 4 + m % 4, :], ACT.Exp).then_inc(e_exp, 1)
                for n, (h, d) in enumerate(units):
                    act.wait_ge(t_psum, n + 1)
                    if n >= 1:
                        act.wait_ge(qk_ready, n)
                        act.wait_ge(s_ready, n)
                    bank = ps[:, 0, :].rearrange("p (t a n) -> p t a n", t=XT, a=2)
                    act.activation(ex[:, 0], bank[:, :, 0, :], ACT.Exp)
                    act.activation(ex[:, 1], bank[:, :, 1, :], ACT.Exp)
                    act.activation(ex[:, 2], bank[:, :, 1, :], ACT.Exp, scale=-1.0).then_inc(t_exp, 1)
                    if d == 1:
                        act.wait_ge(o_psum, n + 1)
                        for tile in range(XT):
                            ins = act.activation(O[:, tile, h * C_DV:(h + 1) * C_DV], ps[:, 4 + 2 * (h % 2) + tile, 0:C_DV], ACT.Copy)
                        ins.then_inc(o_ready, 1)

            @block.vector
            def _(dve):
                then = Steps(dve, step)
                dve.memset(aT, 0.0).then_inc(zeroed, 1)
                dve.wait_ge(zeroed, 1)
                dve.wait_ge(tab_landed, 80)
                for m in range(2 * NT):
                    dve.wait_ge(e_exp, m + 1)
                    to = ke[:, m // NT, m % NT, :]
                    dve.tensor_tensor(to, to, k_[:, m % NT, :], ALU.mult).then_inc(ke_ready, 1)
                dve.wait_ge(turn_evac, 4)
                for n, (h, d) in enumerate(units):
                    dve.wait_ge(t_exp, n + 1)
                    if n >= 1:
                        dve.wait_ge(o_psum, n)
                    qh, kh = (x[:, h, :].rearrange("p (t n) -> p t n", n=P) for x in (qT, kT))
                    dve.tensor_tensor(qkm[:, 0], qh, ex[:, 0], ALU.mult)
                    dve.tensor_tensor(qkm[:, 1], qh, ex[:, 1], ALU.mult)
                    dve.tensor_tensor(qkm[:, 2], kh, ex[:, 2], ALU.mult).then_inc(qk_ready, 1)
                    dve.wait_ge(s_psum, n + 1)
                    seq = order[d]
                    then(dve.tensor_copy(state[:, d, seq[0], :], product(d, None)))
                    for m, c in enumerate(seq[:-1]):
                        last = c % 2 * CHUNK + (CHUNK - 1 if d == 0 else 0)
                        ins = dve.scalar_tensor_tensor(state[:, d, seq[m + 1], :], state[:, d, c, :], ex[:, 0, c // 2, last:last + 1],
                                                       product(d, c), ALU.mult, ALU.add)
                        if m < NCH - 2:
                            then(ins)
                    ins.then_inc(s_ready, 1)
                    dve.wait_ge(a_psum, n + 1)
                    for c in range(2):
                        r = slice(c * CHUNK, (c + 1) * CHUNK)
                        ins = dve.copy_predicated(aT[r, d, :, r], bc(low[r, d, :], 1, (CHUNK, XT, CHUNK)).bitcast(U32),
                                                  ps[r, 1, 0:XT * P].rearrange("p (t n) -> p t n", n=P)[:, :, 0:CHUNK])
                    ins.then_inc(a_ready, 1)


def final_stage(T):
    nc, t, f = T.nc, T.t, T.f
    X, g_row, y = f(XR, NT, D), f(HI, D), f(HI + D, XT, D)
    ss, rstd = f(HI + 3 * D, XT), f(HI + 3 * D + XT, XT)
    with ExitStack() as ctx:
        g_landed, ss_ready, var_ready, std_ready, y_ready, stored, step = T.sems(
            ctx, *[f"f_{n}" for n in ("g_landed", "ss_ready", "var_ready", "std_ready", "y_ready", "stored", "step")])
        with nc.Block() as block:
            @block.sync
            def _(sp):
                sp.dma_start(g_row, t["final_g"].partition_broadcast(P)).then_inc(g_landed, 16)
                for n in range(XT):
                    sp.wait_ge(y_ready, n + 1)
                    sp.dma_start(T.out[0, n * P:(n + 1) * P, :], y[:, n, :]).then_inc(stored, 16)
                sp.wait_ge(g_landed, 16)
                sp.wait_ge(stored, 16 * XT)

            @block.scalar
            def _(act):
                for n in range(XT):
                    act.activation(y[:, n, :], X[:, n, :], ACT.Square, accum_out=ss[:, n:n + 1]).then_inc(ss_ready, 1)
                act.wait_ge(var_ready, 1)
                act.activation(rstd, ss, ACT.Sqrt).then_inc(std_ready, 1)

            @block.vector
            def _(dve):
                then = Steps(dve, step)
                dve.wait_ge(ss_ready, XT)
                dve.tensor_scalar(ss, ss, 1.0 / D, EPS, ALU.mult, ALU.add).then_inc(var_ready, 1)
                dve.wait_ge(std_ready, 1)
                then(dve.reciprocal(rstd, rstd))
                dve.wait_ge(g_landed, 16)
                for n in range(XT):
                    dve.scalar_tensor_tensor(y[:, n, :], X[:, n, :], rstd[:, n:n + 1], g_row, ALU.mult, ALU.mult).then_inc(y_ready, 1)


def hybrid_trunk(nc, t, out, stages=99, dump=None):
    with ExitStack() as ctx:
        T = Trunk(nc, ctx, t, out)
        f = T.f
        every, of_x = list(range(NT)), list(range(XT))
        none = lambda *a: None
        steps = [
            lambda: setup_stage(T),
            lambda: mod_stage(T, 0),
            lambda: norm_stage(T, 0, 0, every, none, False),
            lambda: attn_project_stage(T),
            lambda: attention_stage(T),
            lambda: out_stage(T, 0, NT, f(ORow, NT, D), f(LO, KD, NT * P),
                              (f(HI + 8 * D, A_DV), f(HI + 9 * D, D), f(HI + 10 * D, 16), f(HI + 10 * D + 16, 16), None),
                              lambda sp, first, used: None),
            lambda: norm_stage(T, 0, 1, every, none, True),
            lambda: route_stage(T, 0, NT),
            lambda: moe_stage(T, 0, NT),
            lambda: overflow_stage(T, 0, NT),
            lambda: combine_stage(T, 0, NT, lambda sp: T.load_chunks(sp, 23, 20, None)),
            lambda: mod_stage(T, 1),
            lambda: norm_stage(T, 1, 0, every, none, False),
            lambda: gla_project_stage(T),
            lambda: decay_stage(T, none),
            lambda: gla_stage(T, none),
            lambda: out_stage(T, 1, XT, f(GO, XT, D), f(HI, KD, XT * P),
                              (f(HI + 8 * D, C_DV), f(HI + 9 * D, D), f(HI + 10 * D, 8), f(HI + 10 * D + 8, 8), f(GT, XT, D)),
                              lambda sp, first, used: None),
            lambda: norm_stage(T, 1, 1, of_x, none, True),
            lambda: route_stage(T, 1, XT),
            lambda: moe_stage(T, 1, XT),
            lambda: overflow_stage(T, 1, XT),
            lambda: combine_stage(T, 1, XT, none),
            lambda: final_stage(T),
        ]
        for n, stage in enumerate(steps[:stages]):
            stage()
            if dump is not None:
                dump(n, T)


def shape_constants():
    c = {"k_ident": np.eye(P, dtype=np.float32), "k_ones": np.ones((P, P), np.float32)}
    p = np.arange(P)
    c["k_iota16"] = np.arange(NE, dtype=np.float32)[None]
    c["k_token"] = (p[:, None] + P * np.arange(NT)[None]).astype(np.float32)
    c["k_iota512"] = np.arange(NT * P, dtype=np.float32)[None]
    c["k_before"] = (p[:, None] < p[None]).astype(np.float32)
    j, pos = p % 32 % 16, np.arange(SEQ)
    inv = np.power(np.float32(10000.0), -(2 * j).astype(np.float32) / np.float32(32))
    at = np.where((p % 64 < 32)[:, None], (pos // GRID_W)[None], (pos % GRID_W)[None]).astype(np.float32)
    ang = (at * inv[:, None].astype(np.float32)).astype(np.float32)
    c["k_cos"], c["k_sin"] = np.cos(ang).astype(np.float32), np.sin(ang).astype(np.float32)
    rot = np.zeros((P, P), np.float32)
    for m in range(P):
        if m % 32 < 16:
            rot[m + 16, m] = -1.0
        else:
            rot[m - 16, m] = 1.0
    c["k_rope"] = rot
    col = np.arange(GRID_W)
    start = np.clip(col - NA_COLS // 2, 0, GRID_W - NA_COLS)
    seen = (col[None] >= start[:, None]) & (col[None] < start[:, None] + NA_COLS)
    c["k_namask"] = np.tile(np.where(seen, 0.0, MASKED), (SEQ // GRID_W, SEQ // GRID_W)).astype(np.float32)
    for i, nt in ((0, NT), (1, XT)):
        e, b = np.meshgrid(np.arange(NE), np.arange(1, nt), indexing="ij")
        c[f"k_over{i}"] = np.stack([b * P, e]).astype(np.float32)
    s, tt = p[:, None], p[None]
    same = s // CHUNK == tt // CHUNK
    w = np.float32(1.0 / TAU)
    sums, ends, ends_ctx, low = [], [], [], []
    for d in range(2):
        run = same & (s <= tt if d == 0 else s >= tt)
        mid = tt // CHUNK * CHUNK + (CHUNK // 2 - 1 if d == 0 else CHUNK // 2)
        to_mid = same & (s <= mid if d == 0 else s >= mid)
        sums += [run * w, (run.astype(np.float32) - to_mid.astype(np.float32)) * w]
        ends.append((same & (s > tt if d == 0 else s < tt)) * w)
        ends_ctx.append((s > tt if d == 0 else s < tt) * w)
        a, b = p[:, None] % CHUNK, np.arange(CHUNK)[None]
        low.append(a <= b if d == 0 else a >= b)
    cat = lambda xs: np.ascontiguousarray(np.concatenate(xs, 1).astype(np.float32))
    c["k_sums"], c["k_ends"], c["k_ends_ctx"], c["k_low"] = cat(sums), cat(ends), cat(ends_ctx), cat(low)
    c["k_all"] = np.full((P, P), w, np.float32)
    return c


def window_layout(na_bias):
    rows, pos = SEQ // GRID_W, np.arange(SEQ)
    dr = pos[None] // GRID_W - pos[:, None] // GRID_W + NA_ROWS - 1
    dc = pos[None] % GRID_W - pos[:, None] % GRID_W + NA_COLS - 1
    dc = np.clip(dc, 0, 2 * NA_COLS - 2)
    return np.ascontiguousarray(np.asarray(na_bias)[0][:, dr, dc])


_INS = ["x", "ctx", "w_mod", "b_mod", "norm_g", "final_g", "att_w_in", "att_w_out", "att_lambda", "att_subln_g",
        "gla_w_in", "gla_w_gate", "gla_b_gate", "gla_norm_g", "gla_w_out", "router_w", "router_bias",
        "moe_w1", "moe_w3", "moe_w2"]


def launch_arrays(inputs):
    a = {n: np.ascontiguousarray(inputs[n]) for n in _INS}
    a["final_g"] = a["final_g"].reshape(1, D)
    a["router_bias"] = a["router_bias"].reshape(1, NE)
    a["c_cols"] = np.ascontiguousarray(np.asarray(inputs["c"]).reshape(KD, P).T)
    a["c_ctx_cols"] = np.ascontiguousarray(np.asarray(inputs["c_ctx"]).reshape(KD, P).T)
    a["na_window"] = window_layout(inputs["na_bias"])
    a.update(shape_constants())
    return a


def kernel(**inputs):
    import concourse.bacc as _bacc
    from concourse.bass_utils import run_bass_kernel_spmd as _run

    nc = _bacc.Bacc("TRN2", target_bir_lowering=False, num_devices=1)
    arrays = launch_arrays(inputs)
    t = {n: nc.dram_tensor(n, a.shape, F32, kind="ExternalInput").ap() for n, a in arrays.items()}
    out = nc.dram_tensor("out_x", (1, SEQ, D), F32, kind="ExternalOutput").ap()
    hybrid_trunk(nc, t, out)
    r = _run(nc, [arrays], core_ids=[0])
    return r.results[0]["out_x"]
```

```python
import math
from contextlib import ExitStack

import numpy as np

import concourse.bass as bass
from concourse import mybir

F32 = mybir.dt.float32
I32 = mybir.dt.int32
U32 = mybir.dt.uint32
ALU = mybir.AluOpType
ACT = mybir.ActivationFunctionType
AX = mybir.AxisListType

P = 128
D = 1024
KD = D // P
SEQ = 256
CTX = 256
XT = SEQ // P
NT = (SEQ + CTX) // P
EPS = 1e-6
GRID_W = 64
NA_ROWS, NA_COLS = 8, 16
A_HEADS, B_HEADS, DH, A_DV = 4, 8, 64, 128
LAM_INIT = 0.8 - 0.6 * math.exp(-0.3 * 0)
C_HEADS, C_DK, C_DV, RANK, TAU, CHUNK = 4, 128, 256, 16, 16.0, 64
NE, NG, EPG, DE = 16, 4, 4, 512
HALF = 512
BIG = 3.0e38
MASKED = -1.0e30

CH = KD * HALF
RING = 0
LO = 3 * CH
XR = 6 * CH
MOD = XR + NT * D
KEEP = MOD + 12 * D
K_ID, K_ONE, K_SILU, K_LAM, K_GATE, K_SLOT, K_ROWS = 0, 128, 256, 272, 280, 288, 296
K_OVIDX, K_OVEXP, K_NOV, K_CUR, K_IOTA, K_TOK, K_RBIAS = 360, 368, 376, 385, 386, 402, 406
HI = KEEP + 512
END = 53200
SH1, SC1, G1, SH2, SC2, G2 = range(6)
SLOT3 = HI + 4 * D
BIAS = END - 4 * HALF


class Steps:

    def __init__(self, engine, sem):
        self.engine, self.sem, self.n = engine, sem, 0

    def __call__(self, ins):
        self.n += 1
        ins.then_inc(self.sem, 1)
        self.engine.wait_ge(self.sem, self.n)

    def mark(self, ins):
        self.n += 1
        ins.then_inc(self.sem, 1)
        return self.n

    def until(self, n):
        self.engine.wait_ge(self.sem, n)


def bc(ap, axis, shape):
    return ap.unsqueeze(axis).to_broadcast(shape)


class Trunk:

    def __init__(self, nc, ctx, t, out):
        self.nc, self.t, self.out = nc, t, out
        self.A = ctx.enter_context(nc.sbuf_tensor("arena", [P, END], F32))
        self.ps = ctx.enter_context(nc.psum_tensor("ps", [P, 8, HALF], F32))
        self.h2_dram = nc.dram_tensor("h2_rows", (NT * P, D), F32).ap()
        self.y_dram = nc.dram_tensor("expert_rows", ((NE + 2 * NT - 1) * P, D), F32).ap()
        self.mod_landed = ctx.enter_context(nc.semaphore("mod_landed"))
        self.mod_dram = nc.dram_tensor("mod_rows", (1, 16 * HALF), F32).ap()
        self.landed = [ctx.enter_context(nc.semaphore(f"chunk_landed{s}")) for s in range(4)]
        self.w_landed = {k: [ctx.enter_context(nc.semaphore(f"{k}_landed{s}")) for s in range(2)]
                         for k in ("w1", "w3", "w2")}
        self.w_base = {0: 0, 1: 8 * 16}
        self.chunks, self.ids, landed = [], {}, [0] * 4
        for name, slot in CHUNKS:
            kind, i, j = name
            w = {"mod": t["w_mod"][i], "in": t[("att_w_in", "gla_w_in")[i]][0],
                 "out": t[("att_w_out", "gla_w_out")[i]][0]}[kind]
            landed[slot] += 32 if kind == "mod" else 16
            self.ids[name] = len(self.chunks)
            self.chunks.append((name, w[:, j * HALF:(j + 1) * HALF], slot, landed[slot]))
        self.loaded = 0
        self.cleared = []

    def f(self, at, *shape):
        n = int(np.prod(shape))
        v = self.A[:, at:at + n]
        if len(shape) == 1:
            return v
        names = "abcd"[:len(shape)]
        return v.rearrange(f"p ({' '.join(names)}) -> p {' '.join(names)}",
                           **{a: s for a, s in zip(names, shape)})

    def slot(self, s):
        return self.f(RING + s * CH, KD, HALF)

    def sems(self, ctx, *names):
        sems = [self.nc.alloc_semaphore(n) for n in names]

        def retire():
            for s in sems:
                self.nc.gpsimd.sem_clear(s)
            for s in self.cleared:
                self.nc.release_semaphore(s)
            self.cleared = sems
        ctx.callback(retire)
        return sems

    def chunk(self, name):
        slot = self.chunks[self.ids[name]][2]
        return self.slot(slot) if slot < 3 else self.f(SLOT3, KD, HALF)

    def bias(self, name):
        return self.f(BIAS + self.chunks[self.ids[name]][2] * HALF, HALF)

    def wait_chunk(self, engine, name):
        _, _, slot, landed = self.chunks[self.ids[name]]
        engine.wait_ge(self.landed[slot], landed)

    def load_chunks(self, sp, end, released):
        while self.loaded <= self.ids[end]:
            name, w, slot, _ = self.chunks[self.loaded]
            before = [n for n, _, s, _ in self.chunks[:self.loaded] if s == slot][-1:]
            if before and before[0] in released:
                sp.wait_ge(*released[before[0]])
            sp.dma_start(self.chunk(name), w.rearrange("(k p) n -> p k n", p=P)).then_inc(self.landed[slot], 16)
            if name[0] == "mod":
                _, i, j = name
                sp.dma_start(self.bias(name)[0:1], self.t["b_mod"][i:i + 1, j * HALF:(j + 1) * HALF])\
                  .then_inc(self.landed[slot], 16)
            self.loaded += 1


CHUNKS = [(("mod", 0, j), j) for j in range(4)]
CHUNKS += [(("in", 0, 0), 0), (("in", 0, 1), 1)]
SUMS = [("mod", 0, j) for j in range(4, 12)] + [("mod", 1, j) for j in range(12)]
PROJECT_SUMS, ATTENTION_SUMS = SUMS[:11], SUMS[11:]
CHUNKS += [(SUMS[m], 2 + m % 2) for m in range(4)] + [(("in", 0, 2), 0)]
CHUNKS += [(SUMS[m], 2 + m % 2) for m in range(4, 6)] + [(("in", 0, 3), 1)]
CHUNKS += [(SUMS[m], 2 + m % 2) for m in range(6, 8)] + [(("in", 0, 4), 0)]
CHUNKS += [(SUMS[m], 2 + m % 2) for m in range(8, 10)] + [(("in", 0, 5), 1)]
CHUNKS += [(SUMS[10], 2)]
CHUNKS += [(SUMS[m], (m - 11) % 3) for m in range(11, 20)]
CHUNKS += [(("out", 0, 0), 0), (("out", 0, 1), 1)]
CHUNKS += [(("in", 1, j), j % 3) for j in range(6)] + [(("out", 1, j), j) for j in range(2)]


def sum_items(chunks):
    return [(m, name, v) for m, name in enumerate(chunks) for v in range(2)
            if v == 0 or name[1] == 0 or name[2] < 4]


def mod_row_at(name, v):
    return (name[2] + 12 * v) * HALF


def setup_stage(T):
    nc, t, f = T.nc, T.t, T.f
    with ExitStack() as ctx:
        in_landed, silu_done, zeroed = T.sems(ctx, "setup_landed", "setup_silu", "bias_zeroed")
        with nc.Block() as block:
            @block.sync
            def _(sp):
                sp.dma_start(f(KEEP + K_ID, P), t["k_ident"]).then_inc(in_landed, 16)
                sp.dma_start(f(KEEP + K_ONE, P), t["k_ones"]).then_inc(in_landed, 16)
                sp.dma_start(f(KEEP + K_IOTA, NE), t["k_iota16"].partition_broadcast(P)).then_inc(in_landed, 16)
                sp.dma_start(f(KEEP + K_TOK, NT), t["k_token"]).then_inc(in_landed, 16)
                sp.dma_start(f(KEEP + K_RBIAS, NE), t["router_bias"].partition_broadcast(P)).then_inc(in_landed, 16)
                sp.dma_start(f(KEEP + K_SILU, 2, KD)[:, 0, :], t["c_cols"]).then_inc(in_landed, 16)
                sp.dma_start(f(KEEP + K_SILU, 2, KD)[:, 1, :], t["c_ctx_cols"]).then_inc(in_landed, 16)
                sp.wait_ge(zeroed, 1)
                T.load_chunks(sp, ("mod", 0, 3), {})
                sp.dma_start(f(XR, NT, D)[:, 0:XT, :], t["x"][0].rearrange("(t p) d -> p t d", p=P)).then_inc(in_landed, 16)
                sp.dma_start(f(XR, NT, D)[:, XT:NT, :], t["ctx"][0].rearrange("(t p) d -> p t d", p=P)).then_inc(in_landed, 16)
                sp.wait_ge(in_landed, 9 * 16)

            @block.gpsimd
            def _(pool):
                pool.memset(f(BIAS, 4 * HALF), 0.0).then_inc(zeroed, 1)

            @block.scalar
            def _(act):
                act.wait_ge(in_landed, 9 * 16)
                act.activation(f(KEEP + K_SILU, 2 * KD), f(KEEP + K_SILU, 2 * KD), ACT.Silu).then_inc(silu_done, 1)


def mod_stage(T):
    nc, t, f, ps = T.nc, T.t, T.f, T.ps
    spread, acc = f(LO, KD, P), f(LO + KD * P, 2, HALF)
    silu = f(KEEP + K_SILU, 2, KD)
    mod = f(MOD, 2, 12, HALF)
    ones = f(KEEP + K_ONE, P)
    with ExitStack() as ctx:
        spread_ready, acc_ready, mod_psum, mod_done, step = T.sems(
            ctx, "spread_ready", "acc_ready", "mod_psum", "mod_done", "mod_step")
        with nc.Block() as block:
            @block.sync
            def _(sp):
                T.load_chunks(sp, ("mod", 0, 5), {("mod", 0, j): (mod_psum, j + 1) for j in range(4)})

            @block.vector
            def _(dve):
                then = Steps(dve, step)
                for k in range(KD):
                    last = dve.tensor_scalar(spread[:, k, :], ones, silu[:, 1, k:k + 1], None, ALU.mult)
                last.then_inc(spread_ready, 1)
                for j in range(4):
                    name = ("mod", 0, j)
                    w = T.chunk(name)
                    T.wait_chunk(dve, name)
                    if j >= 2:
                        dve.wait_ge(mod_psum, j - 1)
                    for k in range(KD):
                        ins = dve.scalar_tensor_tensor(acc[:, j % 2, :], w[:, k, :], silu[:, 0, k:k + 1],
                                                       T.bias(name) if k == 0 else acc[:, j % 2, :], ALU.mult, ALU.add)
                        if k < KD - 1:
                            then(ins)
                    ins.then_inc(acc_ready, 1)

            @block.tensor
            def _(pe):
                pe.wait_ge(spread_ready, 1)
                for j in range(4):
                    name = ("mod", 0, j)
                    w = T.chunk(name)
                    T.wait_chunk(pe, name)
                    if j >= 2:
                        pe.wait_ge(mod_done, j - 1)
                    bank = 2 * (j % 2)
                    for k in range(KD):
                        pe.matmul(ps[:, bank + 1, :], spread[:, k, :], w[:, k, :], start=(k == 0), stop=False)
                    pe.matmul(ps[:, bank + 1, :], ones, T.bias(name), start=False, stop=True)
                    pe.wait_ge(acc_ready, j + 1)
                    pe.matmul(ps[:, bank, :], ones, acc[:, j % 2, :], start=True, stop=True).then_inc(mod_psum, 1)

            @block.scalar
            def _(act):
                for j in range(4):
                    bank = 2 * (j % 2)
                    act.wait_ge(mod_psum, j + 1)
                    act.activation(mod[:, 0, j, :], ps[:, bank, :], ACT.Copy)
                    act.activation(mod[:, 1, j, :], ps[:, bank + 1, :], ACT.Copy).then_inc(mod_done, 1)


def norm_stage(T, i, which, tiles, load_to, store_rows):
    nc, t, f, ps = T.nc, T.t, T.f, T.ps
    tag = f"n{i}{which}"
    X, mod, hT = f(XR, NT, D), f(MOD, 2, 6, D), f(HI, KD, NT * P)
    g_row, junk, h_row = f(LO, D), f(LO + D, NT, D), f(LO + 5 * D, 2, D)
    ss, rstd = f(LO + 7 * D, NT), f(LO + 7 * D + NT, NT)
    shift, scale = (SH1, SC1) if which == 0 else (SH2, SC2)
    ident = f(KEEP + K_ID, P)
    kinds = sorted({0 if n < XT else 1 for n in tiles})
    with ExitStack() as ctx:
        g_landed, ss_ready, var_ready, std_ready, h_ready, h_psum, h_evac, row_stored0, row_stored1, step = T.sems(
            ctx, *[f"{tag}_{n}" for n in ("g_landed", "ss_ready", "var_ready", "std_ready", "h_ready",
                                          "h_psum", "h_evac", "row_stored0", "row_stored1", "step")])
        row_stored = (row_stored0, row_stored1)
        with nc.Block() as block:
            @block.sync
            def _(sp):
                sp.dma_start(g_row, t["norm_g"][i, which:which + 1, :].partition_broadcast(P)).then_inc(g_landed, 16)
                load_to(sp)
                if store_rows:
                    for n, tile in enumerate(tiles):
                        sp.wait_ge(h_ready, n + 1)
                        sp.dma_start(T.h2_dram[tile * P:(tile + 1) * P, :], h_row[:, n % 2, :]).then_inc(row_stored[n % 2], 16)
                    for s in row_stored:
                        sp.wait_ge(s, 16 * len(tiles) // 2)
                sp.wait_ge(g_landed, 16)

            @block.scalar
            def _(act):
                for n, tile in enumerate(tiles):
                    act.activation(junk[:, n, :], X[:, tile, :], ACT.Square, accum_out=ss[:, n:n + 1]).then_inc(ss_ready, 1)
                act.wait_ge(var_ready, 1)
                act.activation(rstd[:, 0:len(tiles)], ss[:, 0:len(tiles)], ACT.Sqrt).then_inc(std_ready, 1)
                for n, tile in enumerate(tiles):
                    act.wait_ge(h_psum, n + 1)
                    for b in range(2):
                        ins = act.activation(hT[:, 4 * b:4 * b + 4, tile * P:(tile + 1) * P],
                                             ps[:, 2 * (n % 2) + b, :].rearrange("p (k n) -> p k n", n=P), ACT.Copy)
                    ins.then_inc(h_evac, 1)

            @block.vector
            def _(dve):
                then = Steps(dve, step)
                dve.wait_ge(g_landed, 16)
                if i == 1 and which == 0:
                    dve.wait_ge(T.mod_landed, 48)
                for v in kinds:
                    ins = dve.scalar_tensor_tensor(mod[:, v, scale, :], mod[:, v, scale, :], 1.0, g_row, ALU.add, ALU.mult)
                then(ins)
                dve.wait_ge(ss_ready, len(tiles))
                dve.tensor_scalar(ss[:, 0:len(tiles)], ss[:, 0:len(tiles)], 1.0 / D, EPS, ALU.mult, ALU.add).then_inc(var_ready, 1)
                dve.wait_ge(std_ready, 1)
                then(dve.reciprocal(rstd[:, 0:len(tiles)], rstd[:, 0:len(tiles)]))
                for n, tile in enumerate(tiles):
                    v = 0 if tile < XT else 1
                    if n >= 2:
                        dve.wait_ge(h_psum, n - 1)
                        if store_rows:
                            dve.wait_ge(row_stored[n % 2], 16 * (n // 2))
                    then(dve.scalar_tensor_tensor(h_row[:, n % 2, :], X[:, tile, :], rstd[:, n:n + 1],
                                                  mod[:, v, scale, :], ALU.mult, ALU.mult))
                    dve.tensor_tensor(h_row[:, n % 2, :], h_row[:, n % 2, :], mod[:, v, shift, :], ALU.add).then_inc(h_ready, 1)

            @block.tensor
            def _(pe):
                for n, tile in enumerate(tiles):
                    pe.wait_ge(h_ready, n + 1)
                    if n >= 2:
                        pe.wait_ge(h_evac, n - 1)
                    for k in range(KD):
                        ins = pe.transpose(ps[:, 2 * (n % 2) + k // 4, (k % 4) * P:(k % 4 + 1) * P],
                                           h_row[:, n % 2, k * P:(k + 1) * P], ident)
                    ins.then_inc(h_psum, 1)


QKT, V0 = LO, LO + 16 * HALF


def attn_project_stage(T):
    nc, t, f, ps = T.nc, T.t, T.f, T.ps
    hT, qkT, v = f(HI, KD, NT * P), f(QKT, 16, HALF), f(V0, NT, D)
    free = MOD + 6 * D
    rope_r, cos, sin = f(free, P), f(free + P, SEQ), f(free + P + SEQ, SEQ)
    free += P + 2 * SEQ
    tmp = f(free, 2, SEQ)
    lp, lq, ls = f(free + 512, 4, DH), f(free + 768, 2, DH), f(free + 896, 2)
    acc, row = f(MOD, 4, HALF), f(HI + 8 * D, 2, HALF)
    mod, ones, silu = f(MOD, 2, 12, HALF), f(KEEP + K_ONE, P), f(KEEP + K_SILU, 2, KD)
    items = sum_items(PROJECT_SUMS)
    in_dram = [i for i, (_, name, _) in enumerate(items) if name[1] == 1]
    after = {min(2 * m + 3, 23): [i for i, item in enumerate(items) if min(2 * item[0] + 3, 23) == min(2 * m + 3, 23)]
             for m in range(len(PROJECT_SUMS))}
    lam = f(KEEP + K_LAM, 4)
    kinds = ["q", "q", "v", "q", "q", "v"]
    dest = [0, 4, 0, 8, 12, 1]
    groups = [(c, g) for c in range(6) for g in range(4)]
    with ExitStack() as ctx:
        tab_landed, proj_done, proj_evac, rot_done, rope_done, lam_step, step, acc_ready, sum_psum, sum_kept, row_stored0, row_stored1 = T.sems(
            ctx, "tab_landed", "proj_done", "proj_evac", "rot_done", "rope_done", "lam_exp", "proj_step",
            "p_acc_ready", "p_sum_psum", "p_sum_kept", "p_row_stored0", "p_row_stored1")
        row_stored = (row_stored0, row_stored1)
        used = {("in", 0, j): (proj_done, 4 * (j + 1)) for j in range(6)}
        for i, (_, name, _) in enumerate(items):
            used[name] = (acc_ready, i + 1)
        with nc.Block() as block:
            @block.sync
            def _(sp):
                sp.dma_start(rope_r, t["k_rope"]).then_inc(tab_landed, 16)
                sp.dma_start(cos, t["k_cos"]).then_inc(tab_landed, 16)
                sp.dma_start(sin, t["k_sin"]).then_inc(tab_landed, 16)
                sp.dma_start(lp, t["att_lambda"].partition_broadcast(P)).then_inc(tab_landed, 16)
                T.load_chunks(sp, ATTENTION_SUMS[2], used)
                sp.wait_ge(tab_landed, 64)

            @block.tensor
            def _(pe):
                def rotate(n):
                    pe.wait_ge(proj_evac, n + 1)
                    if n >= 2:
                        pe.wait_ge(rope_done, n - 1)
                    pe.matmul(ps[:, 4 + n % 2, 0:SEQ], rope_r, qkT[:, n, 0:SEQ], start=True, stop=True).then_inc(rot_done, 1)

                pe.wait_ge(tab_landed, 64)
                for n, (c, g) in enumerate(groups):
                    w = T.chunk(("in", 0, c))
                    if g == 0:
                        T.wait_chunk(pe, ("in", 0, c))
                    if n >= 4:
                        pe.wait_ge(proj_evac, n - 3)
                    for k in range(KD):
                        if kinds[c] == "q":
                            a, b = w[:, k, g * P:(g + 1) * P], hT[:, k, :]
                        else:
                            a, b = hT[:, k, g * P:(g + 1) * P], w[:, k, :]
                        ins = pe.matmul(ps[:, n % 4, :], a, b, start=(k == 0), stop=(k == KD - 1))
                    ins.then_inc(proj_done, 1)
                    if 1 <= n <= 8:
                        rotate(n - 1)
                    for i in after.get(n, ()):
                        pe.wait_ge(acc_ready, i + 1)
                        if i >= 2:
                            pe.wait_ge(sum_kept, i - 1)
                        pe.matmul(ps[:, 6 + i % 2, :], ones, acc[:, i % 4, :], start=True, stop=True).then_inc(sum_psum, 1)

            @block.scalar
            def _(act):
                for n, (c, g) in enumerate(groups):
                    act.wait_ge(proj_done, n + 1)
                    to = qkT[:, dest[c] + g, :] if kinds[c] == "q" else v[:, g, dest[c] * HALF:(dest[c] + 1) * HALF]
                    act.activation(to, ps[:, n % 4, :], ACT.Copy).then_inc(proj_evac, 1)
                    for i in after.get(n, ()):
                        _, name, v_ = items[i]
                        act.wait_ge(sum_psum, i + 1)
                        if name[1] == 0:
                            act.activation(mod[:, v_, name[2], :], ps[:, 6 + i % 2, :], ACT.Copy).then_inc(sum_kept, 1)
                        else:
                            r = in_dram.index(i)
                            if r >= 2:
                                act.wait_ge(row_stored[r % 2], 16 * (r // 2))
                            at = mod_row_at(name, v_)
                            act.activation(row[0:1, r % 2, :], ps[0:1, 6 + i % 2, :], ACT.Copy).then_inc(sum_kept, 1)
                            act.wait_ge(sum_kept, i + 1)
                            act.dma_start(T.mod_dram[:, at:at + HALF], row[0:1, r % 2, :]).then_inc(row_stored[r % 2], 16)
                for r in range(2):
                    act.wait_ge(row_stored[r], 16 * (len(in_dram) // 2))
                act.wait_ge(lam_step, 1)
                act.activation(lam[:, 0:2], ls, ACT.Exp).then_inc(lam_step, 1)

            @block.vector
            def _(dve):
                then = Steps(dve, step)

                def modulation(m):
                    mine = [(i, v_) for i, (m_, _, v_) in enumerate(items) if m_ == m]
                    name = PROJECT_SUMS[m]
                    T.wait_chunk(dve, name)
                    if mine[-1][0] >= 4:
                        dve.wait_ge(sum_psum, mine[-1][0] - 3)
                    landed = {}
                    for k in range(KD):
                        for i, v_ in mine:
                            to = acc[:, i % 4, :]
                            if k > 0:
                                then.until(landed[i])
                            ins = dve.scalar_tensor_tensor(to, T.chunk(name)[:, k, :], silu[:, v_, k:k + 1],
                                                           T.bias(name) if k == 0 else to, ALU.mult, ALU.add)
                            if k < KD - 1:
                                landed[i] = then.mark(ins)
                            else:
                                ins.then_inc(acc_ready, 1)

                dve.wait_ge(tab_landed, 64)
                for n in range(8):
                    if n % 2 == 1:
                        modulation(n // 2)
                    q = qkT[:, n, 0:SEQ]
                    dve.wait_ge(rot_done, n + 1)
                    dve.tensor_tensor(tmp[:, 0, :], ps[:, 4 + n % 2, 0:SEQ], sin, ALU.mult)
                    then(dve.tensor_tensor(tmp[:, 1, :], q, cos, ALU.mult))
                    dve.tensor_tensor(q, tmp[:, 1, :], tmp[:, 0, :], ALU.add).then_inc(rope_done, 1)
                    dve.wait_ge(rope_done, n + 1)
                for m in range(4, len(PROJECT_SUMS)):
                    modulation(m)
                lps = lp.rearrange("p (a b) n -> p a b n", b=2)
                then(dve.tensor_tensor(lq, lps[:, :, 0, :], lps[:, :, 1, :], ALU.mult))
                dve.tensor_reduce(ls, lq, AX.X, ALU.add).then_inc(lam_step, 1)
                dve.wait_ge(lam_step, 2)
                then(dve.tensor_tensor(lam[:, 2:3], lam[:, 1:2], lam[:, 0:1], ALU.subtract))
                then(dve.tensor_scalar(lam[:, 3:4], lam[:, 2:3], LAM_INIT, None, ALU.subtract))


ORow = HI


def attention_stage(T):
    nc, t, f, ps = T.nc, T.t, T.f, T.ps
    qkT, v, O = f(QKT, 16, HALF), f(V0, NT, D), f(ORow, NT, D)
    Pb = f(HI + 4 * D, 2, 2, HALF)
    aT = f(HI + 6 * D, 2, 2, HALF)
    bm = f(MOD + 6 * D, 2, 2, XT, SEQ)
    mask = f(HI + 8 * D, XT, SEQ)
    st = HI + 8 * D + 2 * SEQ
    acc, row = f(MOD, 2, HALF), f(MOD + 2 * HALF, 2, HALF)
    ones, silu = f(KEEP + K_ONE, P), f(KEEP + K_SILU, 2, KD)
    items = sum_items(ATTENTION_SUMS)
    slices = [(i, k) for i in range(len(items)) for k in range(KD)]
    PER_JOB = 3
    total_at = {}
    for i in range(len(items)):
        total_at.setdefault(min(KD * (i + 1) // PER_JOB + 1, 31), []).append(i)
    NJ = 32
    mx, nm, sm, rs, cs = (f(st + k * 64, 64) for k in range(5))
    zero = f(st + 5 * 64, HALF)
    assert st + 5 * 64 + HALF <= BIAS
    neg_lam = f(KEEP + K_LAM, 4)[:, 3:4]
    ident = f(KEEP + K_ID, P)
    jobs = [("A", b, n) for b in range(4) for n in range(NT)] + [("B", b, n) for b in range(4) for n in range(NT)]

    def keys(n):
        return list(range(NT)) if n < XT else list(range(XT, NT))

    def turned(j):
        return j if j <= 16 else 16 + 2 * (j - 16)

    with ExitStack() as ctx:
        zero_ready, zeros_stored, bias_landed0, bias_landed1, mask_landed, bias_half, bias_ready, scored, shifted, exp_done, a_ready, a_turned, at_ready, av_done, o_done, step, acc_ready, sum_psum, sum_kept, row_stored0, row_stored1 = T.sems(
            ctx, "zero_ready", "zeros_stored", "bias_landed0", "bias_landed1", "mask_landed", "bias_half", "bias_ready", "scored", "shifted", "exp_done", "a_ready",
            "a_turned", "at_ready", "av_done", "o_done", "att_step",
            "a_acc_ready", "a_sum_psum", "a_sum_kept", "a_row_stored0", "a_row_stored1")
        row_stored = (row_stored0, row_stored1)
        used = {}
        for i, (_, name, _) in enumerate(items):
            used[name] = (acc_ready, i + 1)
        bias_landed = (bias_landed0, bias_landed1)
        with nc.Block() as block:
            @block.sync
            def _(sp):
                sp.dma_start(mask, t["k_namask"].rearrange("(t p) n -> p t n", p=P)).then_inc(mask_landed, 16)
                for hp in range(4):
                    if hp == 2:
                        T.load_chunks(sp, ATTENTION_SUMS[6], used)
                    if hp >= 2:
                        sp.wait_ge(scored, 16 + 4 * (hp - 2) + 2)
                    for u in range(2):
                        sp.dma_start(bm[:, hp % 2, u], t["na_window"][2 * hp + u].rearrange("(t p) n -> p t n", p=P))\
                          .then_inc(bias_landed[hp % 2], 16)
                T.load_chunks(sp, ("out", 0, 1), used)
                for s in bias_landed:
                    sp.wait_ge(s, 4 * 16)
                sp.wait_ge(zero_ready, 1)
                for m in range(2 * NT - 1):
                    at = (NE + m) * P
                    sp.dma_start(T.y_dram[at:at + P, :].rearrange("p (b n) -> p b n", n=HALF), bc(zero, 1, (P, 2, HALF)))\
                      .then_inc(zeros_stored, 16)
                sp.wait_ge(zeros_stored, 16 * (2 * NT - 1))

            @block.gpsimd
            def _(pool):
                pool.memset(zero, 0.0).then_inc(zero_ready, 1)
                pool.wait_ge(mask_landed, 16)
                for hp in range(4):
                    pool.wait_ge(bias_landed[hp % 2], 32 * (hp // 2 + 1))
                    b = bm[:, hp % 2]
                    pool.tensor_scalar(b, b, float(DH) ** 0.5, None, ALU.mult).then_inc(bias_half, 1)
                    pool.wait_ge(bias_half, hp + 1)
                    pool.tensor_tensor(b, b, bc(mask, 1, (P, 2, XT, SEQ)), ALU.add).then_inc(bias_ready, 1)

            @block.tensor
            def _(pe):
                def scores(j):
                    kind, b, n = jobs[j]
                    ks = keys(n)
                    qb, kb = (b, 4 + b) if kind == "A" else (8 + b, 12 + b)
                    if j >= 2:
                        pe.wait_ge(exp_done, 2 * (j - 1))
                    if kind == "B" and n < XT:
                        pe.wait_ge(bias_ready, b + 1)
                    for u in range(2):
                        rows = slice(DH * u, DH * u + DH)
                        to = ps[:, 2 * (j % 2) + u, 0:P * len(ks)]
                        biased = kind == "B" and n < XT
                        ins = pe.matmul(to, qkT[rows, qb, n * P:(n + 1) * P], qkT[rows, kb, ks[0] * P:NT * P],
                                        start=True, stop=not biased)
                        if biased:
                            ins = pe.matmul(ps[:, 2 * (j % 2) + u, 0:SEQ], ident, bm[:, b % 2, u, n, :],
                                            start=False, stop=True)
                    ins.then_inc(scored, 1)

                def turn(j):
                    kind, b, n = jobs[j]
                    if kind == "A":
                        pe.wait_ge(a_ready, j + 1)
                    else:
                        pe.wait_ge(exp_done, 2 * (j + 1))
                    if j >= 1:
                        pe.wait_ge(at_ready, turned(j))
                    for u in range(1 if kind == "A" else 2):
                        for m in range(len(keys(n))):
                            ins = pe.transpose(ps[:, 4 + u, m * P:(m + 1) * P], Pb[:, j % 2, u, m * P:(m + 1) * P], ident)
                        ins.then_inc(a_turned, 1)

                def values(j):
                    kind, b, n = jobs[j]
                    ks = keys(n)
                    pe.wait_ge(at_ready, turned(j + 1))
                    if j >= 1:
                        pe.wait_ge(o_done, j)
                    for u in range(1 if kind == "A" else 2):
                        w = A_DV if kind == "A" else DH
                        col = b * A_DV if kind == "A" else HALF + (2 * b + u) * DH
                        for m, kt in enumerate(ks):
                            ins = pe.matmul(ps[:, 6, u * w:(u + 1) * w], aT[:, j % 2, u, m * P:(m + 1) * P],
                                            v[:, kt, col:col + w], start=(m == 0), stop=(m == len(ks) - 1))
                    ins.then_inc(av_done, 1)

                scores(0)
                scores(1)
                for j in range(NJ):
                    turn(j)
                    if j + 2 < NJ:
                        scores(j + 2)
                    values(j)
                    for i in total_at.get(j, ()):
                        pe.wait_ge(acc_ready, i + 1)
                        if i >= 1:
                            pe.wait_ge(sum_kept, i)
                        pe.matmul(ps[:, 7, :], ones, acc[:, i % 2, :], start=True, stop=True).then_inc(sum_psum, 1)

            @block.scalar
            def _(act):
                def turned_copy(j):
                    kind, b, n = jobs[j]
                    w = P * len(keys(n))
                    if j >= 2:
                        act.wait_ge(av_done, j - 1)
                    for u in range(1 if kind == "A" else 2):
                        act.wait_ge(a_turned, turned(j) + u + 1)
                        act.activation(aT[:, j % 2, u, 0:w], ps[:, 4 + u, 0:w], ACT.Copy).then_inc(at_ready, 1)

                def exponentials(j):
                    w = P * len(keys(jobs[j][2]))
                    if j >= 2:
                        act.wait_ge(a_turned, turned(j - 1))
                    act.wait_ge(shifted, j + 1)
                    for u in range(2):
                        act.activation(Pb[:, j % 2, u, 0:w], ps[:, 2 * (j % 2) + u, 0:w], ACT.Exp,
                                       bias=nm[:, 2 * j + u:2 * j + u + 1], scale=DH ** -0.5,
                                       accum_out=sm[:, 2 * j + u:2 * j + u + 1]).then_inc(exp_done, 1)

                exponentials(0)
                exponentials(1)
                for j in range(NJ):
                    turned_copy(j)
                    if j + 2 < NJ:
                        exponentials(j + 2)
                    for i in total_at.get(j, ()):
                        _, name, v_ = items[i]
                        at = mod_row_at(name, v_)
                        act.wait_ge(sum_psum, i + 1)
                        if i >= 2:
                            act.wait_ge(row_stored[i % 2], 16 * (i // 2))
                        act.activation(row[0:1, i % 2, :], ps[0:1, 7, :], ACT.Copy).then_inc(sum_kept, 1)
                        act.wait_ge(sum_kept, i + 1)
                        act.dma_start(T.mod_dram[:, at:at + HALF], row[0:1, i % 2, :]).then_inc(row_stored[i % 2], 16)
                for r in range(2):
                    act.wait_ge(row_stored[r], 16 * (len(items) // 2))

            @block.vector
            def _(dve):
                then = Steps(dve, step)

                def shift(j):
                    w = P * len(keys(jobs[j][2]))
                    c = slice(2 * j, 2 * j + 2)
                    dve.wait_ge(scored, j + 1)
                    then(dve.tensor_reduce(mx[:, c], ps[:, 2 * (j % 2):2 * (j % 2) + 2, 0:w], AX.X, ALU.max))
                    dve.tensor_scalar(nm[:, c], mx[:, c], -(DH ** -0.5), None, ALU.mult).then_inc(shifted, 1)

                def combine(j):
                    kind, b, n = jobs[j]
                    w = P * len(keys(n))
                    dve.wait_ge(exp_done, 2 * (j + 1))
                    then(dve.reciprocal(rs[:, 2 * j:2 * j + 2], sm[:, 2 * j:2 * j + 2]))
                    if kind == "A":
                        then(dve.tensor_scalar(cs[:, 2 * j:2 * j + 1], rs[:, 2 * j + 1:2 * j + 2], neg_lam, sm[:, 2 * j:2 * j + 1],
                                               ALU.mult, ALU.mult))
                        dve.scalar_tensor_tensor(Pb[:, j % 2, 0, 0:w], Pb[:, j % 2, 1, 0:w], cs[:, 2 * j:2 * j + 1],
                                                 Pb[:, j % 2, 0, 0:w], ALU.mult, ALU.add).then_inc(a_ready, 1)

                def keep(j):
                    kind, b, n = jobs[j]
                    dve.wait_ge(av_done, j + 1)
                    bank = ps[:, 6, :]
                    if kind == "A":
                        dve.tensor_scalar(O[:, n, b * A_DV:(b + 1) * A_DV], bank[:, 0:A_DV],
                                          rs[:, 2 * j:2 * j + 1], None, ALU.mult).then_inc(o_done, 1)
                    else:
                        for u in range(2):
                            c = HALF + (2 * b + u) * DH
                            ins = dve.tensor_scalar(O[:, n, c:c + DH], bank[:, u * DH:(u + 1) * DH],
                                                    rs[:, 2 * j + u:2 * j + u + 1], None, ALU.mult)
                        ins.then_inc(o_done, 1)

                def modulation(i, k):
                    m, name, v_ = items[i]
                    to = acc[:, i % 2, :]
                    if k == 0:
                        T.wait_chunk(dve, name)
                        if i >= 2:
                            dve.wait_ge(sum_psum, i - 1)
                    ins = dve.scalar_tensor_tensor(to, T.chunk(name)[:, k, :], silu[:, v_, k:k + 1],
                                                   T.bias(name) if k == 0 else to, ALU.mult, ALU.add)
                    if k < KD - 1:
                        then(ins)
                    else:
                        ins.then_inc(acc_ready, 1)

                shift(0)
                shift(1)
                combine(0)
                for j in range(NJ):
                    if j + 1 < NJ:
                        combine(j + 1)
                    if j >= 1:
                        keep(j - 1)
                    if j + 2 < NJ:
                        shift(j + 2)
                    for i, k in slices[PER_JOB * j:PER_JOB * (j + 1)]:
                        modulation(i, k)
                keep(NJ - 1)


def out_stage(T, i, ntiles, O, oT, work):
    nc, t, f, ps = T.nc, T.t, T.f, T.ps
    X, mod = f(XR, NT, D), f(MOD, 2, 6, D)
    ident = f(KEEP + K_ID, P)
    nh, dv = (A_HEADS, A_DV) if i == 0 else (C_HEADS, C_DV)
    wn = nh * dv
    sub_g, sq, ss, rstd, gate = work
    with ExitStack() as ctx:
        g_landed, var_ready, std_ready, o_ready, o_psum, o_evac, out_done, x_done, silu_done, step = T.sems(
            ctx, *[f"o{i}_{n}" for n in ("g_landed", "var_ready", "std_ready", "o_ready", "o_psum", "o_evac",
                                         "out_done", "x_done", "silu_done", "step")])
        groups = [(c, n) for c in range(2) for n in range(ntiles)]
        with nc.Block() as block:
            @block.sync
            def _(sp):
                g = t["att_subln_g"] if i == 0 else t["gla_norm_g"]
                sp.dma_start(sub_g, g.partition_broadcast(P)).then_inc(g_landed, 16)
                sp.wait_ge(g_landed, 16)

            @block.scalar
            def _(act):
                if i == 1:
                    act.activation(gate, gate, ACT.Silu).then_inc(silu_done, 1)
                act.wait_ge(var_ready, 1)
                act.activation(rstd, ss, ACT.Sqrt).then_inc(std_ready, 1)
                for n in range(ntiles):
                    act.wait_ge(o_psum, n + 1)
                    for b in range(2):
                        ins = act.activation(oT[:, 4 * b:4 * b + 4, n * P:(n + 1) * P],
                                             ps[:, 2 * (n % 2) + b, :].rearrange("p (k n) -> p k n", n=P), ACT.Copy)
                    ins.then_inc(o_evac, 1)

            @block.vector
            def _(dve):
                then = Steps(dve, step)
                dve.wait_ge(g_landed, 16)
                if i == 0:
                    then(dve.tensor_scalar(sub_g, sub_g, 1.0 - LAM_INIT, None, ALU.mult))
                for n in range(ntiles):
                    then(dve.tensor_tensor(sq[:, 0:wn], O[:, n, 0:wn], O[:, n, 0:wn], ALU.mult))
                    then(dve.tensor_reduce(ss[:, n * nh:(n + 1) * nh], sq[:, 0:wn].rearrange("p (h d) -> p h d", d=dv), AX.X, ALU.add))
                dve.tensor_scalar(ss, ss, 1.0 / dv, EPS, ALU.mult, ALU.add).then_inc(var_ready, 1)
                dve.wait_ge(std_ready, 1)
                then(dve.reciprocal(rstd, rstd))
                if i == 1:
                    dve.wait_ge(silu_done, 1)
                for n in range(ntiles):
                    for h in range(nh):
                        part = O[:, n, h * dv:(h + 1) * dv]
                        ins = dve.scalar_tensor_tensor(part, part, rstd[:, n * nh + h:n * nh + h + 1], sub_g, ALU.mult, ALU.mult)
                    if i == 1:
                        then(ins)
                        ins = dve.tensor_tensor(O[:, n, :], O[:, n, :], gate[:, n, :], ALU.mult)
                    ins.then_inc(o_ready, 1)
                for m, (c, n) in enumerate(groups):
                    cols = slice(c * HALF, (c + 1) * HALF)
                    dve.wait_ge(out_done, m + 1)
                    v = 0 if n < XT else 1
                    dve.tensor_tensor(sq[:, (m % 2) * HALF:(m % 2 + 1) * HALF], ps[:, 4 + m % 4, :], mod[:, v, G1, cols], ALU.mult).then_inc(x_done, 1)
                    dve.wait_ge(x_done, m + 1)
                    then(dve.tensor_tensor(X[:, n, cols], X[:, n, cols], sq[:, (m % 2) * HALF:(m % 2 + 1) * HALF], ALU.add))

            @block.tensor
            def _(pe):
                for n in range(ntiles):
                    pe.wait_ge(o_ready, n + 1)
                    if n >= 2:
                        pe.wait_ge(o_evac, n - 1)
                    for k in range(KD):
                        ins = pe.transpose(ps[:, 2 * (n % 2) + k // 4, (k % 4) * P:(k % 4 + 1) * P],
                                           O[:, n, k * P:(k + 1) * P], ident)
                    ins.then_inc(o_psum, 1)
                for m, (c, n) in enumerate(groups):
                    w = T.chunk(("out", i, c))
                    if n == 0:
                        T.wait_chunk(pe, ("out", i, c))
                    if m < ntiles:
                        pe.wait_ge(o_evac, m + 1)
                    if m >= 4:
                        pe.wait_ge(x_done, m - 3)
                    for k in range(KD):
                        ins = pe.matmul(ps[:, 4 + m % 4, :], oT[:, k, n * P:(n + 1) * P], w[:, k, :], start=(k == 0), stop=(k == KD - 1))
                    ins.then_inc(out_done, 1)


def expert_weights(T, i, kind, e):
    w = T.t[f"moe_{kind}"][i]
    if isinstance(e, int):
        w = w[e:e + 1]
    else:
        w = w[bass.ds(e, 1)]
    return w.rearrange("o (k p) n -> p (o k) n", p=P)


def expert_slot(T, kind, e):
    s = 3 * (e % 2) + ("w1", "w3", "w2").index(kind)
    return T.slot(s) if kind != "w2" else T.f(RING + s * CH, DE // P, D)


def first_expert_loads(T, sp, i):
    for e in range(2):
        for kind in ("w1", "w3", "w2"):
            sp.dma_start(expert_slot(T, kind, e), expert_weights(T, i, kind, e)).then_inc(T.w_landed[kind][e], 16)


def load_modulation(T, sp):
    n = G2 * D
    sp.dma_start(T.f(MOD, n), T.mod_dram[:, 0:n].partition_broadcast(P)).then_inc(T.mod_landed, 16)
    sp.dma_start(T.f(MOD + 6 * D, 2 * D), T.mod_dram[:, 6 * D:8 * D].partition_broadcast(P)).then_inc(T.mod_landed, 16)


def load_gate2(T, sp):
    sp.dma_start(T.f(MOD + G2 * D, D), T.mod_dram[:, G2 * D:6 * D].partition_broadcast(P)).then_inc(T.mod_landed, 16)


def route_stage(T, i, nt):
    nc, t, f, ps = T.nc, T.t, T.f, T.ps
    hT = f(HI, KD, NT * P)
    cap = nt * P
    nb = nt - 1
    nov = 2 * nt - 1
    at = [HI + 4 * D]

    def take(*shape):
        v = f(at[0], *shape)
        at[0] += int(np.prod(shape))
        return v

    pick = take(2 * nt, cap)
    rw = take(KD, NE)
    tri, iota_cap = take(P), take(cap)
    sc, sel, ing, m1, m2, cand, oh0, oh1, rank = (take(nt, NE) for _ in range(9))
    pair = take(nt, NG, 6)
    gs, geq, gc = (take(nt, NG) for _ in range(3))
    gmx, grp, mxv, e0, e1, w0, w1, r0, r1, wsum = (take(nt) for _ in range(10))
    ohtok = take(2 * nt, NE)
    prod = take(nt, NE)
    cnt = take(NE)
    rows = take(nt, NE)
    ovf = take(NE, nb)
    ovp = take(2, 32 + NE * nb)
    ovs = take(nov, NE * nb)
    ovm = take(nov, NE * nb)
    ovr, ovk, ovl = take(2, nov), take(2, NE, nb), take(NE, nb)
    nov_f = take(1)
    ebase = take(NE)
    assert at[0] <= END, at[0]
    i16 = f(KEEP + K_IOTA, NE)
    tok = f(KEEP + K_TOK, NT)
    rbias = f(KEEP + K_RBIAS, NE)
    ones = f(KEEP + K_ONE, P)
    gate = f(KEEP + K_GATE, 2, NT)
    slot = f(KEEP + K_SLOT, 2, NT).bitcast(U32)
    rows_u = f(KEEP + K_ROWS, NT, NE).bitcast(U32)
    S3 = (P, nt, NE)
    with ExitStack() as ctx:
        in_landed, logits, sig, masks, ranks, picked, listed, step = T.sems(
            ctx, *[f"r{i}_{n}" for n in ("in_landed", "logits", "sigmoid", "masks", "ranks", "picked", "listed", "step")])
        with nc.Block() as block:
            @block.sync
            def _(sp):
                sp.dma_start(rw, t["router_w"].rearrange("(k p) e -> p k e", p=P)).then_inc(in_landed, 16)
                sp.dma_start(tri, t["k_before"]).then_inc(in_landed, 16)
                sp.dma_start(iota_cap, t["k_iota512"][:, 0:cap].partition_broadcast(P)).then_inc(in_landed, 16)
                sp.dma_start(ovk, t[f"k_over{i}"].partition_broadcast(P)).then_inc(in_landed, 16)
                first_expert_loads(T, sp, i)
                if i == 0:
                    load_modulation(T, sp)
                sp.wait_ge(in_landed, 64)

            @block.tensor
            def _(pe):
                pe.wait_ge(in_landed, 64)
                for n in range(nt):
                    for k in range(KD):
                        ins = pe.matmul(ps[:, 0, n * NE:(n + 1) * NE], hT[:, k, n * P:(n + 1) * P], rw[:, k, :],
                                        start=(k == 0), stop=(k == KD - 1))
                ins.then_inc(logits, 1)
                pe.wait_ge(masks, 1)
                for n in range(nt):
                    for m in range(n + 1):
                        pe.matmul(ps[:, 1, n * NE:(n + 1) * NE], ones if m < n else tri, prod[:, m, :], start=(m == 0), stop=(m == n))
                for m in range(nt):
                    ins = pe.matmul(ps[:, 1, nt * NE:(nt + 1) * NE], ones, prod[:, m, :], start=(m == 0), stop=(m == nt - 1))
                ins.then_inc(ranks, 1)
                pe.wait_ge(picked, 1)
                for b in range(nt):
                    for m in range(2 * nt):
                        ins = pe.matmul(ps[:, 2, b * NE:(b + 1) * NE], pick[:, m, b * P:(b + 1) * P], ohtok[:, m, :],
                                        start=(m == 0), stop=(m == 2 * nt - 1))
                ins.then_inc(listed, 1)

            @block.scalar
            def _(act):
                act.wait_ge(logits, 1)
                act.activation(sc, ps[:, 0, 0:nt * NE].rearrange("p (n e) -> p n e", e=NE), ACT.Sigmoid).then_inc(sig, 1)

            @block.vector
            def _(dve):
                then = Steps(dve, step)
                tt, ts, stt, red = dve.tensor_tensor, dve.tensor_scalar, dve.scalar_tensor_tensor, dve.tensor_reduce
                dve.wait_ge(sig, 1)
                then(tt(sel, sc, bc(rbias, 1, S3), ALU.add))
                s4 = sel.rearrange("p n (g e) -> p n g e", e=EPG)
                tt(pair[:, :, :, 0:3], s4[:, :, :, 0:3], s4[:, :, :, 1:4], ALU.add)
                tt(pair[:, :, :, 3:5], s4[:, :, :, 0:2], s4[:, :, :, 2:4], ALU.add)
                then(tt(pair[:, :, :, 5:6], s4[:, :, :, 0:1], s4[:, :, :, 3:4], ALU.add))
                then(red(gs, pair, AX.X, ALU.max))
                then(red(gmx, gs, AX.X, ALU.max))
                then(tt(geq, gs, bc(gmx, 2, (P, nt, NG)), ALU.is_equal))
                then(ts(geq, geq, -64.0, 64.0, ALU.mult, ALU.add))
                then(tt(gc, geq, bc(i16[:, 0:NG], 1, (P, nt, NG)), ALU.add))
                then(red(grp, gc, AX.X, ALU.min))
                then(tt(geq, bc(i16[:, 0:NG], 1, (P, nt, NG)), bc(grp, 2, (P, nt, NG)), ALU.is_equal))
                then(dve.tensor_copy(ing.rearrange("p n (g e) -> p n g e", e=EPG), bc(geq, 3, (P, nt, NG, EPG))))
                then(ts(m2, ing, 1.0, BIG, ALU.subtract, ALU.mult))
                then(tt(m1, sel, ing, ALU.mult))
                then(tt(m1, m1, m2, ALU.add))
                for oh, e in ((oh0, e0), (oh1, e1)):
                    then(red(mxv, m1, AX.X, ALU.max))
                    then(tt(cand, m1, bc(mxv, 2, S3), ALU.is_equal))
                    then(ts(cand, cand, -64.0, 64.0, ALU.mult, ALU.add))
                    then(tt(cand, cand, bc(i16, 1, S3), ALU.add))
                    then(red(e, cand, AX.X, ALU.min))
                    then(tt(oh, bc(i16, 1, S3), bc(e, 2, S3), ALU.is_equal))
                    if oh is oh0:
                        then(stt(m1, oh, -BIG, m1, ALU.mult, ALU.add))
                dve.tensor_tensor(prod, oh0, oh1, ALU.add).then_inc(masks, 1)
                for oh, w in ((oh0, w0), (oh1, w1)):
                    then(tt(cand, sc, oh, ALU.mult))
                    then(red(w, cand, AX.X, ALU.add))
                then(tt(wsum, w0, w1, ALU.add))
                then(dve.reciprocal(wsum, wsum))
                tt(gate[:, 0, 0:nt], w0, wsum, ALU.mult)
                tt(gate[:, 1, 0:nt], w1, wsum, ALU.mult)
                for m, oh in enumerate((oh0, oh1)):
                    ins = tt(ohtok[:, m * nt:(m + 1) * nt, :], oh, bc(tok[:, 0:nt], 2, S3), ALU.mult)
                then(ins)
                dve.wait_ge(ranks, 1)
                dve.tensor_copy(cnt, ps[:, 1, nt * NE:(nt + 1) * NE])
                then(dve.tensor_copy(rank, ps[:, 1, 0:nt * NE].rearrange("p (n e) -> p n e", e=NE)))
                for m, (oh, e, r) in enumerate(((oh0, e0, r0), (oh1, e1, r1))):
                    then(tt(cand, rank, oh, ALU.mult))
                    then(red(r, cand, AX.X, ALU.add))
                    for n in range(nt):
                        ins = ts(pick[:, m * nt + n, :], iota_cap, r[:, n:n + 1], None, ALU.is_equal)
                ins.then_inc(picked, 1)
                ovflat = ovf.rearrange("p e b -> p (e b)")
                then(tt(ovf, bc(cnt, 2, (P, NE, nb)), ovk[:, 0], ALU.is_gt))
                then(red(nov_f, ovflat, AX.X, ALU.add))
                then(dve.tensor_copy(f(KEEP + K_NOV, 1).bitcast(I32), nov_f))
                width = NE * nb
                then(dve.memset(ovp, 0.0))
                then(dve.tensor_copy(ovp[:, 0, 32:32 + width], ovflat))
                src, d = 0, 1
                while d < width:
                    then(tt(ovp[:, 1 - src, 32:32 + width], ovp[:, src, 32:32 + width], ovp[:, src, 32 - d:32 - d + width], ALU.add))
                    src, d = 1 - src, 2 * d
                run = ovp[:, src, 32:32 + width].rearrange("p (e b) -> p e b", b=nb)[:, :, 0]
                then(tt(ebase, run, ovf[:, :, 0], ALU.subtract))
                then(ts(ebase, ebase, float(P), float((NE - 1) * P), ALU.mult, ALU.add))
                for m, (oh, e, r) in enumerate(((oh0, e0, r0), (oh1, e1, r1))):
                    then(tt(cand, oh, bc(ebase, 1, S3), ALU.mult))
                    then(red(mxv, cand, AX.X, ALU.add))
                    then(stt(mxv, e, -float(P), mxv, ALU.mult, ALU.add))
                    then(ts(wsum, r, float(P), None, ALU.is_ge))
                    then(tt(mxv, mxv, wsum, ALU.mult))
                    then(stt(mxv, e, float(P), mxv, ALU.mult, ALU.add))
                    then(tt(mxv, mxv, r, ALU.add))
                    then(dve.tensor_copy(slot[:, m, 0:nt], mxv))
                then(tt(ovs, bc(ovp[:, src, 32:32 + width], 1, (P, nov, width)),
                        bc(iota_cap[:, 1:nov + 1], 2, (P, nov, width)), ALU.is_equal))
                then(tt(ovs, ovs, bc(ovflat, 1, (P, nov, width)), ALU.mult))
                then(tt(ovm, ovs, bc(ovk[:, 1].rearrange("p e b -> p (e b)"), 1, (P, nov, width)), ALU.mult))
                then(red(ovr[:, 1, :], ovm, AX.X, ALU.add))
                dve.wait_ge(listed, 1)
                then(dve.tensor_copy(rows, ps[:, 2, 0:nt * NE].rearrange("p (b e) -> p b e", e=NE)))
                dve.tensor_copy(rows_u[:, 0:nt, :], rows)
                for b in range(nb):
                    ins = dve.tensor_copy(ovl[:, :, b], rows[:, b + 1, :])
                then(ins)
                then(tt(ovm, ovs, bc(ovl.rearrange("p e b -> p (e b)"), 1, (P, nov, width)), ALU.mult))
                then(red(ovr[:, 0, :], ovm, AX.X, ALU.add))
                dve.tensor_copy(f(KEEP + K_OVIDX, nov).bitcast(U32), ovr[:, 0, :])
                dve.tensor_copy(f(KEEP + K_OVEXP, nov).bitcast(I32), ovr[:, 1, :])



class ExpertBuffers:
    def __init__(self, T):
        f, at = T.f, HI
        self.rows = f(at, 2, D)
        self.rT = f(at + 2 * D, 2, KD, P)
        self.s = f(at + 4 * D, DE)
        self.g = f(at + 4 * D + DE, DE)
        self.gT = f(at + 5 * D, DE // P, P)
        self.y = f(at + 6 * D, 2, D)


def moe_stage(T, i, nt):
    nc, t, f, ps = T.nc, T.t, T.f, T.ps
    B = ExpertBuffers(T)
    ident = f(KEEP + K_ID, P)
    rows_u = f(KEEP + K_ROWS, NT, NE).bitcast(U32)
    base = T.w_base[i]
    with ExitStack() as ctx:
        (rows_turned, rT_ready, up_done, act_done, lin_done, g_ready, g_turned, gT_ready,
         y_psum, y_ready, y_stored0, y_stored1, rows_landed0, rows_landed1) = T.sems(
            ctx, *[f"m{i}_{n}" for n in ("rows_turned", "rT_ready", "up_done", "act_done",
                                         "lin_done", "g_ready", "g_turned", "gT_ready", "y_psum", "y_ready", "y_stored0", "y_stored1", "rows_landed0", "rows_landed1")])
        y_stored, rows_landed = (y_stored0, y_stored1), (rows_landed0, rows_landed1)
        with nc.Block() as block:
            @block.gpsimd
            def _(pool):
                for e in range(NE):
                    if e >= 2:
                        pool.wait_ge(rows_turned, e - 1)
                    pool.indirect_dma_start(B.rows[:, e % 2, :], None, T.h2_dram,
                                            bass.IndirectOffsetOnAxis(ap=rows_u[:, 0, e:e + 1], axis=0)).then_inc(rows_landed[e % 2], 16)

            @block.sync
            def _(sp):
                with sp.Fori(0, (NE - 2) // 2) as n:
                    for s in range(2):
                        e = n * 2 + (2 + s)
                        for kind, done in (("w1", up_done), ("w3", lin_done), ("w2", y_psum)):
                            sp.wait_ge(done, e - 1)
                            sp.dma_start(expert_slot(T, kind, s), expert_weights(T, i, kind, e))\
                              .then_inc(T.w_landed[kind][s], 16)

            @block.tensor
            def _(pe):
                def arrived(kind, s, m):
                    pe.wait_ge(T.w_landed[kind][s], (m + 1) * 16 + base)

                def up(e, s, m):
                    pe.wait_ge(rT_ready, (e + 1) * 2)
                    if not isinstance(e, int) or e >= 1:
                        pe.wait_ge(act_done, e)
                    arrived("w1", s, m)
                    w = expert_slot(T, "w1", s)
                    for k in range(KD):
                        ins = pe.matmul(ps[:, 0, :], B.rT[:, s, k, :], w[:, k, :], start=(k == 0), stop=(k == KD - 1))
                    ins.then_inc(up_done, 1)

                def linear(e, s, m):
                    if not isinstance(e, int) or e >= 1:
                        pe.wait_ge(g_ready, e)
                    arrived("w3", s, m)
                    w = expert_slot(T, "w3", s)
                    for k in range(KD):
                        ins = pe.matmul(ps[:, 1, :], B.rT[:, s, k, :], w[:, k, :], start=(k == 0), stop=(k == KD - 1))
                    ins.then_inc(lin_done, 1)

                def turn_rows(e, s, m):
                    pe.wait_ge(rows_landed[s], (m + 1) * 16)
                    if not isinstance(e, int) or e >= 1:
                        pe.wait_ge(rT_ready, e * 2)
                    for k in range(KD):
                        ins = pe.transpose(ps[:, 2 + k // 4, (k % 4) * P:(k % 4 + 1) * P], B.rows[:, s, k * P:(k + 1) * P], ident)
                    ins.then_inc(rows_turned, 1)

                def turn_hidden(e):
                    pe.wait_ge(g_ready, e + 1)
                    if not isinstance(e, int) or e >= 1:
                        pe.wait_ge(gT_ready, e)
                    for k in range(DE // P):
                        ins = pe.transpose(ps[:, 4, k * P:(k + 1) * P], B.g[:, k * P:(k + 1) * P], ident)
                    ins.then_inc(g_turned, 1)

                def down(e, s, m):
                    pe.wait_ge(gT_ready, e + 1)
                    if not isinstance(e, int) or e >= 1:
                        pe.wait_ge(y_ready, e * 2)
                    arrived("w2", s, m)
                    w = expert_slot(T, "w2", s)
                    for h in range(2):
                        for k in range(DE // P):
                            ins = pe.matmul(ps[:, 5 + h, :], B.gT[:, k, :], w[:, k, h * HALF:(h + 1) * HALF],
                                            start=(k == 0), stop=(k == DE // P - 1))
                    ins.then_inc(y_psum, 1)

                turn_rows(0, 0, 0)
                up(0, 0, 0)
                linear(0, 0, 0)
                turn_rows(1, 1, 0)
                for e in (1, 2):
                    up(e, e % 2, e // 2)
                    turn_hidden(e - 1)
                    linear(e, e % 2, e // 2)
                    turn_rows(e + 1, (e + 1) % 2, (e + 1) // 2)
                    down(e - 1, (e - 1) % 2, (e - 1) // 2)
                with pe.Fori(0, (NE - 4) // 2) as n:
                    for s in range(2):
                        e = n * 2 + (3 + s)
                        up(e, (1 + s) % 2, n + (1 + s))
                        turn_hidden(e - 1)
                        linear(e, (1 + s) % 2, n + (1 + s))
                        turn_rows(e + 1, s, n + 2)
                        down(e - 1, s, n + 1)
                e = NE - 1
                up(e, 1, NE // 2 - 1)
                turn_hidden(e - 1)
                linear(e, 1, NE // 2 - 1)
                down(e - 1, 0, NE // 2 - 1)
                turn_hidden(e)
                down(e, 1, NE // 2 - 1)

            @block.scalar
            def _(act):
                def silu(e):
                    act.wait_ge(up_done, e + 1)
                    if not isinstance(e, int) or e >= 1:
                        act.wait_ge(g_ready, e)
                    act.activation(B.s, ps[:, 0, :], ACT.Silu).then_inc(act_done, 1)

                def copy_rT(e, s):
                    act.wait_ge(rows_turned, e + 1)
                    if not isinstance(e, int) or e >= 2:
                        act.wait_ge(lin_done, e - 1)
                    act.activation(B.rT[:, s, 0:4, :], ps[:, 2, :].rearrange("p (k n) -> p k n", n=P), ACT.Copy).then_inc(rT_ready, 1)

                def copy_y(e, s, m):
                    act.wait_ge(y_psum, e + 1)
                    if not isinstance(m, int) or m >= 1:
                        act.wait_ge(y_stored[s], m * 16)
                    act.activation(B.y[:, s, 0:HALF], ps[:, 5, :], ACT.Copy).then_inc(y_ready, 1)
                    act.wait_ge(y_ready, (e + 1) * 2)
                    to = T.y_dram[e * P:(e + 1) * P, :] if isinstance(e, int) else T.y_dram[bass.ds(e * P, P), :]
                    act.dma_start(to, B.y[:, s, :]).then_inc(y_stored[s], 16)

                copy_rT(0, 0)
                silu(0)
                copy_rT(1, 1)
                silu(1)
                copy_rT(2, 0)
                copy_y(0, 0, 0)
                silu(2)
                copy_rT(3, 1)
                copy_y(1, 1, 0)
                with act.Fori(0, (NE - 4) // 2) as n:
                    for s in range(2):
                        e = n * 2 + (3 + s)
                        silu(e)
                        copy_rT(e + 1, s)
                        copy_y(e - 1, s, n + 1)
                silu(NE - 1)
                copy_y(NE - 2, 0, NE // 2 - 1)
                copy_y(NE - 1, 1, NE // 2 - 1)
                for stored in y_stored:
                    act.wait_ge(stored, NE // 2 * 16)

            @block.vector
            def _(dve):
                def copy_rT(e, s):
                    dve.wait_ge(rows_turned, e + 1)
                    if not isinstance(e, int) or e >= 2:
                        dve.wait_ge(lin_done, e - 1)
                    dve.tensor_copy(B.rT[:, s, 4:8, :], ps[:, 3, :].rearrange("p (k n) -> p k n", n=P)).then_inc(rT_ready, 1)

                def copy_gT(e):
                    dve.wait_ge(g_turned, e + 1)
                    if not isinstance(e, int) or e >= 1:
                        dve.wait_ge(y_psum, e)
                    dve.tensor_copy(B.gT, ps[:, 4, :].rearrange("p (k n) -> p k n", n=P)).then_inc(gT_ready, 1)

                def product(e):
                    dve.wait_ge(act_done, e + 1)
                    dve.wait_ge(lin_done, e + 1)
                    if not isinstance(e, int) or e >= 1:
                        dve.wait_ge(g_turned, e)
                    dve.tensor_tensor(B.g, ps[:, 1, :], B.s, ALU.mult).then_inc(g_ready, 1)

                def copy_y(e, s, m):
                    dve.wait_ge(y_psum, e + 1)
                    if not isinstance(m, int) or m >= 1:
                        dve.wait_ge(y_stored[s], m * 16)
                    dve.tensor_copy(B.y[:, s, HALF:D], ps[:, 6, :]).then_inc(y_ready, 1)

                copy_rT(0, 0)
                product(0)
                copy_rT(1, 1)
                for e in (1, 2):
                    copy_gT(e - 1)
                    product(e)
                    copy_rT(e + 1, (e + 1) % 2)
                    copy_y(e - 1, (e - 1) % 2, 0)
                with dve.Fori(0, (NE - 4) // 2) as n:
                    for s in range(2):
                        e = n * 2 + (3 + s)
                        copy_gT(e - 1)
                        product(e)
                        copy_rT(e + 1, s)
                        copy_y(e - 1, s, n + 1)
                copy_gT(NE - 2)
                product(NE - 1)
                copy_y(NE - 2, 0, NE // 2 - 1)
                copy_gT(NE - 1)
                copy_y(NE - 1, 1, NE // 2 - 1)


def overflow_stage(T, i, nt):
    nc, t, f, ps = T.nc, T.t, T.f, T.ps
    B = ExpertBuffers(T)
    nov = 2 * nt - 1
    ident = f(KEEP + K_ID, P)
    count = f(KEEP + K_NOV, 1).bitcast(I32)[0:1, :]
    ov_idx = f(KEEP + K_OVIDX, nov).bitcast(U32)
    ov_exp = f(KEEP + K_OVEXP, nov).bitcast(I32)
    cur = f(KEEP + K_CUR, 1).bitcast(U32)
    with ExitStack() as ctx:
        (idx_ready, rows_landed, w_landed, rows_turned, rT_ready, up_done, act_done, g_ready, g_turned,
         gT_ready, y_psum, y_ready, y_stored) = T.sems(
            ctx, *[f"v{i}_{n}" for n in ("idx_ready", "rows_landed", "w_landed", "rows_turned", "rT_ready", "up_done",
                                         "act_done", "g_ready", "g_turned", "gT_ready", "y_psum", "y_ready", "y_stored")])

        def repeated(engine, body):
            n_tiles = engine.value_load(count, min_val=0, max_val=nov)
            with engine.If(n_tiles > 0):
                with engine.Fori(0, n_tiles) as n:
                    body(n)
                engine.nop()
            with engine.Else():
                engine.nop()
            engine.nop()

        with nc.Block() as block:
            @block.gpsimd
            def _(pool):
                def tile(n):
                    pool.tensor_copy(cur, ov_idx[:, bass.ds(n, 1)])
                    pool.drain()
                    pool.indirect_dma_start(B.rows[:, 0, :], None, T.h2_dram, bass.IndirectOffsetOnAxis(ap=cur, axis=0))\
                        .then_inc(rows_landed, 16)
                    pool.wait_ge(y_stored, (n + 1) * 16)
                repeated(pool, tile)

            @block.sync
            def _(sp):
                def tile(n):
                    sp.wait_ge(rows_landed, (n + 1) * 16)
                    e = sp.value_load(ov_exp[0:1, bass.ds(n, 1)], min_val=0, max_val=NE - 1)
                    for kind in ("w1", "w3", "w2"):
                        sp.dma_start(expert_slot(T, kind, 0), expert_weights(T, i, kind, e)).then_inc(w_landed, 16)
                repeated(sp, tile)

            @block.tensor
            def _(pe):
                def tile(n):
                    pe.wait_ge(rows_landed, (n + 1) * 16)
                    pe.wait_ge(w_landed, (n + 1) * 48)
                    for k in range(KD):
                        ins = pe.transpose(ps[:, 2 + k // 4, (k % 4) * P:(k % 4 + 1) * P], B.rows[:, 0, k * P:(k + 1) * P], ident)
                    ins.then_inc(rows_turned, 1)
                    pe.wait_ge(rT_ready, n + 1)
                    for b, kind in enumerate(("w1", "w3")):
                        w = expert_slot(T, kind, 0)
                        for k in range(KD):
                            ins = pe.matmul(ps[:, b, :], B.rT[:, 0, k, :], w[:, k, :], start=(k == 0), stop=(k == KD - 1))
                    ins.then_inc(up_done, 1)
                    pe.wait_ge(g_ready, n + 1)
                    for k in range(DE // P):
                        ins = pe.transpose(ps[:, 4, k * P:(k + 1) * P], B.g[:, k * P:(k + 1) * P], ident)
                    ins.then_inc(g_turned, 1)
                    pe.wait_ge(gT_ready, n + 1)
                    w = expert_slot(T, "w2", 0)
                    for h in range(2):
                        for k in range(DE // P):
                            ins = pe.matmul(ps[:, 5 + h, :], B.gT[:, k, :], w[:, k, h * HALF:(h + 1) * HALF],
                                            start=(k == 0), stop=(k == DE // P - 1))
                    ins.then_inc(y_psum, 1)
                repeated(pe, tile)

            @block.scalar
            def _(act):
                def tile(n):
                    act.wait_ge(up_done, n + 1)
                    act.activation(B.s, ps[:, 0, :], ACT.Silu).then_inc(act_done, 1)
                    act.wait_ge(y_ready, n + 1)
                    act.dma_start(T.y_dram[bass.ds(n * P + NE * P, P), :], B.y[:, 0, :]).then_inc(y_stored, 16)
                    act.wait_ge(y_stored, (n + 1) * 16)
                repeated(act, tile)

            @block.vector
            def _(dve):
                def tile(n):
                    dve.wait_ge(rows_turned, n + 1)
                    dve.tensor_copy(B.rT[:, 0].rearrange("p k n -> p (k n)"), ps[:, 2:4, :].rearrange("p b n -> p (b n)")).then_inc(rT_ready, 1)
                    dve.wait_ge(act_done, n + 1)
                    dve.tensor_tensor(B.g, ps[:, 1, :], B.s, ALU.mult).then_inc(g_ready, 1)
                    dve.wait_ge(g_turned, n + 1)
                    dve.tensor_copy(B.gT, ps[:, 4, :].rearrange("p (k n) -> p k n", n=P)).then_inc(gT_ready, 1)
                    dve.wait_ge(y_psum, n + 1)
                    dve.tensor_copy(B.y[:, 0, :], ps[:, 5:7, :].rearrange("p b n -> p (b n)")).then_inc(y_ready, 1)
                repeated(dve, tile)


def combine_stage(T, i, nt, load_to):
    nc, t, f = T.nc, T.t, T.f
    X, mod = f(XR, NT, D), f(MOD, 2, 6, D)
    y = f(HI, 2, 2, D)
    gate, slot = f(KEEP + K_GATE, 2, NT), f(KEEP + K_SLOT, 2, NT).bitcast(U32)
    with ExitStack() as ctx:
        y_landed0, y_landed1, tile_done, step = T.sems(ctx, *[f"c{i}_{n}" for n in ("y_landed0", "y_landed1", "tile_done", "step")])
        y_landed = (y_landed0, y_landed1)
        with nc.Block() as block:
            @block.gpsimd
            def _(pool):
                for n in range(nt):
                    if n >= 2:
                        pool.wait_ge(tile_done, n - 1)
                    for m in range(2):
                        pool.indirect_dma_start(y[:, n % 2, m, :], None, T.y_dram,
                                                bass.IndirectOffsetOnAxis(ap=slot[:, m, n:n + 1], axis=0)).then_inc(y_landed[n % 2], 16)

            @block.sync
            def _(sp):
                load_to(sp)

            @block.vector
            def _(dve):
                then = Steps(dve, step)
                for n in range(nt):
                    v = 0 if n < XT else 1
                    dve.wait_ge(y_landed[n % 2], 32 * (n // 2 + 1))
                    a, b = y[:, n % 2, 0, :], y[:, n % 2, 1, :]
                    then(dve.tensor_scalar(a, a, gate[:, 0, n:n + 1], None, ALU.mult))
                    then(dve.scalar_tensor_tensor(a, b, gate[:, 1, n:n + 1], a, ALU.mult, ALU.add))
                    then(dve.tensor_tensor(a, a, mod[:, v, G2, :], ALU.mult))
                    dve.tensor_tensor(X[:, n, :], X[:, n, :], a, ALU.add).then_inc(tile_done, 1)


QR, KR, VR, GT = LO, LO + XT * HALF, LO + XT * HALF + NT * HALF, LO + XT * HALF + NT * HALF + NT * D
LR, WG = GT + XT * D, GT + XT * D + 2 * HALF
GDEC = HI + 4 * D


def gla_project_stage(T):
    nc, t, f, ps = T.nc, T.t, T.f, T.ps
    hT = f(HI, KD, NT * P)
    q, k_, v, gate = f(QR, XT, HALF), f(KR, NT, HALF), f(VR, NT, D), f(GT, XT, D)
    lrT, w_lr = f(LR, 2, HALF), f(HI + 4 * D, KD, 2 * RANK)
    dests = [(q, 0, XT), (k_, 0, NT), (v, 0, NT), (v, HALF, NT), (gate, 0, XT), (gate, HALF, XT)]
    groups = [(c, n) for c in range(6) for n in range(dests[c][2])]
    ends = np.cumsum([d[2] for d in dests])
    with ExitStack() as ctx:
        lr_landed, proj_done, proj_evac, lr_done, lr_evac = T.sems(ctx, "lr_landed", "gproj_done", "gproj_evac", "lr_done", "lr_evac")
        with nc.Block() as block:
            @block.sync
            def _(sp):
                sp.dma_start(w_lr, t["gla_w_in"][0][:, 6 * HALF:].rearrange("(k p) n -> p k n", p=P)).then_inc(lr_landed, 16)
                T.load_chunks(sp, ("out", 1, 1), {("in", 1, j): (proj_done, int(ends[j])) for j in range(6)})
                sp.wait_ge(lr_landed, 16)

            @block.tensor
            def _(pe):
                pe.wait_ge(lr_landed, 16)
                for d in range(2):
                    for k in range(KD):
                        ins = pe.matmul(ps[0:RANK, 4 + d, :], w_lr[:, k, d * RANK:(d + 1) * RANK], hT[:, k, :],
                                        start=(k == 0), stop=(k == KD - 1))
                ins.then_inc(lr_done, 1)
                for m, (c, n) in enumerate(groups):
                    w = T.chunk(("in", 1, c))
                    if n == 0:
                        T.wait_chunk(pe, ("in", 1, c))
                    if m >= 4:
                        pe.wait_ge(proj_evac, m - 3)
                    for k in range(KD):
                        ins = pe.matmul(ps[:, m % 4, :], hT[:, k, n * P:(n + 1) * P], w[:, k, :], start=(k == 0), stop=(k == KD - 1))
                    ins.then_inc(proj_done, 1)

            @block.scalar
            def _(act):
                act.wait_ge(lr_done, 1)
                for d in range(2):
                    act.activation(lrT[0:RANK, d, :], ps[0:RANK, 4 + d, :], ACT.Copy)
                for m, (c, n) in enumerate(groups):
                    to, col, _ = dests[c]
                    act.wait_ge(proj_done, m + 1)
                    act.activation(to[:, n, col:col + HALF], ps[:, m % 4, :], ACT.Copy,
                                   scale=C_DK ** -0.5 if c == 0 else 1.0).then_inc(proj_evac, 1)


def decay_stage(T, load_to):
    nc, t, f, ps = T.nc, T.t, T.f, T.ps
    lrT, w_g = f(LR, 2, HALF), f(WG, 2, HALF)
    z, u = f(GDEC, 2 * NT, HALF), f(HI, 2 * NT, HALF)
    b_g = f(HI + 8 * D, 2, HALF)
    with ExitStack() as ctx:
        g_landed, z_psum, z_ready, u_in, u_out, ln_out, step = T.sems(
            ctx, "gate_landed", "z_psum", "z_ready", "u_in", "u_out", "ln_out", "decay_step")
        with nc.Block() as block:
            @block.sync
            def _(sp):
                sp.dma_start(w_g[0:RANK], t["gla_w_gate"][0].rearrange("d r n -> r d n")).then_inc(g_landed, 16)
                sp.dma_start(b_g, t["gla_b_gate"][0].partition_broadcast(P)).then_inc(g_landed, 16)
                load_to(sp)
                sp.wait_ge(g_landed, 32)

            @block.tensor
            def _(pe):
                pe.wait_ge(g_landed, 32)
                for m in range(2 * NT):
                    d, n = m // NT, m % NT
                    if m >= 4:
                        pe.wait_ge(z_ready, m - 3)
                    pe.matmul(ps[:, m % 4, :], lrT[0:RANK, d, n * P:(n + 1) * P], w_g[0:RANK, d, :], start=True, stop=True).then_inc(z_psum, 1)

            @block.vector
            def _(dve):
                then = Steps(dve, step)
                dve.wait_ge(g_landed, 32)
                for m in range(2 * NT):
                    dve.wait_ge(z_psum, m + 1)
                    dve.tensor_tensor(z[:, m, :], ps[:, m % 4, :], b_g[:, m // NT, :], ALU.add).then_inc(z_ready, 1)
                    dve.wait_ge(z_ready, m + 1)
                    dve.scalar_tensor_tensor(u[:, m, :], z[:, m, :], -1.0, z[:, m, :], ALU.mult, ALU.min).then_inc(u_in, 1)
                for m in range(2 * NT):
                    dve.wait_ge(ln_out, m + 1)
                    dve.scalar_tensor_tensor(z[:, m, :], z[:, m, :], 0.0, u[:, m, :], ALU.min, ALU.subtract)

            @block.scalar
            def _(act):
                for m in range(2 * NT):
                    act.wait_ge(u_in, m + 1)
                    act.activation(u[:, m, :], u[:, m, :], ACT.Exp).then_inc(u_out, 1)
                for m in range(2 * NT):
                    act.wait_ge(u_out, m + 1)
                    act.activation(u[:, m, :], u[:, m, :], ACT.Ln, bias=1.0).then_inc(ln_out, 1)


SPARE = MOD + 8 * D
GO = SPARE
GSTATE = SPARE + 2 * D


def gla_stage(T, load_to):
    nc, t, f, ps = T.nc, T.t, T.f, T.ps
    q, k_, v = f(QR, XT, HALF), f(KR, NT, HALF), f(VR, NT, D)
    g = f(GDEC, 2, NT, HALF)
    ke = f(HI, 2, NT, HALF)
    c0 = HI + 8 * D
    tm, end_x, end_c, all16, low = f(c0, 2, 2, P), f(c0 + 4 * P, 2, P), f(c0 + 6 * P, 2, P), f(c0 + 8 * P, P), f(c0 + 9 * P, 2, CHUNK)
    wk = c0 + 10 * P
    ex = f(wk, 3, XT, P)
    qkm = f(wk + 3 * XT * P, 3, XT, P)
    qT, kT = f(LR, C_HEADS, XT * P), f(LR + C_HEADS * XT * P, C_HEADS, XT * P)
    aT = f(LR + 2 * C_HEADS * XT * P, 2, XT, P)
    state = f(GSTATE, 2, 4, C_DV)
    O = f(GO, XT, D)
    ident = f(KEEP + K_ID, P)
    NCH = SEQ // CHUNK
    units = [(h, d) for h in range(C_HEADS) for d in range(2)]
    order = {0: list(range(NCH)), 1: list(range(NCH - 1, -1, -1))}

    def product(d, c):
        if c is None:
            bank, half = (3, 1) if d == 0 else (2, 1)
        else:
            bank, half = 2 + c % 2, (0 if c in (order[d][0], order[d][1]) else 1)
        return ps[:, bank, half * C_DV:(half + 1) * C_DV]
    with ExitStack() as ctx:
        (tab_landed, turned, turn_evac, e_psum, e_exp, ke_ready, t_psum, t_exp, qk_ready, a_psum, a_ready,
         s_psum, s_ready, o_psum, o_ready, zeroed, step) = T.sems(
            ctx, *[f"g_{n}" for n in ("tab_landed", "turned", "turn_evac", "e_psum", "e_exp", "ke_ready", "t_psum",
                                      "t_exp", "qk_ready", "a_psum", "a_ready", "s_psum", "s_ready", "o_psum", "o_ready",
                                      "zeroed", "step")])
        with nc.Block() as block:
            @block.sync
            def _(sp):
                for to, name in ((tm.rearrange("p a b n -> p (a b n)"), "k_sums"), (end_x.rearrange("p a n -> p (a n)"), "k_ends"),
                                 (end_c.rearrange("p a n -> p (a n)"), "k_ends_ctx"), (all16, "k_all"),
                                 (low.rearrange("p a n -> p (a n)"), "k_low")):
                    sp.dma_start(to, t[name]).then_inc(tab_landed, 16)
                load_to(sp)
                sp.wait_ge(tab_landed, 80)

            @block.tensor
            def _(pe):
                pe.wait_ge(tab_landed, 80)
                for n, src in enumerate((q, k_)):
                    for m in range(XT * C_HEADS):
                        h, tile = m // XT, m % XT
                        ins = pe.transpose(ps[:, 2 * n + h // 2, (h % 2) * XT * P + tile * P:(h % 2) * XT * P + (tile + 1) * P],
                                           src[:, tile, h * P:(h + 1) * P], ident)
                    ins.then_inc(turned, 1)
                m = 0
                for d in range(2):
                    for tile in range(NT):
                        bank = 4 + m % 4
                        if m >= 4:
                            pe.wait_ge(e_exp, m - 3)
                        if tile < XT:
                            ins = pe.matmul(ps[:, bank, :], end_x[:, d, :], g[:, d, tile, :], start=True, stop=True)
                        else:
                            whole = (d == 0 and tile == XT) or (d == 1 and tile == NT - 1)
                            ins = pe.matmul(ps[:, bank, :], end_c[:, d, :], g[:, d, tile, :], start=True, stop=not whole)
                            if whole:
                                other = XT if d == 1 else NT - 1
                                ins = pe.matmul(ps[:, bank, :], all16, g[:, d, other, :], start=False, stop=True)
                        ins.then_inc(e_psum, 1)
                        m += 1

                def sums(n):
                    h, d = units[n]
                    pe.wait_ge(t_exp, n)
                    for tile in range(XT):
                        ins = pe.matmul(ps[:, 0, tile * 2 * P:(tile + 1) * 2 * P], g[:, d, tile, h * P:(h + 1) * P],
                                        tm[:, d].rearrange("p a n -> p (a n)"), start=True, stop=True)
                    ins.then_inc(t_psum, 1)

                def states(n):
                    h, d = units[n]
                    hv = slice(h * C_DV, (h + 1) * C_DV)
                    hk = slice(h * P, (h + 1) * P)
                    if n >= 1:
                        pe.wait_ge(s_ready, n)
                    for m, tile in enumerate(range(XT, NT)):
                        pe.matmul(product(d, None), ke[:, d, tile, hk], v[:, tile, hv], start=(m == 0), stop=(m == 1))
                    for m, c in enumerate(order[d][:-1]):
                        rows = slice((c % 2) * CHUNK, (c % 2 + 1) * CHUNK)
                        ins = pe.matmul(product(d, c), ke[rows, d, c // 2, hk],
                                        v[rows, c // 2, hv], start=True, stop=True)
                    ins.then_inc(s_psum, 1)

                def scores(n):
                    pe.wait_ge(qk_ready, n + 1)
                    if n >= 1:
                        pe.wait_ge(a_ready, n)
                    for tile in range(XT):
                        for c in range(2):
                            r = slice(c * CHUNK, (c + 1) * CHUNK)
                            ins = pe.matmul(ps[r, 1, tile * P:tile * P + CHUNK], qkm[:, 2, tile, r], qkm[:, 1, tile, r], start=True, stop=True)
                    ins.then_inc(a_psum, 1)

                def outputs(n):
                    h, d = units[n]
                    hv = slice(h * C_DV, (h + 1) * C_DV)
                    pe.wait_ge(a_ready, n + 1)
                    pe.wait_ge(s_ready, n + 1)
                    if d == 0 and h >= 2:
                        pe.wait_ge(o_ready, h - 1)
                    for tile in range(XT):
                        to = ps[:, 4 + 2 * (h % 2) + tile, 0:C_DV]
                        pe.matmul(to, aT[:, d, tile, :], v[:, tile, hv], start=(d == 0), stop=False, skip_group_check=True)
                        for c in range(2):
                            r = slice(c * CHUNK, (c + 1) * CHUNK)
                            ins = pe.matmul(ps[r, 4 + 2 * (h % 2) + tile, 0:C_DV], qkm[:, 0, tile, r], state[:, d, 2 * tile + c, :],
                                            start=False, stop=(d == 1), skip_group_check=True)
                    ins.then_inc(o_psum, 1)

                pe.wait_ge(turn_evac, 4)
                pe.wait_ge(e_exp, 8)
                pe.wait_ge(ke_ready, 8)
                for n in range(len(units)):
                    sums(n)
                    states(n)
                    scores(n)
                    outputs(n)

            @block.scalar
            def _(act):
                for n, to in enumerate((qT, kT)):
                    act.wait_ge(turned, n + 1)
                    for b in range(2):
                        act.activation(to[:, 2 * b:2 * b + 2, :], ps[:, 2 * n + b, :].rearrange("p (h n) -> p h n", n=XT * P),
                                       ACT.Copy).then_inc(turn_evac, 1)
                for m in range(2 * NT):
                    act.wait_ge(e_psum, m + 1)
                    act.activation(ke[:, m // NT, m % NT, :], ps[:, 4 + m % 4, :], ACT.Exp).then_inc(e_exp, 1)
                for n, (h, d) in enumerate(units):
                    act.wait_ge(t_psum, n + 1)
                    if n >= 1:
                        act.wait_ge(qk_ready, n)
                        act.wait_ge(s_ready, n)
                    bank = ps[:, 0, :].rearrange("p (t a n) -> p t a n", t=XT, a=2)
                    act.activation(ex[:, 0], bank[:, :, 0, :], ACT.Exp)
                    act.activation(ex[:, 1], bank[:, :, 1, :], ACT.Exp)
                    act.activation(ex[:, 2], bank[:, :, 1, :], ACT.Exp, scale=-1.0).then_inc(t_exp, 1)
                    if d == 1:
                        act.wait_ge(o_psum, n + 1)
                        for tile in range(XT):
                            ins = act.activation(O[:, tile, h * C_DV:(h + 1) * C_DV], ps[:, 4 + 2 * (h % 2) + tile, 0:C_DV], ACT.Copy)
                        ins.then_inc(o_ready, 1)

            @block.vector
            def _(dve):
                then = Steps(dve, step)
                dve.memset(aT, 0.0).then_inc(zeroed, 1)
                dve.wait_ge(zeroed, 1)
                dve.wait_ge(tab_landed, 80)
                for m in range(2 * NT):
                    dve.wait_ge(e_exp, m + 1)
                    to = ke[:, m // NT, m % NT, :]
                    dve.tensor_tensor(to, to, k_[:, m % NT, :], ALU.mult).then_inc(ke_ready, 1)
                dve.wait_ge(turn_evac, 4)
                for n, (h, d) in enumerate(units):
                    dve.wait_ge(t_exp, n + 1)
                    if n >= 1:
                        dve.wait_ge(o_psum, n)
                    qh, kh = (x[:, h, :].rearrange("p (t n) -> p t n", n=P) for x in (qT, kT))
                    dve.tensor_tensor(qkm[:, 0], qh, ex[:, 0], ALU.mult)
                    dve.tensor_tensor(qkm[:, 1], qh, ex[:, 1], ALU.mult)
                    dve.tensor_tensor(qkm[:, 2], kh, ex[:, 2], ALU.mult).then_inc(qk_ready, 1)
                    dve.wait_ge(s_psum, n + 1)
                    seq = order[d]
                    then(dve.tensor_copy(state[:, d, seq[0], :], product(d, None)))
                    for m, c in enumerate(seq[:-1]):
                        last = c % 2 * CHUNK + (CHUNK - 1 if d == 0 else 0)
                        ins = dve.scalar_tensor_tensor(state[:, d, seq[m + 1], :], state[:, d, c, :], ex[:, 0, c // 2, last:last + 1],
                                                       product(d, c), ALU.mult, ALU.add)
                        if m < NCH - 2:
                            then(ins)
                    ins.then_inc(s_ready, 1)
                    dve.wait_ge(a_psum, n + 1)
                    for c in range(2):
                        r = slice(c * CHUNK, (c + 1) * CHUNK)
                        ins = dve.copy_predicated(aT[r, d, :, r], bc(low[r, d, :], 1, (CHUNK, XT, CHUNK)).bitcast(U32),
                                                  ps[r, 1, 0:XT * P].rearrange("p (t n) -> p t n", n=P)[:, :, 0:CHUNK])
                    ins.then_inc(a_ready, 1)


def final_stage(T):
    nc, t, f = T.nc, T.t, T.f
    X, g_row, y = f(XR, NT, D), f(HI, D), f(HI + D, XT, D)
    ss, rstd = f(HI + 3 * D, XT), f(HI + 3 * D + XT, XT)
    with ExitStack() as ctx:
        g_landed, ss_ready, var_ready, std_ready, y_ready, stored, step = T.sems(
            ctx, *[f"f_{n}" for n in ("g_landed", "ss_ready", "var_ready", "std_ready", "y_ready", "stored", "step")])
        with nc.Block() as block:
            @block.sync
            def _(sp):
                sp.dma_start(g_row, t["final_g"].partition_broadcast(P)).then_inc(g_landed, 16)
                for n in range(XT):
                    sp.wait_ge(y_ready, n + 1)
                    sp.dma_start(T.out[0, n * P:(n + 1) * P, :], y[:, n, :]).then_inc(stored, 16)
                sp.wait_ge(g_landed, 16)
                sp.wait_ge(stored, 16 * XT)

            @block.scalar
            def _(act):
                for n in range(XT):
                    act.activation(y[:, n, :], X[:, n, :], ACT.Square, accum_out=ss[:, n:n + 1]).then_inc(ss_ready, 1)
                act.wait_ge(var_ready, 1)
                act.activation(rstd, ss, ACT.Sqrt).then_inc(std_ready, 1)

            @block.vector
            def _(dve):
                then = Steps(dve, step)
                dve.wait_ge(ss_ready, XT)
                dve.tensor_scalar(ss, ss, 1.0 / D, EPS, ALU.mult, ALU.add).then_inc(var_ready, 1)
                dve.wait_ge(std_ready, 1)
                then(dve.reciprocal(rstd, rstd))
                dve.wait_ge(g_landed, 16)
                for n in range(XT):
                    dve.scalar_tensor_tensor(y[:, n, :], X[:, n, :], rstd[:, n:n + 1], g_row, ALU.mult, ALU.mult).then_inc(y_ready, 1)


def hybrid_trunk(nc, t, out, stages=99, dump=None):
    with ExitStack() as ctx:
        T = Trunk(nc, ctx, t, out)
        f = T.f
        every, of_x = list(range(NT)), list(range(XT))
        none = lambda *a: None
        steps = [
            lambda: setup_stage(T),
            lambda: mod_stage(T),
            lambda: norm_stage(T, 0, 0, every, none, False),
            lambda: attn_project_stage(T),
            lambda: attention_stage(T),
            lambda: out_stage(T, 0, NT, f(ORow, NT, D), f(LO, KD, NT * P),
                              (f(HI + 8 * D, A_DV), f(HI + 9 * D, D), f(HI + 10 * D, 16), f(HI + 10 * D + 16, 16), None)),
            lambda: norm_stage(T, 0, 1, every, none, True),
            lambda: route_stage(T, 0, NT),
            lambda: moe_stage(T, 0, NT),
            lambda: overflow_stage(T, 0, NT),
            lambda: combine_stage(T, 0, NT, lambda sp: T.load_chunks(sp, ("in", 1, 2), {})),
            lambda: norm_stage(T, 1, 0, every, lambda sp: load_gate2(T, sp), False),
            lambda: gla_project_stage(T),
            lambda: decay_stage(T, none),
            lambda: gla_stage(T, none),
            lambda: out_stage(T, 1, XT, f(GO, XT, D), f(HI, KD, XT * P),
                              (f(HI + 8 * D, C_DV), f(HI + 9 * D, D), f(HI + 10 * D, 8), f(HI + 10 * D + 8, 8), f(GT, XT, D))),
            lambda: norm_stage(T, 1, 1, of_x, none, True),
            lambda: route_stage(T, 1, XT),
            lambda: moe_stage(T, 1, XT),
            lambda: overflow_stage(T, 1, XT),
            lambda: combine_stage(T, 1, XT, none),
            lambda: final_stage(T),
        ]
        for n, stage in enumerate(steps[:stages]):
            stage()
            if dump is not None:
                dump(n, T)


def shape_constants():
    c = {"k_ident": np.eye(P, dtype=np.float32), "k_ones": np.ones((P, P), np.float32)}
    p = np.arange(P)
    c["k_iota16"] = np.arange(NE, dtype=np.float32)[None]
    c["k_token"] = (p[:, None] + P * np.arange(NT)[None]).astype(np.float32)
    c["k_iota512"] = np.arange(NT * P, dtype=np.float32)[None]
    c["k_before"] = (p[:, None] < p[None]).astype(np.float32)
    j, pos = p % 32 % 16, np.arange(SEQ)
    inv = np.power(np.float32(10000.0), -(2 * j).astype(np.float32) / np.float32(32))
    at = np.where((p % 64 < 32)[:, None], (pos // GRID_W)[None], (pos % GRID_W)[None]).astype(np.float32)
    ang = (at * inv[:, None].astype(np.float32)).astype(np.float32)
    c["k_cos"], c["k_sin"] = np.cos(ang).astype(np.float32), np.sin(ang).astype(np.float32)
    rot = np.zeros((P, P), np.float32)
    for m in range(P):
        if m % 32 < 16:
            rot[m + 16, m] = -1.0
        else:
            rot[m - 16, m] = 1.0
    c["k_rope"] = rot
    col = np.arange(GRID_W)
    start = np.clip(col - NA_COLS // 2, 0, GRID_W - NA_COLS)
    seen = (col[None] >= start[:, None]) & (col[None] < start[:, None] + NA_COLS)
    c["k_namask"] = np.tile(np.where(seen, 0.0, MASKED), (SEQ // GRID_W, SEQ // GRID_W)).astype(np.float32)
    for i, nt in ((0, NT), (1, XT)):
        e, b = np.meshgrid(np.arange(NE), np.arange(1, nt), indexing="ij")
        c[f"k_over{i}"] = np.stack([b * P, e]).astype(np.float32)
    s, tt = p[:, None], p[None]
    same = s // CHUNK == tt // CHUNK
    w = np.float32(1.0 / TAU)
    sums, ends, ends_ctx, low = [], [], [], []
    for d in range(2):
        run = same & (s <= tt if d == 0 else s >= tt)
        mid = tt // CHUNK * CHUNK + (CHUNK // 2 - 1 if d == 0 else CHUNK // 2)
        to_mid = same & (s <= mid if d == 0 else s >= mid)
        sums += [run * w, (run.astype(np.float32) - to_mid.astype(np.float32)) * w]
        ends.append((same & (s > tt if d == 0 else s < tt)) * w)
        ends_ctx.append((s > tt if d == 0 else s < tt) * w)
        a, b = p[:, None] % CHUNK, np.arange(CHUNK)[None]
        low.append(a <= b if d == 0 else a >= b)
    cat = lambda xs: np.ascontiguousarray(np.concatenate(xs, 1).astype(np.float32))
    c["k_sums"], c["k_ends"], c["k_ends_ctx"], c["k_low"] = cat(sums), cat(ends), cat(ends_ctx), cat(low)
    c["k_all"] = np.full((P, P), w, np.float32)
    return c


def window_layout(na_bias):
    rows, pos = SEQ // GRID_W, np.arange(SEQ)
    dr = pos[None] // GRID_W - pos[:, None] // GRID_W + NA_ROWS - 1
    dc = pos[None] % GRID_W - pos[:, None] % GRID_W + NA_COLS - 1
    dc = np.clip(dc, 0, 2 * NA_COLS - 2)
    return np.ascontiguousarray(np.asarray(na_bias)[0][:, dr, dc])


_INS = ["x", "ctx", "w_mod", "b_mod", "norm_g", "final_g", "att_w_in", "att_w_out", "att_lambda", "att_subln_g",
        "gla_w_in", "gla_w_gate", "gla_b_gate", "gla_norm_g", "gla_w_out", "router_w", "router_bias",
        "moe_w1", "moe_w3", "moe_w2"]


def launch_arrays(inputs):
    a = {n: np.ascontiguousarray(inputs[n]) for n in _INS}
    a["final_g"] = a["final_g"].reshape(1, D)
    a["router_bias"] = a["router_bias"].reshape(1, NE)
    a["c_cols"] = np.ascontiguousarray(np.asarray(inputs["c"]).reshape(KD, P).T)
    a["c_ctx_cols"] = np.ascontiguousarray(np.asarray(inputs["c_ctx"]).reshape(KD, P).T)
    a["na_window"] = window_layout(inputs["na_bias"])
    a.update(shape_constants())
    return a


def kernel(**inputs):
    import concourse.bacc as _bacc
    from concourse.bass_utils import run_bass_kernel_spmd as _run

    nc = _bacc.Bacc("TRN2", target_bir_lowering=False, num_devices=1)
    arrays = launch_arrays(inputs)
    t = {n: nc.dram_tensor(n, a.shape, F32, kind="ExternalInput").ap() for n, a in arrays.items()}
    out = nc.dram_tensor("out_x", (1, SEQ, D), F32, kind="ExternalOutput").ap()
    hybrid_trunk(nc, t, out)
    r = _run(nc, [arrays], core_ids=[0])
    return r.results[0]["out_x"]
```

```python
import math
from contextlib import ExitStack

import numpy as np

import concourse.bass as bass
from concourse import mybir

F32 = mybir.dt.float32
F32R = mybir.dt.float32r
I32 = mybir.dt.int32
U32 = mybir.dt.uint32
ALU = mybir.AluOpType
ACT = mybir.ActivationFunctionType
AX = mybir.AxisListType

P = 128
D = 1024
KD = D // P
SEQ = 256
CTX = 256
XT = SEQ // P
NT = (SEQ + CTX) // P
EPS = 1e-6
GRID_W = 64
NA_ROWS, NA_COLS = 8, 16
A_HEADS, B_HEADS, DH, A_DV = 4, 8, 64, 128
LAM_INIT = 0.8 - 0.6 * math.exp(-0.3 * 0)
C_HEADS, C_DK, C_DV, RANK, TAU, CHUNK = 4, 128, 256, 16, 16.0, 64
NE, NG, EPG, DE = 16, 4, 4, 512
HALF = 512
BIG = 3.0e38
MASKED = -1.0e30

CH = KD * HALF
RING = 0
LO = 3 * CH
KEEP = 6 * CH
XR = KEEP + 512
GATE2 = XR + NT * D
SPLIT = GATE2 + 2 * D
MOD = SPLIT
K_ID, K_ONE, K_SILU, K_LAM, K_GATE, K_SLOT, K_ROWS = 0, 128, 256, 272, 280, 288, 296
K_OVIDX, K_OVEXP, K_NOV, K_CUR, K_IOTA, K_TOK, K_RBIAS = 360, 368, 376, 385, 386, 402, 406
HI = MOD + 10 * D
END = 53200
SH1, SC1, G1, SH2, SC2, G2 = range(6)
BIAS = END - 4 * HALF


class Steps:

    def __init__(self, engine, sem):
        self.engine, self.sem, self.n = engine, sem, 0

    def __call__(self, ins):
        self.n += 1
        ins.then_inc(self.sem, 1)
        self.engine.wait_ge(self.sem, self.n)

    def mark(self, ins):
        self.n += 1
        ins.then_inc(self.sem, 1)
        return self.n

    def until(self, n):
        self.engine.wait_ge(self.sem, n)


def bc(ap, axis, shape):
    return ap.unsqueeze(axis).to_broadcast(shape)


class Trunk:

    def __init__(self, nc, ctx, t, out):
        self.nc, self.t, self.out = nc, t, out
        base = -(-nc.sbuf_base // 32) * 32
        self.A = ctx.enter_context(nc.sbuf_tensor("arena", [P, SPLIT], F32))
        self.H = ctx.enter_context(nc.sbuf_tensor("arena_upper", [P, END - SPLIT], F32))
        self.R = nc.alloc_sbuf_tensor_at("arena_split", [P, END - SPLIT], F32R, offset=base + 4 * SPLIT)
        self.ps = ctx.enter_context(nc.psum_tensor("ps", [P, 8, HALF], F32))
        self.h2_dram = nc.dram_tensor("h2_rows", (NT * P, D), F32).ap()
        self.y_dram = nc.dram_tensor("expert_rows", ((NE + 2 * NT - 1) * P, D), F32).ap()
        self.route_landed = ctx.enter_context(nc.semaphore("route_landed"))
        self.x_landed = ctx.enter_context(nc.semaphore("x_landed"))
        self.mod_landed = ctx.enter_context(nc.semaphore("mod_landed"))
        self.mod_dram = nc.dram_tensor("mod_rows", (1, 40 * HALF), F32).ap()
        self.landed = [ctx.enter_context(nc.semaphore(f"chunk_landed{s}")) for s in range(3)]
        self.w_landed = {k: ctx.enter_context(nc.semaphore(f"{k}_landed")) for k in KINDS}
        self.w_base = {0: {k: 0 for k in KINDS}, 1: {"w1": 16 * (NE + 1), "w3": 16 * NE, "w2": 16 * (NE - 1)}}
        self.chunks, self.ids, landed = [], {}, [0] * 3
        for name, slot in CHUNKS:
            kind, i, j = name
            w = {"mod": t["w_mod"][i], "in": t[("att_w_in", "gla_w_in")[i]][0],
                 "out": t[("att_w_out", "gla_w_out")[i]][0]}[kind]
            landed[slot] += 32 if kind == "mod" else 16
            self.ids[name] = len(self.chunks)
            self.chunks.append((name, w[:, j * HALF:(j + 1) * HALF], slot, landed[slot]))
        self.loaded = 0
        self.cleared = []

    def f(self, at, *shape):
        n = int(np.prod(shape))
        assert at + n <= SPLIT or at >= SPLIT
        return self.shaped(self.A[:, at:at + n] if at < SPLIT else self.H[:, at - SPLIT:at - SPLIT + n], shape)

    def r(self, at, *shape):
        return self.shaped(self.R[:, at - SPLIT:at - SPLIT + int(np.prod(shape))], shape)

    def mod(self, v, row):
        return self.f(GATE2 + v * D if row == G2 else MOD + (2 * row + v) * D, D)

    @staticmethod
    def shaped(v, shape):
        if len(shape) == 1:
            return v
        names = "abcd"[:len(shape)]
        return v.rearrange(f"p ({' '.join(names)}) -> p {' '.join(names)}",
                           **{a: s for a, s in zip(names, shape)})

    def slot(self, s):
        return self.f(RING + s * CH, KD, HALF)

    def mod_half(self, v, j):
        return self.mod(v, j // 2)[:, j % 2 * HALF:(j % 2 + 1) * HALF]

    def sems(self, ctx, *names):
        sems = [self.nc.alloc_semaphore(n) for n in names]

        def retire():
            for s in sems:
                self.nc.gpsimd.sem_clear(s)
            for s in self.cleared:
                self.nc.release_semaphore(s)
            self.cleared = sems
        ctx.callback(retire)
        return sems

    def chunk(self, name):
        return self.slot(self.chunks[self.ids[name]][2])

    def bias(self, name):
        return self.f(BIAS + self.chunks[self.ids[name]][2] * HALF, HALF)

    def wait_chunk(self, engine, name):
        _, _, slot, landed = self.chunks[self.ids[name]]
        engine.wait_ge(self.landed[slot], landed)

    def load_chunks(self, sp, end, released):
        while self.loaded <= self.ids[end]:
            name, w, slot, _ = self.chunks[self.loaded]
            before = [n for n, _, s, _ in self.chunks[:self.loaded] if s == slot][-1:]
            if before and before[0] in released:
                for sem, value in released[before[0]]:
                    sp.wait_ge(sem, value)
            sp.dma_start(self.chunk(name), w.rearrange("(k p) n -> p k n", p=P)).then_inc(self.landed[slot], 16)
            if name[0] == "mod":
                _, i, j = name
                sp.dma_start(self.bias(name)[0:1], self.t["b_mod"][i:i + 1, j * HALF:(j + 1) * HALF])\
                  .then_inc(self.landed[slot], 16)
            self.loaded += 1


SUMS = [("mod", 0, j) for j in range(4, 12)] + [("mod", 1, j) for j in range(12)]
PROJECT_SUMS, ATTENTION_SUMS = SUMS[:11], SUMS[11:]
SUMS_BESIDE = ((0, 1), (2, 3), (4, 5), (6, 7), (8, 9), (10,))


def project_chunks():
    order = [(("mod", 0, 0), 1), (("mod", 0, 1), 2), (("mod", 0, 2), 0), (("mod", 0, 3), 1)]
    done = 0
    for c, sums in enumerate((1, 1, 2, 2, 2, 2)):
        order += [(SUMS[m], 2 - m % 2) for m in range(done, done + sums)] + [(("in", 0, c), 0)]
        done += sums
    return order + [(SUMS[10], 2)]


CHUNKS = project_chunks()
CHUNKS += [(SUMS[m], (m - 10) % 3) for m in range(11, 20)]
CHUNKS += [(("out", 0, 0), 1), (("out", 0, 1), 2)]
CHUNKS += [(("in", 1, j), j % 3) for j in range(6)] + [(("out", 1, j), j) for j in range(2)]


def sum_items(chunks):
    return [(m, name, v) for m, name in enumerate(chunks) for v in range(2)
            if v == 0 or name[1] == 0 or name[2] < 4]


def mod_row_at(name, v):
    return (name[2] + 12 * v + (16 if name[1] == 0 else 0)) * HALF


def setup_stage(T):
    nc, t, f = T.nc, T.t, T.f
    with ExitStack() as ctx:
        in_landed, silu_done, zeroed = T.sems(ctx, "setup_landed", "setup_silu", "bias_zeroed")
        with nc.Block() as block:
            @block.sync
            def _(sp):
                sp.dma_start(f(KEEP + K_ID, P), t["k_ident"]).then_inc(in_landed, 16)
                sp.dma_start(f(KEEP + K_ONE, P), t["k_ones"]).then_inc(in_landed, 16)
                sp.dma_start(f(KEEP + K_IOTA, NE), t["k_iota16"].partition_broadcast(P)).then_inc(in_landed, 16)
                sp.dma_start(f(KEEP + K_TOK, NT), t["k_token"]).then_inc(in_landed, 16)
                sp.dma_start(f(KEEP + K_RBIAS, NE), t["router_bias"].partition_broadcast(P)).then_inc(in_landed, 16)
                sp.dma_start(f(KEEP + K_SILU, 2, KD)[:, 0, :], t["c_cols"]).then_inc(in_landed, 16)
                sp.dma_start(f(KEEP + K_SILU, 2, KD)[:, 1, :], t["c_ctx_cols"]).then_inc(in_landed, 16)
                sp.wait_ge(zeroed, 1)
                T.load_chunks(sp, ("mod", 0, 2), {})
                sp.dma_start(f(XR, NT, D)[:, 0:XT, :], t["x"][0].rearrange("(t p) d -> p t d", p=P)).then_inc(T.x_landed, 16)
                sp.dma_start(f(XR, NT, D)[:, XT:NT, :], t["ctx"][0].rearrange("(t p) d -> p t d", p=P)).then_inc(T.x_landed, 16)
                sp.wait_ge(in_landed, 7 * 16)

            @block.gpsimd
            def _(pool):
                pool.memset(f(BIAS, 4 * HALF), 0.0).then_inc(zeroed, 1)

            @block.scalar
            def _(act):
                act.wait_ge(in_landed, 7 * 16)
                act.activation(f(KEEP + K_SILU, 2 * KD), f(KEEP + K_SILU, 2 * KD), ACT.Silu).then_inc(silu_done, 1)


def mod_stage(T):
    nc, t, f, ps = T.nc, T.t, T.f, T.ps
    spread, acc = f(LO, KD, P), f(LO + KD * P, 2, HALF)
    silu = f(KEEP + K_SILU, 2, KD)
    ones = f(KEEP + K_ONE, P)
    with ExitStack() as ctx:
        spread_ready, acc_ready, mod_psum, mod_done, step = T.sems(
            ctx, "spread_ready", "acc_ready", "mod_psum", "mod_done", "mod_step")
        with nc.Block() as block:
            @block.sync
            def _(sp):
                T.load_chunks(sp, ("in", 0, 0), {("mod", 0, j): [(mod_psum, j + 1)] for j in range(4)})

            @block.vector
            def _(dve):
                then = Steps(dve, step)
                for k in range(KD):
                    last = dve.tensor_scalar(spread[:, k, :], ones, silu[:, 1, k:k + 1], None, ALU.mult)
                last.then_inc(spread_ready, 1)
                for j in range(4):
                    name = ("mod", 0, j)
                    w = T.chunk(name)
                    T.wait_chunk(dve, name)
                    if j >= 2:
                        dve.wait_ge(mod_psum, j - 1)
                    for k in range(KD):
                        ins = dve.scalar_tensor_tensor(acc[:, j % 2, :], w[:, k, :], silu[:, 0, k:k + 1],
                                                       T.bias(name) if k == 0 else acc[:, j % 2, :], ALU.mult, ALU.add)
                        if k < KD - 1:
                            then(ins)
                    ins.then_inc(acc_ready, 1)

            @block.tensor
            def _(pe):
                pe.wait_ge(spread_ready, 1)
                for j in range(4):
                    name = ("mod", 0, j)
                    w = T.chunk(name)
                    T.wait_chunk(pe, name)
                    if j >= 2:
                        pe.wait_ge(mod_done, j - 1)
                    bank = 2 * (j % 2)
                    for k in range(KD):
                        pe.matmul(ps[:, bank + 1, :], spread[:, k, :], w[:, k, :], start=(k == 0), stop=False)
                    pe.matmul(ps[:, bank + 1, :], ones, T.bias(name), start=False, stop=True)
                    pe.wait_ge(acc_ready, j + 1)
                    pe.matmul(ps[:, bank, :], ones, acc[:, j % 2, :], start=True, stop=True).then_inc(mod_psum, 1)

            @block.scalar
            def _(act):
                for j in range(4):
                    bank = 2 * (j % 2)
                    act.wait_ge(mod_psum, j + 1)
                    act.activation(T.mod_half(0, j), ps[:, bank, :], ACT.Copy)
                    act.activation(T.mod_half(1, j), ps[:, bank + 1, :], ACT.Copy).then_inc(mod_done, 1)


def norm_stage(T, i, which, tiles, load_to, store_rows, split=False, load_last=None):
    nc, t, f, ps = T.nc, T.t, T.f, T.ps
    tag = f"n{i}{which}"
    X, hT = f(XR, NT, D), (T.r(HI, 2, KD, NT * P)[:, 0] if split else f(HI, KD, NT * P))
    hT_low = T.r(HI, 2, KD, NT * P)[:, 1] if split else None
    g_row, junk, h_row = f(LO, D), f(LO + D, NT, D), f(LO + 5 * D, 2, D)
    ss, rstd = f(HI + 9 * D, NT), f(HI + 9 * D + NT, NT)
    shift, scale = (SH1, SC1) if which == 0 else (SH2, SC2)
    ident = f(KEEP + K_ID, P)
    kinds = sorted({0 if n < XT else 1 for n in tiles})
    with ExitStack() as ctx:
        g_landed, ss_ready, var_ready, std_ready, h_ready, h_psum, h_high, h_evac, row_stored0, row_stored1, step = T.sems(
            ctx, *[f"{tag}_{n}" for n in ("g_landed", "ss_ready", "var_ready", "std_ready", "h_ready",
                                          "h_psum", "h_high", "h_evac", "row_stored0", "row_stored1", "step")])
        row_stored = (row_stored0, row_stored1)
        with nc.Block() as block:
            @block.sync
            def _(sp):
                sp.dma_start(g_row, t["norm_g"][i, which:which + 1, :].partition_broadcast(P)).then_inc(g_landed, 16)
                load_to(sp)
                if store_rows:
                    for n, tile in enumerate(tiles):
                        sp.wait_ge(h_ready, n + 1)
                        sp.dma_start(T.h2_dram[tile * P:(tile + 1) * P, :], h_row[:, n % 2, :]).then_inc(row_stored[n % 2], 16)
                    load_last(sp)
                    for s in row_stored:
                        sp.wait_ge(s, 16 * len(tiles) // 2)
                sp.wait_ge(g_landed, 16)

            @block.scalar
            def _(act):
                if i == 0 and which == 0:
                    act.wait_ge(T.x_landed, 32)
                for n, tile in enumerate(tiles):
                    act.activation(junk[:, n, :], X[:, tile, :], ACT.Square, accum_out=ss[:, n:n + 1]).then_inc(ss_ready, 1)
                act.wait_ge(var_ready, 1)
                act.activation(rstd[:, 0:len(tiles)], ss[:, 0:len(tiles)], ACT.Sqrt).then_inc(std_ready, 1)
                for n, tile in enumerate(tiles):
                    act.wait_ge(h_psum, n + 1)
                    for b in range(2):
                        ins = act.activation(hT[:, 4 * b:4 * b + 4, tile * P:(tile + 1) * P],
                                             ps[:, 2 * (n % 2) + b, :].rearrange("p (k n) -> p k n", n=P), ACT.Copy)
                    ins.then_inc(h_high if split else h_evac, 1)

            @block.vector
            def _(dve):
                then = Steps(dve, step)
                dve.wait_ge(g_landed, 16)
                if i == 1 and which == 0:
                    dve.wait_ge(T.mod_landed, 112)
                for v in kinds:
                    ins = dve.scalar_tensor_tensor(T.mod(v, scale), T.mod(v, scale), 1.0, g_row, ALU.add, ALU.mult)
                then(ins)
                dve.wait_ge(ss_ready, len(tiles))
                dve.tensor_scalar(ss[:, 0:len(tiles)], ss[:, 0:len(tiles)], 1.0 / D, EPS, ALU.mult, ALU.add).then_inc(var_ready, 1)
                dve.wait_ge(std_ready, 1)
                then(dve.reciprocal(rstd[:, 0:len(tiles)], rstd[:, 0:len(tiles)]))

                def low(n):
                    tile = tiles[n]
                    cols = slice(tile * P, (tile + 1) * P)
                    dve.wait_ge(h_high, n + 1)
                    for b in range(2):
                        ins = dve.tensor_tensor(hT_low[:, 4 * b:4 * b + 4, cols], ps[:, 2 * (n % 2) + b, :].rearrange("p (k n) -> p k n", n=P),
                                                hT[:, 4 * b:4 * b + 4, cols].bitcast(F32), ALU.subtract)
                    ins.then_inc(h_evac, 1)

                for n, tile in enumerate(tiles):
                    v = 0 if tile < XT else 1
                    if split and n >= 2:
                        low(n - 2)
                    if n >= 2:
                        dve.wait_ge(h_psum, n - 1)
                        if store_rows:
                            dve.wait_ge(row_stored[n % 2], 16 * (n // 2))
                    then(dve.scalar_tensor_tensor(h_row[:, n % 2, :], X[:, tile, :], rstd[:, n:n + 1],
                                                  T.mod(v, scale), ALU.mult, ALU.mult))
                    dve.tensor_tensor(h_row[:, n % 2, :], h_row[:, n % 2, :], T.mod(v, shift), ALU.add).then_inc(h_ready, 1)
                if split:
                    for n in range(len(tiles) - 2, len(tiles)):
                        low(n)

            @block.tensor
            def _(pe):
                for n, tile in enumerate(tiles):
                    pe.wait_ge(h_ready, n + 1)
                    if n >= 2:
                        pe.wait_ge(h_evac, n - 1)
                    for k in range(KD):
                        ins = pe.transpose(ps[:, 2 * (n % 2) + k // 4, (k % 4) * P:(k % 4 + 1) * P],
                                           h_row[:, n % 2, k * P:(k + 1) * P], ident)
                    ins.then_inc(h_psum, 1)


QKT, V0 = LO, LO + 16 * HALF


def attn_project_stage(T):
    nc, t, f, ps = T.nc, T.t, T.f, T.ps
    hT, w = T.r(HI, 2, KD, NT * P), T.r(MOD, 2, KD, HALF)
    qkT, v = f(QKT, 16, HALF), f(V0, NT, D)
    free = MOD + 8 * D
    rope_r, cos, sin = f(free, P), f(free + P, SEQ), f(free + P + SEQ, SEQ)
    free += P + 2 * SEQ
    tmp = f(free, 2, SEQ)
    lp, lq, ls = f(free + 512, 4, DH), f(free + 768, 2, DH), f(free + 896, 2)
    lam = f(KEEP + K_LAM, 4)
    acc, row = f(GATE2, 4, HALF), f(HI + 8 * D, 2, HALF)
    assert HI + 9 * D <= BIAS
    ones, silu = f(KEEP + K_ONE, P), f(KEEP + K_SILU, 2, KD)
    kinds = ["q", "q", "v", "q", "q", "v"]
    dest = [0, 4, 0, 8, 12, 1]
    items = sum_items(PROJECT_SUMS)
    total_at = {}
    for c, beside in enumerate(SUMS_BESIDE):
        for at, m in enumerate(beside):
            total_at[KD * c + (5, KD + 1)[at]] = [2 * m, 2 * m + 1]
    with ExitStack() as ctx:
        (tab_landed, w_high, w_low, w_used, proj_evac, rot_done, rope_done, lam_step, step, acc_ready,
         sum_psum, sum_kept, row_stored0, row_stored1) = T.sems(
            ctx, "tab_landed", "pw_high", "pw_low", "pw_used", "proj_evac", "rot_done", "rope_done", "lam_exp", "proj_step",
            "p_acc_ready", "p_sum_psum", "p_sum_kept", "p_row_stored0", "p_row_stored1")
        row_stored = (row_stored0, row_stored1)
        used = {("in", 0, j): [(w_low, KD * (j + 1))] for j in range(6)}
        for m, name in enumerate(PROJECT_SUMS):
            used[name] = [(acc_ready, 2 * m + 2)]

        with nc.Block() as block:
            @block.sync
            def _(sp):
                sp.dma_start(rope_r, t["k_rope"]).then_inc(tab_landed, 16)
                sp.dma_start(cos, t["k_cos"]).then_inc(tab_landed, 16)
                sp.dma_start(sin, t["k_sin"]).then_inc(tab_landed, 16)
                sp.dma_start(lp, t["att_lambda"].partition_broadcast(P)).then_inc(tab_landed, 16)
                T.load_chunks(sp, ATTENTION_SUMS[1], used)
                sp.wait_ge(tab_landed, 64)

            @block.tensor
            def _(pe):
                def rotate(n):
                    pe.wait_ge(proj_evac, n + 1)
                    if n >= 2:
                        pe.wait_ge(rope_done, n - 1)
                    pe.matmul(ps[:, 4 + n % 2, 0:SEQ], rope_r, qkT[:, n, 0:SEQ], start=True, stop=True).then_inc(rot_done, 1)

                def total(i):
                    pe.wait_ge(acc_ready, i + 1)
                    if i >= 2:
                        pe.wait_ge(sum_kept, i - 1)
                    pe.matmul(ps[:, 6 + i % 2, :], ones, acc[:, i % 4, :], start=True, stop=True).then_inc(sum_psum, 1)

                pe.wait_ge(tab_landed, 64)
                parts = ((0, 0), (1, 0), (0, 1))
                for c in range(6):
                    for k in range(KD):
                        pe.wait_ge(w_low, KD * c + k + 1)
                        for g in range(4):
                            if k == 0 and c >= 1:
                                pe.wait_ge(proj_evac, 4 * (c - 1) + g + 1)
                            for m, (a, b) in enumerate(parts):
                                w_part, h_part = w[:, a, k, :], hT[:, b, k, :]
                                if kinds[c] == "q":
                                    left, right = w_part[:, g * P:(g + 1) * P], h_part
                                else:
                                    left, right = h_part[:, g * P:(g + 1) * P], w_part
                                ins = pe.matmul(ps[:, g, :], left, right, start=(k == 0 and m == 0), stop=(k == KD - 1 and m == 2))
                        ins.then_inc(w_used, 1)
                        if c in (1, 2) and k % 2 == 1:
                            rotate(4 * (c - 1) + k // 2)
                        for i in total_at.get(KD * c + k, ()):
                            total(i)

            @block.scalar
            def _(act):
                def high(c, k):
                    if k == 0:
                        T.wait_chunk(act, ("in", 0, c))
                    if c >= 1:
                        act.wait_ge(w_used, KD * (c - 1) + k + 1)
                    act.activation(w[:, 0, k, :], T.chunk(("in", 0, c))[:, k, :], ACT.Copy).then_inc(w_high, 1)

                def keep(i):
                    _, name, v_ = items[i]
                    at = mod_row_at(name, v_)
                    act.wait_ge(sum_psum, i + 1)
                    if i >= 2:
                        act.wait_ge(row_stored[i % 2], 16 * (i // 2))
                    act.activation(row[0:1, i % 2, :], ps[0:1, 6 + i % 2, :], ACT.Copy).then_inc(sum_kept, 1)
                    act.wait_ge(sum_kept, i + 1)
                    act.dma_start(T.mod_dram[:, at:at + HALF], row[0:1, i % 2, :]).then_inc(row_stored[i % 2], 16)

                for k in range(KD):
                    high(0, k)
                for c in range(6):
                    for i in total_at.get(KD * c + 1, ()):
                        keep(i)
                    for k in range(KD):
                        if k == KD - 1:
                            act.wait_ge(w_used, KD * (c + 1))
                            for g in range(4):
                                to = qkT[:, dest[c] + g, :] if kinds[c] == "q" else v[:, g, dest[c] * HALF:(dest[c] + 1) * HALF]
                                act.activation(to, ps[:, g, :], ACT.Copy).then_inc(proj_evac, 1)
                        if c < 5:
                            high(c + 1, k)
                        for i in total_at.get(KD * c + k, ()) if k > 1 else ():
                            keep(i)
                for r in range(2):
                    act.wait_ge(row_stored[r], 16 * (len(items) // 2))
                act.wait_ge(lam_step, 1)
                act.activation(lam[:, 0:2], ls, ACT.Exp).then_inc(lam_step, 1)

            @block.gpsimd
            def _(pool):
                for c in range(6):
                    for k in range(KD):
                        pool.wait_ge(w_high, KD * c + k + 1)
                        pool.tensor_tensor(w[:, 1, k, :], T.chunk(("in", 0, c))[:, k, :], w[:, 0, k, :].bitcast(F32),
                                           ALU.subtract).then_inc(w_low, 1)

            @block.vector
            def _(dve):
                then = Steps(dve, step)

                def modulation(m):
                    name, landed = PROJECT_SUMS[m], {}
                    T.wait_chunk(dve, name)
                    if m >= 2:
                        dve.wait_ge(sum_psum, 2 * m - 2)
                    for k in range(KD):
                        for v_ in range(2):
                            to = acc[:, (2 * m + v_) % 4, :]
                            if k > 0:
                                then.until(landed[v_])
                            ins = dve.scalar_tensor_tensor(to, T.chunk(name)[:, k, :], silu[:, v_, k:k + 1],
                                                           T.bias(name) if k == 0 else to, ALU.mult, ALU.add)
                            if k < KD - 1:
                                landed[v_] = then.mark(ins)
                            else:
                                ins.then_inc(acc_ready, 1)

                def rope(n):
                    q = qkT[:, n, 0:SEQ]
                    dve.wait_ge(rot_done, n + 1)
                    dve.tensor_tensor(tmp[:, 0, :], ps[:, 4 + n % 2, 0:SEQ], sin, ALU.mult)
                    then(dve.tensor_tensor(tmp[:, 1, :], q, cos, ALU.mult))
                    dve.tensor_tensor(q, tmp[:, 1, :], tmp[:, 0, :], ALU.add).then_inc(rope_done, 1)
                    dve.wait_ge(rope_done, n + 1)

                dve.wait_ge(tab_landed, 64)
                lps = lp.rearrange("p (a b) n -> p a b n", b=2)
                then(dve.tensor_tensor(lq, lps[:, :, 0, :], lps[:, :, 1, :], ALU.mult))
                dve.tensor_reduce(ls, lq, AX.X, ALU.add).then_inc(lam_step, 1)
                for c in range(6):
                    for m in SUMS_BESIDE[c]:
                        modulation(m)
                        if c in (1, 2):
                            rope(4 * (c - 1) + 2 * (m % 2))
                            rope(4 * (c - 1) + 2 * (m % 2) + 1)
                dve.wait_ge(lam_step, 2)
                then(dve.tensor_tensor(lam[:, 2:3], lam[:, 1:2], lam[:, 0:1], ALU.subtract))
                then(dve.tensor_scalar(lam[:, 3:4], lam[:, 2:3], LAM_INIT, None, ALU.subtract))


ORow = HI


def attention_stage(T):
    nc, t, f, ps = T.nc, T.t, T.f, T.ps
    qkT, v, O = f(QKT, 16, HALF), f(V0, NT, D), f(ORow, NT, D)
    Pb = f(HI + 4 * D, 2, 2, HALF)
    aT = f(HI + 6 * D, 2, 2, HALF)
    bm = f(MOD + 2 * D, 2, 2, XT, SEQ)
    mask = f(HI + 8 * D, XT, SEQ)
    st = HI + 8 * D + 2 * SEQ
    NJ = 32
    acc, row = f(MOD, 2, HALF), f(MOD + 2 * HALF, 2, HALF)
    ones, silu = f(KEEP + K_ONE, P), f(KEEP + K_SILU, 2, KD)
    items = sum_items(ATTENTION_SUMS)
    pieces = [(i, k) for i in range(len(items)) for k in range(KD)]
    done = [min(2 * (j + 1) if j < 16 else 32 + 5 * (j - 15), len(pieces)) for j in range(NJ)]
    total_at = {}
    for i in range(len(items)):
        total_at.setdefault(min([j for j in range(NJ) if done[j] >= KD * (i + 1)][0] + 1, NJ - 1), []).append(i)
    mx, nm, sm, rs, cs = (f(st + k * 64, 64) for k in range(5))
    zero = f(st + 5 * 64, HALF)
    assert st + 5 * 64 + HALF <= BIAS
    neg_lam = f(KEEP + K_LAM, 4)[:, 3:4]
    ident = f(KEEP + K_ID, P)
    jobs = [("A", b, n) for b in range(4) for n in range(NT)] + [("B", b, n) for b in range(4) for n in range(NT)]

    def keys(n):
        return list(range(NT)) if n < XT else list(range(XT, NT))

    def turned(j):
        return j if j <= 16 else 16 + 2 * (j - 16)

    with ExitStack() as ctx:
        zero_ready, zeros_stored, bias_landed0, bias_landed1, mask_landed, bias_half, bias_ready, scored, shifted, exp_done, a_ready, a_turned, at_ready, av_done, o_done, step, acc_ready, sum_psum, sum_kept, row_stored0, row_stored1 = T.sems(
            ctx, "zero_ready", "zeros_stored", "bias_landed0", "bias_landed1", "mask_landed", "bias_half", "bias_ready", "scored", "shifted", "exp_done", "a_ready",
            "a_turned", "at_ready", "av_done", "o_done", "att_step",
            "a_acc_ready", "a_sum_psum", "a_sum_kept", "a_row_stored0", "a_row_stored1")
        row_stored = (row_stored0, row_stored1)
        used = {}
        for i, (_, name, _) in enumerate(items):
            used[name] = [(acc_ready, i + 1)]
        bias_landed = (bias_landed0, bias_landed1)
        with nc.Block() as block:
            @block.sync
            def _(sp):
                sp.dma_start(mask, t["k_namask"].rearrange("(t p) n -> p t n", p=P)).then_inc(mask_landed, 16)
                load_layer0_modulation(T, sp)
                for hp in range(4):
                    if hp == 2:
                        T.load_chunks(sp, ATTENTION_SUMS[6], used)
                    if hp >= 2:
                        sp.wait_ge(scored, 16 + 4 * (hp - 2) + 2)
                    for u in range(2):
                        sp.dma_start(bm[:, hp % 2, u], t["na_window"][2 * hp + u].rearrange("(t p) n -> p t n", p=P))\
                          .then_inc(bias_landed[hp % 2], 16)
                T.load_chunks(sp, ("out", 0, 1), used)
                sp.wait_ge(T.mod_landed, 64)
                for s in bias_landed:
                    sp.wait_ge(s, 4 * 16)
                sp.wait_ge(zero_ready, 1)
                for m in range(2 * NT - 1):
                    at = (NE + m) * P
                    sp.dma_start(T.y_dram[at:at + P, :].rearrange("p (b n) -> p b n", n=HALF), bc(zero, 1, (P, 2, HALF)))\
                      .then_inc(zeros_stored, 16)
                sp.wait_ge(zeros_stored, 16 * (2 * NT - 1))

            @block.gpsimd
            def _(pool):
                pool.memset(zero, 0.0).then_inc(zero_ready, 1)
                pool.wait_ge(mask_landed, 16)
                for hp in range(4):
                    pool.wait_ge(bias_landed[hp % 2], 32 * (hp // 2 + 1))
                    b = bm[:, hp % 2]
                    pool.tensor_scalar(b, b, float(DH) ** 0.5, None, ALU.mult).then_inc(bias_half, 1)
                    pool.wait_ge(bias_half, hp + 1)
                    pool.tensor_tensor(b, b, bc(mask, 1, (P, 2, XT, SEQ)), ALU.add).then_inc(bias_ready, 1)

            @block.tensor
            def _(pe):
                def scores(j):
                    kind, b, n = jobs[j]
                    ks = keys(n)
                    qb, kb = (b, 4 + b) if kind == "A" else (8 + b, 12 + b)
                    if j >= 2:
                        pe.wait_ge(exp_done, 2 * (j - 1))
                    if kind == "B" and n < XT:
                        pe.wait_ge(bias_ready, b + 1)
                    for u in range(2):
                        rows = slice(DH * u, DH * u + DH)
                        to = ps[:, 2 * (j % 2) + u, 0:P * len(ks)]
                        biased = kind == "B" and n < XT
                        ins = pe.matmul(to, qkT[rows, qb, n * P:(n + 1) * P], qkT[rows, kb, ks[0] * P:NT * P],
                                        start=True, stop=not biased)
                        if biased:
                            ins = pe.matmul(ps[:, 2 * (j % 2) + u, 0:SEQ], ident, bm[:, b % 2, u, n, :],
                                            start=False, stop=True)
                    ins.then_inc(scored, 1)

                def turn(j):
                    kind, b, n = jobs[j]
                    if kind == "A":
                        pe.wait_ge(a_ready, j + 1)
                    else:
                        pe.wait_ge(exp_done, 2 * (j + 1))
                    if j >= 1:
                        pe.wait_ge(at_ready, turned(j))
                    for u in range(1 if kind == "A" else 2):
                        for m in range(len(keys(n))):
                            ins = pe.transpose(ps[:, 4 + u, m * P:(m + 1) * P], Pb[:, j % 2, u, m * P:(m + 1) * P], ident)
                        ins.then_inc(a_turned, 1)

                def values(j):
                    kind, b, n = jobs[j]
                    ks = keys(n)
                    pe.wait_ge(at_ready, turned(j + 1))
                    if j >= 1:
                        pe.wait_ge(o_done, j)
                    for u in range(1 if kind == "A" else 2):
                        w = A_DV if kind == "A" else DH
                        col = b * A_DV if kind == "A" else HALF + (2 * b + u) * DH
                        for m, kt in enumerate(ks):
                            ins = pe.matmul(ps[:, 6, u * w:(u + 1) * w], aT[:, j % 2, u, m * P:(m + 1) * P],
                                            v[:, kt, col:col + w], start=(m == 0), stop=(m == len(ks) - 1))
                    ins.then_inc(av_done, 1)

                scores(0)
                scores(1)
                for j in range(NJ):
                    turn(j)
                    if j + 2 < NJ:
                        scores(j + 2)
                    values(j)
                    for i in total_at.get(j, ()):
                        pe.wait_ge(acc_ready, i + 1)
                        if i >= 1:
                            pe.wait_ge(sum_kept, i)
                        pe.matmul(ps[:, 7, :], ones, acc[:, i % 2, :], start=True, stop=True).then_inc(sum_psum, 1)

            @block.scalar
            def _(act):
                def turned_copy(j):
                    kind, b, n = jobs[j]
                    w = P * len(keys(n))
                    if j >= 2:
                        act.wait_ge(av_done, j - 1)
                    for u in range(1 if kind == "A" else 2):
                        act.wait_ge(a_turned, turned(j) + u + 1)
                        act.activation(aT[:, j % 2, u, 0:w], ps[:, 4 + u, 0:w], ACT.Copy).then_inc(at_ready, 1)

                def exponentials(j):
                    w = P * len(keys(jobs[j][2]))
                    if j >= 2:
                        act.wait_ge(a_turned, turned(j - 1))
                    act.wait_ge(shifted, j + 1)
                    for u in range(2):
                        act.activation(Pb[:, j % 2, u, 0:w], ps[:, 2 * (j % 2) + u, 0:w], ACT.Exp,
                                       bias=nm[:, 2 * j + u:2 * j + u + 1], scale=DH ** -0.5,
                                       accum_out=sm[:, 2 * j + u:2 * j + u + 1]).then_inc(exp_done, 1)

                exponentials(0)
                exponentials(1)
                for j in range(NJ):
                    turned_copy(j)
                    if j + 2 < NJ:
                        exponentials(j + 2)
                    for i in total_at.get(j, ()):
                        _, name, v_ = items[i]
                        at = mod_row_at(name, v_)
                        act.wait_ge(sum_psum, i + 1)
                        if i >= 2:
                            act.wait_ge(row_stored[i % 2], 16 * (i // 2))
                        act.activation(row[0:1, i % 2, :], ps[0:1, 7, :], ACT.Copy).then_inc(sum_kept, 1)
                        act.wait_ge(sum_kept, i + 1)
                        act.dma_start(T.mod_dram[:, at:at + HALF], row[0:1, i % 2, :]).then_inc(row_stored[i % 2], 16)
                for r in range(2):
                    act.wait_ge(row_stored[r], 16 * (len(items) // 2))

            @block.vector
            def _(dve):
                then = Steps(dve, step)

                def shift(j):
                    w = P * len(keys(jobs[j][2]))
                    c = slice(2 * j, 2 * j + 2)
                    dve.wait_ge(scored, j + 1)
                    then(dve.tensor_reduce(mx[:, c], ps[:, 2 * (j % 2):2 * (j % 2) + 2, 0:w], AX.X, ALU.max))
                    dve.tensor_scalar(nm[:, c], mx[:, c], -(DH ** -0.5), None, ALU.mult).then_inc(shifted, 1)

                def combine(j):
                    kind, b, n = jobs[j]
                    w = P * len(keys(n))
                    dve.wait_ge(exp_done, 2 * (j + 1))
                    then(dve.reciprocal(rs[:, 2 * j:2 * j + 2], sm[:, 2 * j:2 * j + 2]))
                    if kind == "A":
                        then(dve.tensor_scalar(cs[:, 2 * j:2 * j + 1], rs[:, 2 * j + 1:2 * j + 2], neg_lam, sm[:, 2 * j:2 * j + 1],
                                               ALU.mult, ALU.mult))
                        dve.scalar_tensor_tensor(Pb[:, j % 2, 0, 0:w], Pb[:, j % 2, 1, 0:w], cs[:, 2 * j:2 * j + 1],
                                                 Pb[:, j % 2, 0, 0:w], ALU.mult, ALU.add).then_inc(a_ready, 1)

                def keep(j):
                    kind, b, n = jobs[j]
                    dve.wait_ge(av_done, j + 1)
                    bank = ps[:, 6, :]
                    if kind == "A":
                        dve.tensor_scalar(O[:, n, b * A_DV:(b + 1) * A_DV], bank[:, 0:A_DV],
                                          rs[:, 2 * j:2 * j + 1], None, ALU.mult).then_inc(o_done, 1)
                    else:
                        for u in range(2):
                            c = HALF + (2 * b + u) * DH
                            ins = dve.tensor_scalar(O[:, n, c:c + DH], bank[:, u * DH:(u + 1) * DH],
                                                    rs[:, 2 * j + u:2 * j + u + 1], None, ALU.mult)
                        ins.then_inc(o_done, 1)

                def modulation(i, k):
                    _, name, v_ = items[i]
                    to = acc[:, i % 2, :]
                    if k == 0:
                        T.wait_chunk(dve, name)
                        if i >= 2:
                            dve.wait_ge(sum_psum, i - 1)
                    ins = dve.scalar_tensor_tensor(to, T.chunk(name)[:, k, :], silu[:, v_, k:k + 1],
                                                   T.bias(name) if k == 0 else to, ALU.mult, ALU.add)
                    if k < KD - 1:
                        then(ins)
                    else:
                        ins.then_inc(acc_ready, 1)

                shift(0)
                shift(1)
                combine(0)
                for j in range(NJ):
                    if j + 1 < NJ:
                        combine(j + 1)
                    if j >= 1:
                        keep(j - 1)
                    if j + 2 < NJ:
                        shift(j + 2)
                    for i, k in pieces[done[j - 1] if j >= 1 else 0:done[j]]:
                        modulation(i, k)
                keep(NJ - 1)


def out_stage(T, i, ntiles, O, oT, work):
    nc, t, f, ps = T.nc, T.t, T.f, T.ps
    X = f(XR, NT, D)
    ident = f(KEEP + K_ID, P)
    nh, dv = (A_HEADS, A_DV) if i == 0 else (C_HEADS, C_DV)
    wn = nh * dv
    sub_g, sq, ss, rstd, gate = work
    with ExitStack() as ctx:
        g_landed, var_ready, std_ready, o_ready, o_psum, o_evac, out_done, x_done, silu_done, step = T.sems(
            ctx, *[f"o{i}_{n}" for n in ("g_landed", "var_ready", "std_ready", "o_ready", "o_psum", "o_evac",
                                         "out_done", "x_done", "silu_done", "step")])
        groups = [(c, n) for c in range(2) for n in range(ntiles)]
        with nc.Block() as block:
            @block.sync
            def _(sp):
                g = t["att_subln_g"] if i == 0 else t["gla_norm_g"]
                sp.dma_start(sub_g, g.partition_broadcast(P)).then_inc(g_landed, 16)
                sp.wait_ge(g_landed, 16)

            @block.scalar
            def _(act):
                if i == 1:
                    act.activation(gate, gate, ACT.Silu).then_inc(silu_done, 1)
                act.wait_ge(var_ready, 1)
                act.activation(rstd, ss, ACT.Sqrt).then_inc(std_ready, 1)
                for n in range(ntiles):
                    act.wait_ge(o_psum, n + 1)
                    for b in range(2):
                        ins = act.activation(oT[:, 4 * b:4 * b + 4, n * P:(n + 1) * P],
                                             ps[:, 2 * (n % 2) + b, :].rearrange("p (k n) -> p k n", n=P), ACT.Copy)
                    ins.then_inc(o_evac, 1)

            @block.vector
            def _(dve):
                then = Steps(dve, step)
                dve.wait_ge(g_landed, 16)
                if i == 0:
                    then(dve.tensor_scalar(sub_g, sub_g, 1.0 - LAM_INIT, None, ALU.mult))
                for n in range(ntiles):
                    then(dve.tensor_tensor(sq[:, 0:wn], O[:, n, 0:wn], O[:, n, 0:wn], ALU.mult))
                    then(dve.tensor_reduce(ss[:, n * nh:(n + 1) * nh], sq[:, 0:wn].rearrange("p (h d) -> p h d", d=dv), AX.X, ALU.add))
                dve.tensor_scalar(ss, ss, 1.0 / dv, EPS, ALU.mult, ALU.add).then_inc(var_ready, 1)
                dve.wait_ge(std_ready, 1)
                then(dve.reciprocal(rstd, rstd))
                if i == 1:
                    dve.wait_ge(silu_done, 1)
                for n in range(ntiles):
                    for h in range(nh):
                        part = O[:, n, h * dv:(h + 1) * dv]
                        ins = dve.scalar_tensor_tensor(part, part, rstd[:, n * nh + h:n * nh + h + 1], sub_g, ALU.mult, ALU.mult)
                    if i == 1:
                        then(ins)
                        ins = dve.tensor_tensor(O[:, n, :], O[:, n, :], gate[:, n, :], ALU.mult)
                    ins.then_inc(o_ready, 1)
                for m, (c, n) in enumerate(groups):
                    cols = slice(c * HALF, (c + 1) * HALF)
                    dve.wait_ge(out_done, m + 1)
                    v = 0 if n < XT else 1
                    dve.tensor_tensor(sq[:, (m % 2) * HALF:(m % 2 + 1) * HALF], ps[:, 4 + m % 4, :], T.mod(v, G1)[:, cols], ALU.mult).then_inc(x_done, 1)
                    dve.wait_ge(x_done, m + 1)
                    then(dve.tensor_tensor(X[:, n, cols], X[:, n, cols], sq[:, (m % 2) * HALF:(m % 2 + 1) * HALF], ALU.add))

            @block.tensor
            def _(pe):
                for n in range(ntiles):
                    pe.wait_ge(o_ready, n + 1)
                    if n >= 2:
                        pe.wait_ge(o_evac, n - 1)
                    for k in range(KD):
                        ins = pe.transpose(ps[:, 2 * (n % 2) + k // 4, (k % 4) * P:(k % 4 + 1) * P],
                                           O[:, n, k * P:(k + 1) * P], ident)
                    ins.then_inc(o_psum, 1)
                for m, (c, n) in enumerate(groups):
                    w = T.chunk(("out", i, c))
                    if n == 0:
                        T.wait_chunk(pe, ("out", i, c))
                    if m < ntiles:
                        pe.wait_ge(o_evac, m + 1)
                    if m >= 4:
                        pe.wait_ge(x_done, m - 3)
                    for k in range(KD):
                        ins = pe.matmul(ps[:, 4 + m % 4, :], oT[:, k, n * P:(n + 1) * P], w[:, k, :], start=(k == 0), stop=(k == KD - 1))
                    ins.then_inc(out_done, 1)


def expert_weights(T, i, kind, e):
    w = T.t[f"moe_{kind}"][i]
    if isinstance(e, int):
        w = w[e:e + 1]
    else:
        w = w[bass.ds(e, 1)]
    return w.rearrange("o (k p) n -> p (o k) n", p=P)


KINDS = ("w1", "w3", "w2")
Q = 4 * HALF
PART = 3 * HALF


def expert_slot(T, kind):
    s = KINDS.index(kind)
    return T.slot(s) if kind != "w2" else T.f(RING + s * CH, DE // P, D)


def expert_raw(T, kind, e):
    s = 0 if kind == "w2" and isinstance(e, int) and e == NE - 1 else KINDS.index(kind)
    return T.slot(s).rearrange("p k n -> p (k n)")


def first_expert_loads(T, sp, i):
    for kind in KINDS:
        sp.dma_start(expert_slot(T, kind), expert_weights(T, i, kind, 0)).then_inc(T.w_landed[kind], 16)


def load_layer0_modulation(T, sp):
    rows, each = T.f(MOD, 5, 2, D), T.mod_dram.rearrange("a (r n) -> a r n", n=D)
    for v in range(2):
        at = 8 + 6 * v
        sp.dma_start(rows[:, 2:5, v, :], each[:, at + G1:at + G2, :].partition_broadcast(P)).then_inc(T.mod_landed, 16)
        sp.dma_start(T.mod(v, G2), each[:, at + G2, :].partition_broadcast(P)).then_inc(T.mod_landed, 16)


def load_modulation(T, sp):
    rows, each = T.f(MOD, 5, 2, D), T.mod_dram.rearrange("a (r n) -> a r n", n=D)
    sp.dma_start(rows[:, 0:2, 0, :], each[:, 0:2, :].partition_broadcast(P)).then_inc(T.mod_landed, 16)
    sp.dma_start(rows[:, 0:2, 1, :], each[:, 6:8, :].partition_broadcast(P)).then_inc(T.mod_landed, 16)


def load_late_modulation(T, sp):
    rows, each = T.f(MOD, 5, 2, D), T.mod_dram.rearrange("a (r n) -> a r n", n=D)
    sp.dma_start(rows[:, 2:5, 0, :], each[:, 2:5, :].partition_broadcast(P)).then_inc(T.mod_landed, 16)
    sp.wait_ge(T.mod_landed, 128)


def load_gate2(T, sp):
    sp.dma_start(T.mod(0, G2), T.mod_dram[:, G2 * D:6 * D].partition_broadcast(P)).then_inc(T.mod_landed, 16)


class RouteBuffers:
    def __init__(self, T, nt):
        f = T.f
        self.cap = cap = nt * P
        self.nb = nb = nt - 1
        self.nov = nov = 2 * nt - 1
        at = [LO + 7 * D]

        def take(*shape):
            v = f(at[0], *shape)
            at[0] += int(np.prod(shape))
            return v

        self.iota_cap = take(cap)
        self.sc, self.sel, self.ing, self.m1, self.m2, self.cand, self.oh0, self.oh1, self.rank = (take(nt, NE) for _ in range(9))
        self.pair = take(nt, NG, 6)
        self.gs, self.geq, self.gcand = (take(nt, NG) for _ in range(3))
        self.gmx, self.grp, self.mxv, self.e0, self.e1, self.w0, self.w1, self.r0, self.r1, self.wsum = (take(nt) for _ in range(10))
        self.cnt = take(NE)
        self.rows = take(nt, NE)
        self.ovf = take(NE, nb)
        self.ovp = take(2, 32 + NE * nb)
        self.ovs = take(nov, NE * nb)
        self.ovm = take(nov, NE * nb)
        self.ovr, self.ovk, self.ovl = take(2, nov), take(2, NE, nb), take(NE, nb)
        self.nov_f = take(1)
        self.ebase = take(NE)
        assert at[0] <= LO + 3 * CH
        self.pick = T.r(HI + 4 * D, 2 * nt, cap)
        self.rw, self.tri = f(HI + 8 * D, KD, NE), f(HI + 8 * D + KD * NE, P)
        at[0] = HI + 8 * D + KD * NE + P
        self.ohtok, self.chosen = T.r(at[0], 2 * nt, NE), T.r(at[0] + 2 * nt * NE, nt, NE)
        self.tri_r, self.ones_r = T.r(at[0] + 3 * nt * NE, P), T.r(at[0] + 3 * nt * NE + P, P)
        self.i16 = f(KEEP + K_IOTA, NE)
        self.tok = f(KEEP + K_TOK, NT)
        self.rbias = f(KEEP + K_RBIAS, NE)
        self.gate = f(KEEP + K_GATE, 2, NT)
        self.slot = f(KEEP + K_SLOT, 2, NT).bitcast(U32)
        self.rows_u = f(KEEP + K_ROWS, NT, NE).bitcast(U32)


def overflow_lists(T, dve, then, b, nt, part):
    f, nb, nov = T.f, b.nb, b.nov
    tt, ts, stt, red = dve.tensor_tensor, dve.tensor_scalar, dve.scalar_tensor_tensor, dve.tensor_reduce
    width = NE * nb
    ovflat = b.ovf.rearrange("p e b -> p (e b)")
    src = len([d for d in (1, 2, 4, 8, 16, 32) if d < width]) % 2
    if part == 0:
        then(tt(b.ovf, bc(b.cnt, 2, (P, NE, nb)), b.ovk[:, 0], ALU.is_gt))
        then(red(b.nov_f, ovflat, AX.X, ALU.add))
        then(dve.tensor_copy(f(KEEP + K_NOV, 1).bitcast(I32), b.nov_f))
        then(dve.memset(b.ovp, 0.0))
        then(dve.tensor_copy(b.ovp[:, 0, 32:32 + width], ovflat))
        at, d = 0, 1
        while d < width:
            then(tt(b.ovp[:, 1 - at, 32:32 + width], b.ovp[:, at, 32:32 + width], b.ovp[:, at, 32 - d:32 - d + width], ALU.add))
            at, d = 1 - at, 2 * d
        assert at == src
        run = b.ovp[:, src, 32:32 + width].rearrange("p (e b) -> p e b", b=nb)[:, :, 0]
        then(tt(b.ebase, run, b.ovf[:, :, 0], ALU.subtract))
        then(ts(b.ebase, b.ebase, float(P), float((NE - 1) * P), ALU.mult, ALU.add))
    if part == 1:
        for m, (oh, e, r) in enumerate(((b.oh0, b.e0, b.r0), (b.oh1, b.e1, b.r1))):
            then(tt(b.cand, oh, bc(b.ebase, 1, (P, nt, NE)), ALU.mult))
            then(red(b.mxv, b.cand, AX.X, ALU.add))
            then(stt(b.mxv, e, -float(P), b.mxv, ALU.mult, ALU.add))
            then(ts(b.wsum, r, float(P), None, ALU.is_ge))
            then(tt(b.mxv, b.mxv, b.wsum, ALU.mult))
            then(stt(b.mxv, e, float(P), b.mxv, ALU.mult, ALU.add))
            then(tt(b.mxv, b.mxv, r, ALU.add))
            then(dve.tensor_copy(b.slot[:, m, 0:nt], b.mxv))
    if part == 2:
        then(tt(b.ovs, bc(b.ovp[:, src, 32:32 + width], 1, (P, nov, width)),
                bc(b.iota_cap[:, 1:nov + 1], 2, (P, nov, width)), ALU.is_equal))
        then(tt(b.ovs, b.ovs, bc(ovflat, 1, (P, nov, width)), ALU.mult))
        then(tt(b.ovm, b.ovs, bc(b.ovk[:, 1].rearrange("p e b -> p (e b)"), 1, (P, nov, width)), ALU.mult))
        then(red(b.ovr[:, 1, :], b.ovm, AX.X, ALU.add))
        for m in range(nb):
            ins = dve.tensor_copy(b.ovl[:, :, m], b.rows[:, m + 1, :])
        then(ins)
        then(tt(b.ovm, b.ovs, bc(b.ovl.rearrange("p e b -> p (e b)"), 1, (P, nov, width)), ALU.mult))
        then(red(b.ovr[:, 0, :], b.ovm, AX.X, ALU.add))
        dve.tensor_copy(f(KEEP + K_OVIDX, nov).bitcast(U32), b.ovr[:, 0, :])
        then(dve.tensor_copy(f(KEEP + K_OVEXP, nov).bitcast(I32), b.ovr[:, 1, :]))


class ExpertSems:
    NAMES = ("w_high", "w_low", "w_low_pool", "matrix_done", "rows_turned", "rT_high", "rT_low",
             "act_done", "g_ready", "g_turned", "gT_high", "gT_low", "y_ready", "y_stored0", "y_stored1",
             "rows_landed0", "rows_landed1", "list_step")

    def __init__(self, T, ctx, i):
        (self.w_high, self.w_low, self.w_low_pool, self.matrix_done, self.rows_turned, self.rT_high, self.rT_low,
         self.act_done, self.g_ready, self.g_turned, self.gT_high, self.gT_low, self.y_ready, y_stored0, y_stored1,
         rows_landed0, rows_landed1, self.list_step) = T.sems(ctx, *[f"m{i}_{n}" for n in self.NAMES])
        self.y_stored, self.rows_landed = (y_stored0, y_stored1), (rows_landed0, rows_landed1)


def gather_rows(T, S, pool, e):
    B, b = ExpertBuffers(T), RouteBuffers(T, NT)
    pool.indirect_dma_start(B.rows[:, e % 2, :], None, T.h2_dram,
                            bass.IndirectOffsetOnAxis(ap=b.rows_u[:, 0, e:e + 1], axis=0)).then_inc(S.rows_landed[e % 2], 16)


def route_loads(T, sp, i, nt):
    b, t = RouteBuffers(T, nt), T.t
    for to, src in ((b.rw, t["router_w"].rearrange("(k p) e -> p k e", p=P)), (b.tri, t["k_before"]),
                    (b.iota_cap, t["k_iota512"][:, 0:b.cap].partition_broadcast(P)),
                    (b.ovk, t[f"k_over{i}"].partition_broadcast(P))):
        sp.dma_start(to, src).then_inc(T.route_landed, 16)


def route_stage(T, i, nt, S):
    nc, t, f, ps = T.nc, T.t, T.f, T.ps
    hT = f(HI, KD, NT * P)
    b = RouteBuffers(T, nt)
    cap, rows, rows_u = b.cap, b.rows, b.rows_u
    i16, gate = b.i16, b.gate
    S3 = (P, nt, NE)
    with ExitStack() as ctx:
        logits, sig, masks, ranks, picked, listed, rows_ready, step = T.sems(
            ctx, *[f"r{i}_{n}" for n in ("logits", "sigmoid", "masks", "ranks", "picked", "listed", "rows_ready", "step")])
        with nc.Block() as block:
            @block.sync
            def _(sp):
                sp.wait_ge(S.w_low, 2)
                sp.wait_ge(S.w_low_pool, 2)
                sp.dma_start(expert_slot(T, "w1"), expert_weights(T, i, "w1", 1)).then_inc(T.w_landed["w1"], 16)

            @block.gpsimd
            def _(pool):
                raw, w = expert_raw(T, "w1", 0), ExpertBuffers(T).w[:, 0]
                pool.wait_ge(S.w_high, 2)
                for h in range(2):
                    for at, done in ((slice(Q * h, Q * h + PART), S.w_low), (slice(Q * h + PART, Q * (h + 1)), S.w_low_pool)):
                        pool.tensor_tensor(w[:, 1, at], raw[:, at], w[:, 0, at].bitcast(F32), ALU.subtract).then_inc(done, 1)
                pool.wait_ge(rows_ready, 1)
                gather_rows(T, S, pool, 0)
                gather_rows(T, S, pool, 1)

            @block.tensor
            def _(pe):
                pe.wait_ge(T.route_landed, 64 * (i + 1))
                for n in range(nt):
                    for k in range(KD):
                        ins = pe.matmul(ps[:, 0, n * NE:(n + 1) * NE], hT[:, k, n * P:(n + 1) * P], b.rw[:, k, :],
                                        start=(k == 0), stop=(k == KD - 1))
                ins.then_inc(logits, 1)
                pe.wait_ge(masks, 1)
                for n in range(nt):
                    for m in range(n + 1):
                        pe.matmul(ps[:, 1, n * NE:(n + 1) * NE], b.ones_r if m < n else b.tri_r, b.chosen[:, m, :], start=(m == 0), stop=(m == n))
                for m in range(nt):
                    ins = pe.matmul(ps[:, 1, nt * NE:(nt + 1) * NE], b.ones_r, b.chosen[:, m, :], start=(m == 0), stop=(m == nt - 1))
                ins.then_inc(ranks, 1)
                pe.wait_ge(picked, 1)
                for c in range(nt):
                    for m in range(2 * nt):
                        ins = pe.matmul(ps[:, 2, c * NE:(c + 1) * NE], b.pick[:, m, c * P:(c + 1) * P], b.ohtok[:, m, :],
                                        start=(m == 0), stop=(m == 2 * nt - 1))
                ins.then_inc(listed, 1)

            @block.scalar
            def _(act):
                act.wait_ge(logits, 1)
                act.activation(b.sc, ps[:, 0, 0:nt * NE].rearrange("p (n e) -> p n e", e=NE), ACT.Sigmoid).then_inc(sig, 1)
                act.wait_ge(T.w_landed["w1"], 16 + T.w_base[i]["w1"])
                raw, w = expert_raw(T, "w1", 0), ExpertBuffers(T).w[:, 0]
                for h in range(2):
                    act.activation(w[:, 0, Q * h:Q * (h + 1)], raw[:, Q * h:Q * (h + 1)], ACT.Copy).then_inc(S.w_high, 1)

            @block.vector
            def _(dve):
                then = Steps(dve, step)
                tt, ts, stt, red = dve.tensor_tensor, dve.tensor_scalar, dve.scalar_tensor_tensor, dve.tensor_reduce
                sc, sel, ing, m1, m2, cand, oh0, oh1, rank = b.sc, b.sel, b.ing, b.m1, b.m2, b.cand, b.oh0, b.oh1, b.rank
                pair, gs, geq, gc, gmx, grp, mxv = b.pair, b.gs, b.geq, b.gcand, b.gmx, b.grp, b.mxv
                e0, e1, w0, w1, r0, r1, wsum = b.e0, b.e1, b.w0, b.w1, b.r0, b.r1, b.wsum
                rbias, tok, ohtok, cnt, pick, iota_cap = b.rbias, b.tok, b.ohtok, b.cnt, b.pick, b.iota_cap
                dve.wait_ge(T.route_landed, 64 * (i + 1))
                dve.tensor_copy(b.tri_r, b.tri)
                dve.tensor_copy(b.ones_r, f(KEEP + K_ONE, P))
                dve.wait_ge(sig, 1)
                then(tt(sel, sc, bc(rbias, 1, S3), ALU.add))
                s4 = sel.rearrange("p n (g e) -> p n g e", e=EPG)
                tt(pair[:, :, :, 0:3], s4[:, :, :, 0:3], s4[:, :, :, 1:4], ALU.add)
                tt(pair[:, :, :, 3:5], s4[:, :, :, 0:2], s4[:, :, :, 2:4], ALU.add)
                then(tt(pair[:, :, :, 5:6], s4[:, :, :, 0:1], s4[:, :, :, 3:4], ALU.add))
                then(red(gs, pair, AX.X, ALU.max))
                then(red(gmx, gs, AX.X, ALU.max))
                then(tt(geq, gs, bc(gmx, 2, (P, nt, NG)), ALU.is_equal))
                then(ts(geq, geq, -64.0, 64.0, ALU.mult, ALU.add))
                then(tt(gc, geq, bc(i16[:, 0:NG], 1, (P, nt, NG)), ALU.add))
                then(red(grp, gc, AX.X, ALU.min))
                then(tt(geq, bc(i16[:, 0:NG], 1, (P, nt, NG)), bc(grp, 2, (P, nt, NG)), ALU.is_equal))
                then(dve.tensor_copy(ing.rearrange("p n (g e) -> p n g e", e=EPG), bc(geq, 3, (P, nt, NG, EPG))))
                then(ts(m2, ing, 1.0, BIG, ALU.subtract, ALU.mult))
                then(tt(m1, sel, ing, ALU.mult))
                then(tt(m1, m1, m2, ALU.add))
                for oh, e in ((oh0, e0), (oh1, e1)):
                    then(red(mxv, m1, AX.X, ALU.max))
                    then(tt(cand, m1, bc(mxv, 2, S3), ALU.is_equal))
                    then(ts(cand, cand, -64.0, 64.0, ALU.mult, ALU.add))
                    then(tt(cand, cand, bc(i16, 1, S3), ALU.add))
                    then(red(e, cand, AX.X, ALU.min))
                    then(tt(oh, bc(i16, 1, S3), bc(e, 2, S3), ALU.is_equal))
                    if oh is oh0:
                        then(stt(m1, oh, -BIG, m1, ALU.mult, ALU.add))
                dve.tensor_tensor(b.chosen, oh0, oh1, ALU.add).then_inc(masks, 1)
                for oh, w in ((oh0, w0), (oh1, w1)):
                    then(tt(cand, sc, oh, ALU.mult))
                    then(red(w, cand, AX.X, ALU.add))
                then(tt(wsum, w0, w1, ALU.add))
                then(dve.reciprocal(wsum, wsum))
                tt(gate[:, 0, 0:nt], w0, wsum, ALU.mult)
                tt(gate[:, 1, 0:nt], w1, wsum, ALU.mult)
                for m, oh in enumerate((oh0, oh1)):
                    ins = tt(ohtok[:, m * nt:(m + 1) * nt, :], oh, bc(tok[:, 0:nt], 2, S3), ALU.mult)
                then(ins)
                dve.wait_ge(ranks, 1)
                dve.tensor_copy(cnt, ps[:, 1, nt * NE:(nt + 1) * NE])
                then(dve.tensor_copy(rank, ps[:, 1, 0:nt * NE].rearrange("p (n e) -> p n e", e=NE)))
                for m, (oh, e, r) in enumerate(((oh0, e0, r0), (oh1, e1, r1))):
                    then(tt(cand, rank, oh, ALU.mult))
                    then(red(r, cand, AX.X, ALU.add))
                    for n in range(nt):
                        ins = ts(pick[:, m * nt + n, :], iota_cap, r[:, n:n + 1], None, ALU.is_equal)
                ins.then_inc(picked, 1)
                dve.wait_ge(listed, 1)
                then(dve.tensor_copy(rows, ps[:, 2, 0:nt * NE].rearrange("p (b e) -> p b e", e=NE)))
                dve.tensor_copy(rows_u[:, 0:nt, :], rows).then_inc(rows_ready, 1)


class ExpertBuffers:
    def __init__(self, T):
        f, r = T.f, T.r
        self.rows = f(LO, 2, D)
        self.s = f(LO + 2 * D, DE)
        self.g = f(LO + 2 * D + DE, DE)
        self.y = f(LO + 3 * D, 2, D)
        self.rT = f(LO + 5 * D, KD, P)
        self.gT = f(LO + 6 * D, DE // P, P)
        self.w = r(SPLIT, 2, 2, KD * HALF)
        at = SPLIT + 4 * CH
        self.rT2 = r(at, 2, KD * P)
        self.gT2 = r(at + 2 * D, 2, DE)
        assert at + 3 * D <= END


def nth(kind, e):
    if isinstance(e, int) and e == 0 and kind != "w2":
        return KINDS.index(kind)
    if isinstance(e, int) and e == NE - 1 and kind == "w2":
        return 3 * NE - 1
    return e * 3 + {"w1": -1, "w3": 0, "w2": 4}[kind]


def moe_stage(T, i, nt, S):
    nc, t, f, ps = T.nc, T.t, T.f, T.ps
    B = ExpertBuffers(T)
    ident = f(KEEP + K_ID, P)
    base = T.w_base[i]

    def buffer(kind, like):
        return nth(kind, like) % 2

    w_high, w_low, w_low_pool, matrix_done, rows_turned = S.w_high, S.w_low, S.w_low_pool, S.matrix_done, S.rows_turned
    rT_high, rT_low, act_done, g_ready, g_turned, gT_high, gT_low = S.rT_high, S.rT_low, S.act_done, S.g_ready, S.g_turned, S.gT_high, S.gT_low
    y_ready, y_stored, rows_landed = S.y_ready, S.y_stored, S.rows_landed
    with nc.Block() as block:
        @block.gpsimd
        def _(pool):
            def gather(e):
                pool.wait_ge(rows_turned, e - 1)
                gather_rows(T, S, pool, e)

            def low(kind, e):
                raw, n = expert_raw(T, kind, e), nth(kind, e)
                w = B.w[:, n % 2]
                for h in range(2):
                    at = slice(Q * h + PART, Q * (h + 1))
                    pool.wait_ge(w_high, 2 * n + h + 1)
                    pool.tensor_tensor(w[:, 1, at], raw[:, at], w[:, 0, at].bitcast(F32), ALU.subtract).then_inc(w_low_pool, 1)

            for e in range(NE):
                low("w3", e)
                if e >= 1:
                    low("w2", e - 1)
                if e + 1 < NE:
                    low("w1", e + 1)
                if e + 2 < NE:
                    gather(e + 2)
            low("w2", NE - 1)

        @block.sync
        def _(sp):
            def load(kind, e):
                n = nth(kind, e - 1)
                sp.wait_ge(w_low, n * 2 + 2)
                sp.wait_ge(w_low_pool, n * 2 + 2)
                sp.dma_start(expert_slot(T, kind), expert_weights(T, i, kind, e)).then_inc(T.w_landed[kind], 16)

            load("w3", 1)
            with sp.Fori(0, NE - 2) as n:
                load("w1", n + 2)
                load("w3", n + 2)
                load("w2", n + 1)
            sp.wait_ge(w_low, nth("w1", NE - 1) * 2 + 2)
            sp.wait_ge(w_low_pool, nth("w1", NE - 1) * 2 + 2)
            sp.dma_start(expert_raw(T, "w2", NE - 1).rearrange("p (k n) -> p k n", n=D), expert_weights(T, i, "w2", NE - 1))\
              .then_inc(T.w_landed["w1"], 16)

        @block.tensor
        def _(pe):
            def passes(kind, e, like, tokens, steps):
                n, w = nth(kind, e), B.w[:, buffer(kind, like)]
                pe.wait_ge(w_high, n * 2 + 2)
                for part in (0, 1):
                    for k, piece, bank in steps:
                        pe.matmul(ps[:, bank, :], tokens[:, part, k * P:(k + 1) * P], w[:, 0, piece * HALF:(piece + 1) * HALF],
                                  start=(part == 0 and k == 0), stop=False)
                pe.wait_ge(w_low, n * 2 + 2)
                pe.wait_ge(w_low_pool, n * 2 + 2)
                last = max(k for k, _, _ in steps)
                for k, piece, bank in steps:
                    ins = pe.matmul(ps[:, bank, :], tokens[:, 0, k * P:(k + 1) * P], w[:, 1, piece * HALF:(piece + 1) * HALF],
                                    start=False, stop=(k == last))
                ins.then_inc(matrix_done, 1)

            def up(e, like):
                pe.wait_ge(rT_low, e + 1)
                if not isinstance(e, int) or e >= 1:
                    pe.wait_ge(act_done, e)
                passes("w1", e, like, B.rT2, [(k, k, 0) for k in range(KD)])

            def linear(e, like):
                if not isinstance(e, int) or e >= 1:
                    pe.wait_ge(g_ready, e)
                passes("w3", e, like, B.rT2, [(k, k, 1) for k in range(KD)])

            def turn_rows(e, s, m):
                pe.wait_ge(rows_landed[s], (m + 1) * 16)
                if not isinstance(e, int) or e >= 1:
                    pe.wait_ge(rT_low, e)
                for k in range(KD):
                    ins = pe.transpose(ps[:, 2 + k // 4, (k % 4) * P:(k % 4 + 1) * P], B.rows[:, s, k * P:(k + 1) * P], ident)
                ins.then_inc(rows_turned, 1)

            def turn_hidden(e):
                pe.wait_ge(g_ready, e + 1)
                if not isinstance(e, int) or e >= 1:
                    pe.wait_ge(gT_low, e)
                for k in range(DE // P):
                    ins = pe.transpose(ps[:, 4, k * P:(k + 1) * P], B.g[:, k * P:(k + 1) * P], ident)
                ins.then_inc(g_turned, 1)

            def down(e, like):
                pe.wait_ge(gT_low, e + 1)
                if not isinstance(e, int) or e >= 1:
                    pe.wait_ge(y_ready, e * 2)
                passes("w2", e, like, B.gT2, [(k, 2 * k + h, 5 + h) for h in range(2) for k in range(DE // P)])

            turn_rows(0, 0, 0)
            up(0, 0)
            linear(0, 0)
            turn_rows(1, 1, 0)
            for e in (1, 2):
                up(e, e)
                turn_hidden(e - 1)
                linear(e, e)
                turn_rows(e + 1, (e + 1) % 2, (e + 1) // 2)
                down(e - 1, e - 1)
            with pe.Fori(0, (NE - 4) // 2) as n:
                for s in range(2):
                    e = n * 2 + (3 + s)
                    up(e, 3 + s)
                    turn_hidden(e - 1)
                    linear(e, 3 + s)
                    turn_rows(e + 1, s, n + 2)
                    down(e - 1, 2 + s)
            e = NE - 1
            up(e, e)
            turn_hidden(e - 1)
            linear(e, e)
            down(e - 1, e - 1)
            turn_hidden(e)
            down(e, e)

        @block.scalar
        def _(act):
            def high(kind, e, like):
                n = nth(kind, e)
                raw, w = expert_raw(T, kind, e), B.w[:, buffer(kind, like)]
                if kind == "w2" and isinstance(e, int) and e == NE - 1:
                    act.wait_ge(T.w_landed["w1"], (NE + 1) * 16 + base["w1"])
                else:
                    act.wait_ge(T.w_landed[kind], e * 16 + (16 + base[kind]))
                if not isinstance(n, int) or n >= 2:
                    act.wait_ge(matrix_done, n - 1)
                for h in range(2):
                    act.activation(w[:, 0, Q * h:Q * (h + 1)], raw[:, Q * h:Q * (h + 1)], ACT.Copy).then_inc(w_high, 1)

            def silu(e):
                act.wait_ge(matrix_done, nth("w1", e) + 1)
                if not isinstance(e, int) or e >= 1:
                    act.wait_ge(g_ready, e)
                act.activation(B.s, ps[:, 0, :], ACT.Silu).then_inc(act_done, 1)

            def split_rT(e):
                act.wait_ge(rows_turned, e + 1)
                act.activation(B.rT2[:, 0, :], ps[:, 2:4, :].rearrange("p b n -> p (b n)"), ACT.Copy).then_inc(rT_high, 1)

            def split_gT(e):
                act.wait_ge(g_turned, e + 1)
                if not isinstance(e, int) or e >= 1:
                    act.wait_ge(matrix_done, nth("w2", e - 1) + 1)
                act.activation(B.gT2[:, 0, :], ps[:, 4, :], ACT.Copy).then_inc(gT_high, 1)

            def copy_y(e, s, m):
                act.wait_ge(matrix_done, nth("w2", e) + 1)
                if not isinstance(m, int) or m >= 1:
                    act.wait_ge(y_stored[s], m * 16)
                act.activation(B.y[:, s, 0:HALF], ps[:, 5, :], ACT.Copy).then_inc(y_ready, 1)
                act.wait_ge(y_ready, (e + 1) * 2)
                to = T.y_dram[e * P:(e + 1) * P, :] if isinstance(e, int) else T.y_dram[bass.ds(e * P, P), :]
                act.dma_start(to, B.y[:, s, :]).then_inc(y_stored[s], 16)

            split_rT(0)
            for e in (0, 1, 2):
                high("w3", e, e)
                if e >= 2:
                    copy_y(e - 2, 0, 0)
                silu(e)
                if e >= 1:
                    split_gT(e - 1)
                    high("w2", e - 1, e - 1)
                high("w1", e + 1, e + 1)
                split_rT(e + 1)
            high("w3", 3, 3)
            copy_y(1, 1, 0)
            silu(3)
            split_gT(2)
            high("w2", 2, 2)
            high("w1", 4, 4)
            split_rT(4)
            with act.Fori(0, (NE - 6) // 2) as n:
                for s in range(2):
                    e = n * 2 + (4 + s)
                    high("w3", e, 4 + s)
                    copy_y(e - 2, s, n + 1)
                    silu(e)
                    split_gT(e - 1)
                    high("w2", e - 1, 3 + s)
                    high("w1", e + 1, 5 + s)
                    split_rT(e + 1)
            for e in (NE - 2, NE - 1):
                high("w3", e, e)
                copy_y(e - 2, e % 2, (e - 2) // 2)
                silu(e)
                split_gT(e - 1)
                high("w2", e - 1, e - 1)
                if e + 1 < NE:
                    high("w1", e + 1, e + 1)
                    split_rT(e + 1)
            high("w2", NE - 1, NE - 1)
            copy_y(NE - 2, 0, NE // 2 - 1)
            split_gT(NE - 1)
            copy_y(NE - 1, 1, NE // 2 - 1)
            for stored in y_stored:
                act.wait_ge(stored, NE // 2 * 16)

        @block.vector
        def _(dve):
            def low(kind, e, like):
                n = nth(kind, e)
                raw, w = expert_raw(T, kind, e), B.w[:, buffer(kind, like)]
                for h in range(2):
                    at = slice(Q * h, Q * h + PART)
                    dve.wait_ge(w_high, n * 2 + (h + 1))
                    dve.tensor_tensor(w[:, 1, at], raw[:, at], w[:, 0, at].bitcast(F32), ALU.subtract).then_inc(w_low, 1)

            def split_rT(e):
                dve.wait_ge(rT_high, e + 1)
                dve.tensor_tensor(B.rT2[:, 1, :], ps[:, 2:4, :].rearrange("p b n -> p (b n)"),
                                  B.rT2[:, 0, :].bitcast(F32), ALU.subtract).then_inc(rT_low, 1)

            def split_gT(e):
                dve.wait_ge(gT_high, e + 1)
                dve.tensor_tensor(B.gT2[:, 1, :], ps[:, 4, :], B.gT2[:, 0, :].bitcast(F32), ALU.subtract).then_inc(gT_low, 1)

            def product(e):
                dve.wait_ge(act_done, e + 1)
                dve.wait_ge(matrix_done, nth("w3", e) + 1)
                if not isinstance(e, int) or e >= 1:
                    dve.wait_ge(g_turned, e)
                dve.tensor_tensor(B.g, ps[:, 1, :], B.s, ALU.mult).then_inc(g_ready, 1)

            def copy_y(e, s, m):
                dve.wait_ge(matrix_done, nth("w2", e) + 1)
                if not isinstance(m, int) or m >= 1:
                    dve.wait_ge(y_stored[s], m * 16)
                dve.tensor_copy(B.y[:, s, HALF:D], ps[:, 6, :]).then_inc(y_ready, 1)

            then, b = Steps(dve, S.list_step), RouteBuffers(T, nt)
            split_rT(0)
            for e in (0, 1, 2):
                low("w3", e, e)
                if e >= 2:
                    copy_y(e - 2, 0, 0)
                if e >= 1:
                    split_gT(e - 1)
                    low("w2", e - 1, e - 1)
                product(e)
                low("w1", e + 1, e + 1)
                split_rT(e + 1)
                overflow_lists(T, dve, then, b, nt, e)
            low("w3", 3, 3)
            copy_y(1, 1, 0)
            split_gT(2)
            low("w2", 2, 2)
            product(3)
            low("w1", 4, 4)
            split_rT(4)
            with dve.Fori(0, (NE - 6) // 2) as n:
                for s in range(2):
                    e = n * 2 + (4 + s)
                    low("w3", e, 4 + s)
                    copy_y(e - 2, s, n + 1)
                    split_gT(e - 1)
                    low("w2", e - 1, 3 + s)
                    product(e)
                    low("w1", e + 1, 5 + s)
                    split_rT(e + 1)
            for e in (NE - 2, NE - 1):
                low("w3", e, e)
                copy_y(e - 2, e % 2, (e - 2) // 2)
                split_gT(e - 1)
                low("w2", e - 1, e - 1)
                product(e)
                if e + 1 < NE:
                    low("w1", e + 1, e + 1)
                    split_rT(e + 1)
            low("w2", NE - 1, NE - 1)
            copy_y(NE - 2, 0, NE // 2 - 1)
            split_gT(NE - 1)
            copy_y(NE - 1, 1, NE // 2 - 1)


def experts(T, i, nt):
    with ExitStack() as ctx:
        S = ExpertSems(T, ctx, i)
        route_stage(T, i, nt, S)
        moe_stage(T, i, nt, S)


def overflow_stage(T, i, nt):
    nc, t, f, ps = T.nc, T.t, T.f, T.ps
    B = ExpertBuffers(T)
    nov = 2 * nt - 1
    ident = f(KEEP + K_ID, P)
    count = f(KEEP + K_NOV, 1).bitcast(I32)[0:1, :]
    ov_idx = f(KEEP + K_OVIDX, nov).bitcast(U32)
    ov_exp = f(KEEP + K_OVEXP, nov).bitcast(I32)
    cur = f(KEEP + K_CUR, 1).bitcast(U32)
    with ExitStack() as ctx:
        (idx_ready, rows_landed, w_landed, rows_turned, rT_ready, up_done, act_done, g_ready, g_turned,
         gT_ready, y_psum, y_ready, y_stored) = T.sems(
            ctx, *[f"v{i}_{n}" for n in ("idx_ready", "rows_landed", "w_landed", "rows_turned", "rT_ready", "up_done",
                                         "act_done", "g_ready", "g_turned", "gT_ready", "y_psum", "y_ready", "y_stored")])

        def repeated(engine, body):
            n_tiles = engine.value_load(count, min_val=0, max_val=nov)
            with engine.If(n_tiles > 0):
                with engine.Fori(0, n_tiles) as n:
                    body(n)
                engine.nop()
            with engine.Else():
                engine.nop()
            engine.nop()

        with nc.Block() as block:
            @block.gpsimd
            def _(pool):
                def tile(n):
                    pool.tensor_copy(cur, ov_idx[:, bass.ds(n, 1)])
                    pool.drain()
                    pool.indirect_dma_start(B.rows[:, 0, :], None, T.h2_dram, bass.IndirectOffsetOnAxis(ap=cur, axis=0))\
                        .then_inc(rows_landed, 16)
                    pool.wait_ge(y_stored, (n + 1) * 16)
                repeated(pool, tile)

            @block.sync
            def _(sp):
                def tile(n):
                    sp.wait_ge(rows_landed, (n + 1) * 16)
                    e = sp.value_load(ov_exp[0:1, bass.ds(n, 1)], min_val=0, max_val=NE - 1)
                    for kind in ("w1", "w3", "w2"):
                        sp.dma_start(expert_slot(T, kind), expert_weights(T, i, kind, e)).then_inc(w_landed, 16)
                repeated(sp, tile)

            @block.tensor
            def _(pe):
                def tile(n):
                    pe.wait_ge(rows_landed, (n + 1) * 16)
                    pe.wait_ge(w_landed, (n + 1) * 48)
                    for k in range(KD):
                        ins = pe.transpose(ps[:, 2 + k // 4, (k % 4) * P:(k % 4 + 1) * P], B.rows[:, 0, k * P:(k + 1) * P], ident)
                    ins.then_inc(rows_turned, 1)
                    pe.wait_ge(rT_ready, n + 1)
                    for b, kind in enumerate(("w1", "w3")):
                        w = expert_slot(T, kind)
                        for k in range(KD):
                            ins = pe.matmul(ps[:, b, :], B.rT[:, k, :], w[:, k, :], start=(k == 0), stop=(k == KD - 1))
                    ins.then_inc(up_done, 1)
                    pe.wait_ge(g_ready, n + 1)
                    for k in range(DE // P):
                        ins = pe.transpose(ps[:, 4, k * P:(k + 1) * P], B.g[:, k * P:(k + 1) * P], ident)
                    ins.then_inc(g_turned, 1)
                    pe.wait_ge(gT_ready, n + 1)
                    w = expert_slot(T, "w2")
                    for h in range(2):
                        for k in range(DE // P):
                            ins = pe.matmul(ps[:, 5 + h, :], B.gT[:, k, :], w[:, k, h * HALF:(h + 1) * HALF],
                                            start=(k == 0), stop=(k == DE // P - 1))
                    ins.then_inc(y_psum, 1)
                repeated(pe, tile)

            @block.scalar
            def _(act):
                def tile(n):
                    act.wait_ge(up_done, n + 1)
                    act.activation(B.s, ps[:, 0, :], ACT.Silu).then_inc(act_done, 1)
                    act.wait_ge(y_ready, n + 1)
                    act.dma_start(T.y_dram[bass.ds(n * P + NE * P, P), :], B.y[:, 0, :]).then_inc(y_stored, 16)
                    act.wait_ge(y_stored, (n + 1) * 16)
                repeated(act, tile)

            @block.vector
            def _(dve):
                def tile(n):
                    dve.wait_ge(rows_turned, n + 1)
                    dve.tensor_copy(B.rT.rearrange("p k n -> p (k n)"), ps[:, 2:4, :].rearrange("p b n -> p (b n)")).then_inc(rT_ready, 1)
                    dve.wait_ge(act_done, n + 1)
                    dve.tensor_tensor(B.g, ps[:, 1, :], B.s, ALU.mult).then_inc(g_ready, 1)
                    dve.wait_ge(g_turned, n + 1)
                    dve.tensor_copy(B.gT, ps[:, 4, :].rearrange("p (k n) -> p k n", n=P)).then_inc(gT_ready, 1)
                    dve.wait_ge(y_psum, n + 1)
                    dve.tensor_copy(B.y[:, 0, :], ps[:, 5:7, :].rearrange("p b n -> p (b n)")).then_inc(y_ready, 1)
                repeated(dve, tile)


def combine_stage(T, i, nt, load_to):
    nc, t, f = T.nc, T.t, T.f
    X = f(XR, NT, D)
    y = f(HI, 2, 2, D)
    gate, slot = f(KEEP + K_GATE, 2, NT), f(KEEP + K_SLOT, 2, NT).bitcast(U32)
    with ExitStack() as ctx:
        y_landed0, y_landed1, scaled, tile_done, step = T.sems(ctx, *[f"c{i}_{n}" for n in ("y_landed0", "y_landed1", "scaled", "tile_done", "step")])
        y_landed = (y_landed0, y_landed1)
        with nc.Block() as block:
            @block.gpsimd
            def _(pool):
                for n in range(nt):
                    if n >= 2:
                        pool.wait_ge(tile_done, n - 1)
                    for m in range(2):
                        pool.indirect_dma_start(y[:, n % 2, m, :], None, T.y_dram,
                                                bass.IndirectOffsetOnAxis(ap=slot[:, m, n:n + 1], axis=0)).then_inc(y_landed[n % 2], 16)

            @block.sync
            def _(sp):
                for half in y_landed:
                    sp.wait_ge(half, 32 * (nt // 2))
                load_to(sp)

            @block.scalar
            def _(act):
                for n in range(nt):
                    a = y[:, n % 2, 0, :]
                    act.wait_ge(y_landed[n % 2], 32 * (n // 2 + 1))
                    act.activation(a, a, ACT.Copy, scale=gate[:, 0, n:n + 1]).then_inc(scaled, 1)

            @block.vector
            def _(dve):
                then = Steps(dve, step)
                for n in range(nt):
                    v = 0 if n < XT else 1
                    dve.wait_ge(scaled, n + 1)
                    a, b = y[:, n % 2, 0, :], y[:, n % 2, 1, :]
                    then(dve.scalar_tensor_tensor(a, b, gate[:, 1, n:n + 1], a, ALU.mult, ALU.add))
                    then(dve.tensor_tensor(a, a, T.mod(v, G2), ALU.mult))
                    dve.tensor_tensor(X[:, n, :], X[:, n, :], a, ALU.add).then_inc(tile_done, 1)


QR, KR, VR, GT = LO, LO + XT * HALF, LO + XT * HALF + NT * HALF, LO + XT * HALF + NT * HALF + NT * D
LR, WG = GT + XT * D, GT + XT * D + 2 * HALF
GDEC = HI + 4 * D


def gla_project_stage(T):
    nc, t, f, ps = T.nc, T.t, T.f, T.ps
    hT = T.r(HI, 2, KD, NT * P)
    w = T.r(MOD, 2, KD, HALF)
    q, k_, v, gate = f(QR, XT, HALF), f(KR, NT, HALF), f(VR, NT, D), f(GT, XT, D)
    lrT, w_lr, w_lr2 = f(LR, 2, HALF), f(MOD + 8 * D, KD, 2 * RANK), T.r(MOD + 8 * D + KD * 2 * RANK, 2, KD, 2 * RANK)
    dests = [(q, 0, XT), (k_, 0, NT), (v, 0, NT), (v, HALF, NT), (gate, 0, XT), (gate, HALF, XT)]
    with ExitStack() as ctx:
        lr_landed, lr_high, lr_low, proj_done, proj_evac, lr_done, w_high, w_low, w_used = T.sems(
            ctx, "lr_landed", "lr_high", "lr_low", "gproj_done", "gproj_evac", "lr_done", "gw_high", "gw_low", "gw_used")
        with nc.Block() as block:
            @block.sync
            def _(sp):
                sp.dma_start(w_lr, t["gla_w_in"][0][:, 6 * HALF:].rearrange("(k p) n -> p k n", p=P)).then_inc(lr_landed, 16)
                T.load_chunks(sp, ("out", 1, 1), {("in", 1, j): [(w_low, KD * (j + 1))] for j in range(6)})
                sp.wait_ge(lr_landed, 16)

            @block.tensor
            def _(pe):
                pe.wait_ge(lr_low, 1)
                parts = ((0, 0), (1, 0), (0, 1))
                for d in range(2):
                    for k in range(KD):
                        for m, (a, b) in enumerate(parts):
                            ins = pe.matmul(ps[0:RANK, 4 + d, :], w_lr2[:, a, k, d * RANK:(d + 1) * RANK], hT[:, b, k, :],
                                            start=(k == 0 and m == 0), stop=(k == KD - 1 and m == 2))
                ins.then_inc(lr_done, 1)
                for c in range(6):
                    if c == 1:
                        pe.wait_ge(proj_evac, 1)
                    if c >= 2:
                        pe.wait_ge(proj_evac, c)
                    for k in range(KD):
                        pe.wait_ge(w_low, KD * c + k + 1)
                        for n in range(dests[c][2]):
                            for m, (a, b) in enumerate(parts):
                                ins = pe.matmul(ps[:, 4 * (c % 2) + n, :], hT[:, b, k, n * P:(n + 1) * P], w[:, a, k, :],
                                                start=(k == 0 and m == 0), stop=(k == KD - 1 and m == 2))
                        ins.then_inc(w_used, 1)

            @block.scalar
            def _(act):
                def high(c):
                    T.wait_chunk(act, ("in", 1, c))
                    for k in range(KD):
                        if c >= 1:
                            act.wait_ge(w_used, KD * (c - 1) + k + 1)
                        act.activation(w[:, 0, k, :], T.chunk(("in", 1, c))[:, k, :], ACT.Copy).then_inc(w_high, 1)

                def evacuate(c):
                    to, col, tiles = dests[c]
                    act.wait_ge(w_used, KD * (c + 1))
                    for n in range(tiles):
                        ins = act.activation(to[:, n, col:col + HALF], ps[:, 4 * (c % 2) + n, :], ACT.Copy,
                                             scale=C_DK ** -0.5 if c == 0 else 1.0)
                    ins.then_inc(proj_evac, 1)

                act.wait_ge(lr_landed, 16)
                act.activation(w_lr2[:, 0], w_lr, ACT.Copy).then_inc(lr_high, 1)
                high(0)
                act.wait_ge(lr_done, 1)
                for d in range(2):
                    ins = act.activation(lrT[0:RANK, d, :], ps[0:RANK, 4 + d, :], ACT.Copy)
                ins.then_inc(proj_evac, 1)
                for c in range(1, 6):
                    high(c)
                    evacuate(c - 1)
                evacuate(5)

            @block.vector
            def _(dve):
                dve.wait_ge(lr_high, 1)
                dve.tensor_tensor(w_lr2[:, 1], w_lr, w_lr2[:, 0].bitcast(F32), ALU.subtract).then_inc(lr_low, 1)
                for c in range(6):
                    for k in range(KD):
                        dve.wait_ge(w_high, KD * c + k + 1)
                        dve.tensor_tensor(w[:, 1, k, :], T.chunk(("in", 1, c))[:, k, :], w[:, 0, k, :].bitcast(F32),
                                          ALU.subtract).then_inc(w_low, 1)


def decay_stage(T, load_to):
    nc, t, f, ps = T.nc, T.t, T.f, T.ps
    lrT, w_g = f(LR, 2, HALF), f(WG, 2, HALF)
    z, u = f(GDEC, 2 * NT, HALF), f(HI, 2 * NT, HALF)
    b_g = f(HI + 8 * D, 2, HALF)
    with ExitStack() as ctx:
        g_landed, z_psum, z_ready, u_in, u_out, ln_out, step = T.sems(
            ctx, "gate_landed", "z_psum", "z_ready", "u_in", "u_out", "ln_out", "decay_step")
        with nc.Block() as block:
            @block.sync
            def _(sp):
                sp.dma_start(w_g[0:RANK], t["gla_w_gate"][0].rearrange("d r n -> r d n")).then_inc(g_landed, 16)
                sp.dma_start(b_g, t["gla_b_gate"][0].partition_broadcast(P)).then_inc(g_landed, 16)
                load_to(sp)
                sp.wait_ge(g_landed, 32)

            @block.tensor
            def _(pe):
                pe.wait_ge(g_landed, 32)
                for m in range(2 * NT):
                    d, n = m // NT, m % NT
                    if m >= 4:
                        pe.wait_ge(z_ready, m - 3)
                    pe.matmul(ps[:, m % 4, :], lrT[0:RANK, d, n * P:(n + 1) * P], w_g[0:RANK, d, :], start=True, stop=True).then_inc(z_psum, 1)

            @block.vector
            def _(dve):
                then = Steps(dve, step)
                dve.wait_ge(g_landed, 32)
                for m in range(2 * NT):
                    dve.wait_ge(z_psum, m + 1)
                    dve.tensor_tensor(z[:, m, :], ps[:, m % 4, :], b_g[:, m // NT, :], ALU.add).then_inc(z_ready, 1)
                    dve.wait_ge(z_ready, m + 1)
                    dve.scalar_tensor_tensor(u[:, m, :], z[:, m, :], -1.0, z[:, m, :], ALU.mult, ALU.min).then_inc(u_in, 1)
                for m in range(2 * NT):
                    dve.wait_ge(ln_out, m + 1)
                    dve.scalar_tensor_tensor(z[:, m, :], z[:, m, :], 0.0, u[:, m, :], ALU.min, ALU.subtract)

            @block.scalar
            def _(act):
                for m in range(2 * NT):
                    act.wait_ge(u_in, m + 1)
                    act.activation(u[:, m, :], u[:, m, :], ACT.Exp).then_inc(u_out, 1)
                for m in range(2 * NT):
                    act.wait_ge(u_out, m + 1)
                    act.activation(u[:, m, :], u[:, m, :], ACT.Ln, bias=1.0).then_inc(ln_out, 1)


SPARE = MOD
GO = SPARE
GSTATE = SPARE + 2 * D


def gla_stage(T, load_to):
    nc, t, f, ps = T.nc, T.t, T.f, T.ps
    q, k_, v = f(QR, XT, HALF), f(KR, NT, HALF), f(VR, NT, D)
    g = f(GDEC, 2, NT, HALF)
    ke = f(HI, 2, NT, HALF)
    c0 = HI + 8 * D
    tm, end_x, end_c, all16, low = f(c0, 2, 2, P), f(c0 + 4 * P, 2, P), f(c0 + 6 * P, 2, P), f(c0 + 8 * P, P), f(c0 + 9 * P, 2, CHUNK)
    wk = c0 + 10 * P
    exs = (f(wk, 3, XT, P), f(MOD + 5 * D, 3, XT, P))
    qkms = (f(wk + 3 * XT * P, 3, XT, P), f(MOD + 7 * D, 3, XT, P))
    qT, kT = f(LR, C_HEADS, XT * P), f(LR + C_HEADS * XT * P, C_HEADS, XT * P)
    aT = f(LR + 2 * C_HEADS * XT * P, 2, XT, P)
    state = f(GSTATE, 2, 4, C_DV)
    O = f(GO, XT, D)
    ident = f(KEEP + K_ID, P)
    NCH = SEQ // CHUNK
    units = [(h, d) for h in range(C_HEADS) for d in range(2)]
    order = {0: list(range(NCH)), 1: list(range(NCH - 1, -1, -1))}

    def product(d, c):
        if c is None:
            bank, half = (3, 1) if d == 0 else (2, 1)
        else:
            bank, half = 2 + c % 2, (0 if c in (order[d][0], order[d][1]) else 1)
        return ps[:, bank, half * C_DV:(half + 1) * C_DV]
    with ExitStack() as ctx:
        (tab_landed, turned, turn_evac, e_psum, e_exp, ke_ready, t_psum, t_exp, qk_ready, a_psum, a_ready,
         s_psum, s_ready, o_psum, o_ready, zeroed, step) = T.sems(
            ctx, *[f"g_{n}" for n in ("tab_landed", "turned", "turn_evac", "e_psum", "e_exp", "ke_ready", "t_psum",
                                      "t_exp", "qk_ready", "a_psum", "a_ready", "s_psum", "s_ready", "o_psum", "o_ready",
                                      "zeroed", "step")])
        with nc.Block() as block:
            @block.sync
            def _(sp):
                for to, name in ((tm.rearrange("p a b n -> p (a b n)"), "k_sums"), (end_x.rearrange("p a n -> p (a n)"), "k_ends"),
                                 (end_c.rearrange("p a n -> p (a n)"), "k_ends_ctx"), (all16, "k_all"),
                                 (low.rearrange("p a n -> p (a n)"), "k_low")):
                    sp.dma_start(to, t[name]).then_inc(tab_landed, 16)
                load_to(sp)
                sp.wait_ge(tab_landed, 80)

            @block.tensor
            def _(pe):
                pe.wait_ge(tab_landed, 80)
                for n, src in enumerate((q, k_)):
                    for m in range(XT * C_HEADS):
                        h, tile = m // XT, m % XT
                        ins = pe.transpose(ps[:, 2 * n + h // 2, (h % 2) * XT * P + tile * P:(h % 2) * XT * P + (tile + 1) * P],
                                           src[:, tile, h * P:(h + 1) * P], ident)
                    ins.then_inc(turned, 1)
                m = 0
                for d in range(2):
                    for tile in range(NT):
                        bank = 4 + m % 4
                        if m >= 4:
                            pe.wait_ge(e_exp, m - 3)
                        if tile < XT:
                            ins = pe.matmul(ps[:, bank, :], end_x[:, d, :], g[:, d, tile, :], start=True, stop=True)
                        else:
                            whole = (d == 0 and tile == XT) or (d == 1 and tile == NT - 1)
                            ins = pe.matmul(ps[:, bank, :], end_c[:, d, :], g[:, d, tile, :], start=True, stop=not whole)
                            if whole:
                                other = XT if d == 1 else NT - 1
                                ins = pe.matmul(ps[:, bank, :], all16, g[:, d, other, :], start=False, stop=True)
                        ins.then_inc(e_psum, 1)
                        m += 1

                def sums(n):
                    h, d = units[n]
                    pe.wait_ge(t_exp, n)
                    for tile in range(XT):
                        ins = pe.matmul(ps[:, 0, tile * 2 * P:(tile + 1) * 2 * P], g[:, d, tile, h * P:(h + 1) * P],
                                        tm[:, d].rearrange("p a n -> p (a n)"), start=True, stop=True)
                    ins.then_inc(t_psum, 1)

                def states(n):
                    h, d = units[n]
                    hv = slice(h * C_DV, (h + 1) * C_DV)
                    hk = slice(h * P, (h + 1) * P)
                    if n >= 1:
                        pe.wait_ge(s_ready, n)
                    for m, tile in enumerate(range(XT, NT)):
                        pe.matmul(product(d, None), ke[:, d, tile, hk], v[:, tile, hv], start=(m == 0), stop=(m == 1))
                    for m, c in enumerate(order[d][:-1]):
                        rows = slice((c % 2) * CHUNK, (c % 2 + 1) * CHUNK)
                        ins = pe.matmul(product(d, c), ke[rows, d, c // 2, hk],
                                        v[rows, c // 2, hv], start=True, stop=True)
                    ins.then_inc(s_psum, 1)

                def scores(n):
                    qkm = qkms[n % 2]
                    pe.wait_ge(qk_ready, n + 1)
                    if n >= 1:
                        pe.wait_ge(a_ready, n)
                    for tile in range(XT):
                        for c in range(2):
                            r = slice(c * CHUNK, (c + 1) * CHUNK)
                            ins = pe.matmul(ps[r, 1, tile * P:tile * P + CHUNK], qkm[:, 2, tile, r], qkm[:, 1, tile, r], start=True, stop=True)
                    ins.then_inc(a_psum, 1)

                def outputs(n):
                    h, d = units[n]
                    qkm = qkms[n % 2]
                    hv = slice(h * C_DV, (h + 1) * C_DV)
                    pe.wait_ge(a_ready, n + 1)
                    pe.wait_ge(s_ready, n + 1)
                    if d == 0 and h >= 2:
                        pe.wait_ge(o_ready, h - 1)
                    for tile in range(XT):
                        to = ps[:, 4 + 2 * (h % 2) + tile, 0:C_DV]
                        pe.matmul(to, aT[:, d, tile, :], v[:, tile, hv], start=(d == 0), stop=False, skip_group_check=True)
                        for c in range(2):
                            r = slice(c * CHUNK, (c + 1) * CHUNK)
                            ins = pe.matmul(ps[r, 4 + 2 * (h % 2) + tile, 0:C_DV], qkm[:, 0, tile, r], state[:, d, 2 * tile + c, :],
                                            start=False, stop=(d == 1), skip_group_check=True)
                    ins.then_inc(o_psum, 1)

                pe.wait_ge(turn_evac, 4)
                pe.wait_ge(e_exp, 8)
                pe.wait_ge(ke_ready, 8)
                sums(0)
                states(0)
                for n in range(len(units)):
                    if n + 1 < len(units):
                        sums(n + 1)
                    scores(n)
                    if n + 1 < len(units):
                        states(n + 1)
                    outputs(n)

            @block.scalar
            def _(act):
                for n, to in enumerate((qT, kT)):
                    act.wait_ge(turned, n + 1)
                    for b in range(2):
                        act.activation(to[:, 2 * b:2 * b + 2, :], ps[:, 2 * n + b, :].rearrange("p (h n) -> p h n", n=XT * P),
                                       ACT.Copy).then_inc(turn_evac, 1)
                for m in range(2 * NT):
                    act.wait_ge(e_psum, m + 1)
                    act.activation(ke[:, m // NT, m % NT, :], ps[:, 4 + m % 4, :], ACT.Exp).then_inc(e_exp, 1)

                def exponentials(n):
                    ex = exs[n % 2]
                    act.wait_ge(t_psum, n + 1)
                    if n >= 2:
                        act.wait_ge(qk_ready, n - 1)
                        act.wait_ge(s_ready, n - 1)
                    bank = ps[:, 0, :].rearrange("p (t a n) -> p t a n", t=XT, a=2)
                    act.activation(ex[:, 0], bank[:, :, 0, :], ACT.Exp)
                    act.activation(ex[:, 1], bank[:, :, 1, :], ACT.Exp)
                    act.activation(ex[:, 2], bank[:, :, 1, :], ACT.Exp, scale=-1.0).then_inc(t_exp, 1)

                exponentials(0)
                for n, (h, d) in enumerate(units):
                    if n + 1 < len(units):
                        exponentials(n + 1)
                    if d == 1:
                        act.wait_ge(o_psum, n + 1)
                        for tile in range(XT):
                            ins = act.activation(O[:, tile, h * C_DV:(h + 1) * C_DV], ps[:, 4 + 2 * (h % 2) + tile, 0:C_DV], ACT.Copy)
                        ins.then_inc(o_ready, 1)

            @block.vector
            def _(dve):
                then = Steps(dve, step)
                dve.memset(aT, 0.0).then_inc(zeroed, 1)
                dve.wait_ge(zeroed, 1)
                dve.wait_ge(tab_landed, 80)
                for m in range(2 * NT):
                    dve.wait_ge(e_exp, m + 1)
                    to = ke[:, m // NT, m % NT, :]
                    dve.tensor_tensor(to, to, k_[:, m % NT, :], ALU.mult).then_inc(ke_ready, 1)
                dve.wait_ge(turn_evac, 4)

                def products(n):
                    h, _ = units[n]
                    ex, qkm = exs[n % 2], qkms[n % 2]
                    dve.wait_ge(t_exp, n + 1)
                    if n >= 2:
                        dve.wait_ge(o_psum, n - 1)
                    qh, kh = (x[:, h, :].rearrange("p (t n) -> p t n", n=P) for x in (qT, kT))
                    dve.tensor_tensor(qkm[:, 1], qh, ex[:, 1], ALU.mult)
                    dve.tensor_tensor(qkm[:, 2], kh, ex[:, 2], ALU.mult)
                    dve.tensor_tensor(qkm[:, 0], qh, ex[:, 0], ALU.mult).then_inc(qk_ready, 1)

                products(0)
                for n, (h, d) in enumerate(units):
                    ex = exs[n % 2]
                    dve.wait_ge(s_psum, n + 1)
                    seq = order[d]
                    then(dve.tensor_copy(state[:, d, seq[0], :], product(d, None)))
                    for m, c in enumerate(seq[:-1]):
                        last = c % 2 * CHUNK + (CHUNK - 1 if d == 0 else 0)
                        ins = dve.scalar_tensor_tensor(state[:, d, seq[m + 1], :], state[:, d, c, :], ex[:, 0, c // 2, last:last + 1],
                                                       product(d, c), ALU.mult, ALU.add)
                        if m < NCH - 2:
                            then(ins)
                    ins.then_inc(s_ready, 1)
                    if n + 1 < len(units):
                        products(n + 1)
                    dve.wait_ge(a_psum, n + 1)
                    for c in range(2):
                        r = slice(c * CHUNK, (c + 1) * CHUNK)
                        ins = dve.copy_predicated(aT[r, d, :, r], bc(low[r, d, :], 1, (CHUNK, XT, CHUNK)).bitcast(U32),
                                                  ps[r, 1, 0:XT * P].rearrange("p (t n) -> p t n", n=P)[:, :, 0:CHUNK])
                    ins.then_inc(a_ready, 1)


def final_stage(T):
    nc, t, f = T.nc, T.t, T.f
    X, g_row, y = f(XR, NT, D), f(HI, D), f(HI + D, XT, D)
    ss, rstd = f(HI + 3 * D, XT), f(HI + 3 * D + XT, XT)
    with ExitStack() as ctx:
        g_landed, ss_ready, var_ready, std_ready, y_ready, stored, step = T.sems(
            ctx, *[f"f_{n}" for n in ("g_landed", "ss_ready", "var_ready", "std_ready", "y_ready", "stored", "step")])
        with nc.Block() as block:
            @block.sync
            def _(sp):
                sp.dma_start(g_row, t["final_g"].partition_broadcast(P)).then_inc(g_landed, 16)
                for n in range(XT):
                    sp.wait_ge(y_ready, n + 1)
                    sp.dma_start(T.out[0, n * P:(n + 1) * P, :], y[:, n, :]).then_inc(stored, 16)
                sp.wait_ge(g_landed, 16)
                sp.wait_ge(stored, 16 * XT)

            @block.scalar
            def _(act):
                for n in range(XT):
                    act.activation(y[:, n, :], X[:, n, :], ACT.Square, accum_out=ss[:, n:n + 1]).then_inc(ss_ready, 1)
                act.wait_ge(var_ready, 1)
                act.activation(rstd, ss, ACT.Sqrt).then_inc(std_ready, 1)

            @block.vector
            def _(dve):
                then = Steps(dve, step)
                dve.wait_ge(ss_ready, XT)
                dve.tensor_scalar(ss, ss, 1.0 / D, EPS, ALU.mult, ALU.add).then_inc(var_ready, 1)
                dve.wait_ge(std_ready, 1)
                then(dve.reciprocal(rstd, rstd))
                dve.wait_ge(g_landed, 16)
                for n in range(XT):
                    dve.scalar_tensor_tensor(y[:, n, :], X[:, n, :], rstd[:, n:n + 1], g_row, ALU.mult, ALU.mult).then_inc(y_ready, 1)


def hybrid_trunk(nc, t, out, stages=99, dump=None):
    with ExitStack() as ctx:
        T = Trunk(nc, ctx, t, out)
        f = T.f
        every, of_x = list(range(NT)), list(range(XT))
        none = lambda *a: None
        steps = [
            lambda: setup_stage(T),
            lambda: mod_stage(T),
            lambda: norm_stage(T, 0, 0, every, none, False, split=True),
            lambda: attn_project_stage(T),
            lambda: attention_stage(T),
            lambda: out_stage(T, 0, NT, f(ORow, NT, D), f(LO, KD, NT * P),
                              (f(HI + 8 * D, A_DV), f(HI + 9 * D, D), f(HI + 10 * D, 16), f(HI + 10 * D + 16, 16), None)),
            lambda: norm_stage(T, 0, 1, every, lambda sp: route_loads(T, sp, 0, NT), True,
                               load_last=lambda sp: first_expert_loads(T, sp, 0)),
            lambda: experts(T, 0, NT),
            lambda: overflow_stage(T, 0, NT),
            lambda: combine_stage(T, 0, NT, lambda sp: load_modulation(T, sp)),
            lambda: norm_stage(T, 1, 0, every, lambda sp: (load_gate2(T, sp), T.load_chunks(sp, ("in", 1, 2), {})), False, split=True),
            lambda: gla_project_stage(T),
            lambda: decay_stage(T, none),
            lambda: gla_stage(T, lambda sp: load_late_modulation(T, sp)),
            lambda: out_stage(T, 1, XT, f(GO, XT, D), f(HI, KD, XT * P),
                              (f(HI + 8 * D, C_DV), f(HI + 9 * D, D), f(HI + 10 * D, 8), f(HI + 10 * D + 8, 8), f(GT, XT, D))),
            lambda: norm_stage(T, 1, 1, of_x, lambda sp: route_loads(T, sp, 1, XT), True,
                               load_last=lambda sp: first_expert_loads(T, sp, 1)),
            lambda: experts(T, 1, XT),
            lambda: overflow_stage(T, 1, XT),
            lambda: combine_stage(T, 1, XT, none),
            lambda: final_stage(T),
        ]
        for n, stage in enumerate(steps[:stages]):
            stage()
            if dump is not None:
                dump(n, T)


def shape_constants():
    c = {"k_ident": np.eye(P, dtype=np.float32), "k_ones": np.ones((P, P), np.float32)}
    p = np.arange(P)
    c["k_iota16"] = np.arange(NE, dtype=np.float32)[None]
    c["k_token"] = (p[:, None] + P * np.arange(NT)[None]).astype(np.float32)
    c["k_iota512"] = np.arange(NT * P, dtype=np.float32)[None]
    c["k_before"] = (p[:, None] < p[None]).astype(np.float32)
    j, pos = p % 32 % 16, np.arange(SEQ)
    inv = np.power(np.float32(10000.0), -(2 * j).astype(np.float32) / np.float32(32))
    at = np.where((p % 64 < 32)[:, None], (pos // GRID_W)[None], (pos % GRID_W)[None]).astype(np.float32)
    ang = (at * inv[:, None].astype(np.float32)).astype(np.float32)
    c["k_cos"], c["k_sin"] = np.cos(ang).astype(np.float32), np.sin(ang).astype(np.float32)
    rot = np.zeros((P, P), np.float32)
    for m in range(P):
        if m % 32 < 16:
            rot[m + 16, m] = -1.0
        else:
            rot[m - 16, m] = 1.0
    c["k_rope"] = rot
    col = np.arange(GRID_W)
    start = np.clip(col - NA_COLS // 2, 0, GRID_W - NA_COLS)
    seen = (col[None] >= start[:, None]) & (col[None] < start[:, None] + NA_COLS)
    c["k_namask"] = np.tile(np.where(seen, 0.0, MASKED), (SEQ // GRID_W, SEQ // GRID_W)).astype(np.float32)
    for i, nt in ((0, NT), (1, XT)):
        e, b = np.meshgrid(np.arange(NE), np.arange(1, nt), indexing="ij")
        c[f"k_over{i}"] = np.stack([b * P, e]).astype(np.float32)
    s, tt = p[:, None], p[None]
    same = s // CHUNK == tt // CHUNK
    w = np.float32(1.0 / TAU)
    sums, ends, ends_ctx, low = [], [], [], []
    for d in range(2):
        run = same & (s <= tt if d == 0 else s >= tt)
        mid = tt // CHUNK * CHUNK + (CHUNK // 2 - 1 if d == 0 else CHUNK // 2)
        to_mid = same & (s <= mid if d == 0 else s >= mid)
        sums += [run * w, (run.astype(np.float32) - to_mid.astype(np.float32)) * w]
        ends.append((same & (s > tt if d == 0 else s < tt)) * w)
        ends_ctx.append((s > tt if d == 0 else s < tt) * w)
        a, b = p[:, None] % CHUNK, np.arange(CHUNK)[None]
        low.append(a <= b if d == 0 else a >= b)
    cat = lambda xs: np.ascontiguousarray(np.concatenate(xs, 1).astype(np.float32))
    c["k_sums"], c["k_ends"], c["k_ends_ctx"], c["k_low"] = cat(sums), cat(ends), cat(ends_ctx), cat(low)
    c["k_all"] = np.full((P, P), w, np.float32)
    return c


def window_layout(na_bias):
    rows, pos = SEQ // GRID_W, np.arange(SEQ)
    dr = pos[None] // GRID_W - pos[:, None] // GRID_W + NA_ROWS - 1
    dc = pos[None] % GRID_W - pos[:, None] % GRID_W + NA_COLS - 1
    dc = np.clip(dc, 0, 2 * NA_COLS - 2)
    return np.ascontiguousarray(np.asarray(na_bias)[0][:, dr, dc])


_INS = ["x", "ctx", "w_mod", "b_mod", "norm_g", "final_g", "att_w_in", "att_w_out", "att_lambda", "att_subln_g",
        "gla_w_in", "gla_w_gate", "gla_b_gate", "gla_norm_g", "gla_w_out", "router_w", "router_bias",
        "moe_w1", "moe_w3", "moe_w2"]


def launch_arrays(inputs):
    a = {n: np.ascontiguousarray(inputs[n]) for n in _INS}
    a["final_g"] = a["final_g"].reshape(1, D)
    a["router_bias"] = a["router_bias"].reshape(1, NE)
    a["c_cols"] = np.ascontiguousarray(np.asarray(inputs["c"]).reshape(KD, P).T)
    a["c_ctx_cols"] = np.ascontiguousarray(np.asarray(inputs["c_ctx"]).reshape(KD, P).T)
    a["na_window"] = window_layout(inputs["na_bias"])
    a.update(shape_constants())
    return a


def kernel(**inputs):
    import concourse.bacc as _bacc
    from concourse.bass_utils import run_bass_kernel_spmd as _run

    nc = _bacc.Bacc("TRN2", target_bir_lowering=False, num_devices=1)
    arrays = launch_arrays(inputs)
    t = {n: nc.dram_tensor(n, a.shape, F32, kind="ExternalInput").ap() for n, a in arrays.items()}
    out = nc.dram_tensor("out_x", (1, SEQ, D), F32, kind="ExternalOutput").ap()
    hybrid_trunk(nc, t, out)
    r = _run(nc, [arrays], core_ids=[0])
    return r.results[0]["out_x"]
```
